# Optimizing a Trainium2 kernel written in Bass

```python
import math
import jax, jax.numpy as jnp
from jax import lax
import numpy as np

D_MODEL = 1024
BATCH = 1
SEQ = 256
DEPTH = 1

CHUNK = 64
D_SSM = D_MODEL // 2
SSM_GROUP = 16
N_GROUPS = D_SSM // SSM_GROUP
STATE = 64
N_HEADS = 8
HEAD_DIM = 64
D_ATTN = N_HEADS * HEAD_DIM
D_IN = D_SSM + 3 * D_ATTN
D_FF = 4 * D_MODEL
Q_BLOCK = 128
EPS = 1e-6
DT_MIN = 1e-3
DT_MAX = 1e-1


def rmsnorm(x, g):
    xf = x.astype(jnp.float32)
    y = xf * lax.rsqrt(jnp.mean(xf * xf, axis=-1, keepdims=True) + EPS)
    return (y * g.astype(jnp.float32)).astype(x.dtype)

def s5_branch(u, A_re, A_im, log_dt, B_re, B_im, C_re, C_im, D_skip, w_glu, b_glu):
    f32 = jnp.float32
    bsz, seq, _ = u.shape
    uf = u.astype(f32)
    ug = uf.reshape(bsz, seq, N_GROUPS, SSM_GROUP)
    lam = lax.complex(A_re.astype(f32), A_im.astype(f32))
    dt = jnp.exp(log_dt.astype(f32))[:, None]
    a_bar = jnp.exp(lam * dt)
    b_bar = ((a_bar - 1.0) / lam)[..., None] * lax.complex(B_re.astype(f32), B_im.astype(f32))
    bu = lax.complex(jnp.einsum('bsgc,gpc->bsgp', ug, b_bar.real),
                     jnp.einsum('bsgc,gpc->bsgp', ug, b_bar.imag))
    a = jnp.broadcast_to(a_bar, (1, seq, N_GROUPS, STATE))

    def combine(left, right):
        a_l, b_l = left
        a_r, b_r = right
        return a_r * a_l, a_r * b_l + b_r

    _, states = lax.associative_scan(combine, (a, bu), axis=1)
    y = (jnp.einsum('bsgp,gcp->bsgc', states.real, C_re.astype(f32))
         - jnp.einsum('bsgp,gcp->bsgc', states.imag, C_im.astype(f32)))
    y = y.reshape(bsz, seq, D_SSM) + D_skip.astype(f32) * uf
    y = jax.nn.gelu(y)
    y = y * jax.nn.sigmoid(y @ w_glu.astype(f32) + b_glu.astype(f32))
    return y.astype(u.dtype)

def stick_breaking_attention(q, k, v):
    f32 = jnp.float32
    bsz, seq, nh, dh = q.shape
    nb = seq // Q_BLOCK
    qb = q.astype(f32).reshape(bsz, nb, Q_BLOCK, nh, dh).transpose(1, 0, 2, 3, 4)
    kf = k.astype(f32)
    vf = v.astype(f32)
    key_pos = jnp.arange(seq)
    scale = HEAD_DIM ** -0.5

    def one_block(args):
        blk, q_blk = args
        q_pos = blk * Q_BLOCK + jnp.arange(Q_BLOCK)
        z = jnp.einsum('bqhd,bkhd->bhqk', q_blk, kf) * scale
        mask = key_pos[None, :] < q_pos[:, None]
        log_fail = jnp.where(mask, jax.nn.log_sigmoid(-z), 0.0)
        after = lax.cumsum(log_fail, axis=3, reverse=True) - log_fail
        log_w = jax.nn.log_sigmoid(z) + after
        w = jnp.where(mask, jnp.exp(log_w), 0.0)
        return jnp.einsum('bhqk,bkhd->bqhd', w, vf)

    out = lax.map(one_block, (jnp.arange(nb), qb))
    return out.transpose(1, 0, 2, 3, 4).reshape(bsz, seq, nh * dh).astype(q.dtype)

def first_inputs(seed: int = 0) -> dict:
    key = jax.random.key(seed)
    ks = jax.random.split(key, 22)
    f32 = jnp.float32

    def nrm(k, shape, scale):
        return jax.random.normal(k, shape, f32) * scale

    x = nrm(ks[0], (BATCH, SEQ, D_MODEL), 1.0)
    norm_mix = 1.0 + nrm(ks[1], (DEPTH, D_MODEL), 0.02)
    w_in = nrm(ks[2], (DEPTH, D_MODEL, D_IN), D_MODEL ** -0.5)
    A_re = -0.5 + nrm(ks[3], (DEPTH, N_GROUPS, STATE), 0.01)
    A_im = jnp.pi * jnp.arange(STATE, dtype=f32) + nrm(ks[4], (DEPTH, N_GROUPS, STATE), 0.01)
    log_dt = jax.random.uniform(ks[5], (DEPTH, N_GROUPS), f32, math.log(DT_MIN), math.log(DT_MAX))
    B_re = nrm(ks[6], (DEPTH, N_GROUPS, STATE, SSM_GROUP), (2 * SSM_GROUP) ** -0.5)
    B_im = nrm(ks[7], (DEPTH, N_GROUPS, STATE, SSM_GROUP), (2 * SSM_GROUP) ** -0.5)
    C_re = nrm(ks[8], (DEPTH, N_GROUPS, SSM_GROUP, STATE), STATE ** -0.5)
    C_im = nrm(ks[9], (DEPTH, N_GROUPS, SSM_GROUP, STATE), STATE ** -0.5)
    D_skip = nrm(ks[10], (DEPTH, D_SSM), 1.0)
    w_glu = nrm(ks[11], (DEPTH, D_SSM, D_SSM), D_SSM ** -0.5)
    b_glu = nrm(ks[12], (DEPTH, D_SSM), 0.02)
    w_up_ssm = nrm(ks[13], (DEPTH, D_SSM, D_MODEL), D_SSM ** -0.5)
    w_up_attn = nrm(ks[14], (DEPTH, D_ATTN, D_MODEL), D_ATTN ** -0.5)
    w_gate = nrm(ks[15], (DEPTH, D_MODEL, 2 * D_MODEL), D_MODEL ** -0.5)
    b_gate = nrm(ks[16], (DEPTH, 2 * D_MODEL), 0.02)
    w_out = nrm(ks[17], (DEPTH, D_MODEL, D_MODEL), D_MODEL ** -0.5)
    norm_mlp = 1.0 + nrm(ks[18], (DEPTH, D_MODEL), 0.02)
    w_ff1 = nrm(ks[19], (DEPTH, D_MODEL, D_FF), D_MODEL ** -0.5)
    w_ff2 = nrm(ks[20], (DEPTH, D_FF, D_MODEL), D_FF ** -0.5)
    norm_final = 1.0 + nrm(ks[21], (D_MODEL,), 0.02)
    return {"x": x, "norm_mix": norm_mix, "w_in": w_in, "A_re": A_re, "A_im": A_im,
            "log_dt": log_dt, "B_re": B_re, "B_im": B_im, "C_re": C_re, "C_im": C_im,
            "D_skip": D_skip, "w_glu": w_glu, "b_glu": b_glu, "w_up_ssm": w_up_ssm,
            "w_up_attn": w_up_attn, "w_gate": w_gate, "b_gate": b_gate, "w_out": w_out,
            "norm_mlp": norm_mlp, "w_ff1": w_ff1, "w_ff2": w_ff2, "norm_final": norm_final}

def first_block(x, norm_mix, w_in, A_re, A_im, log_dt, B_re, B_im, C_re, C_im, D_skip, w_glu, b_glu,
              w_up_ssm, w_up_attn, w_gate, b_gate, w_out, norm_mlp, w_ff1, w_ff2, norm_final):
    h = x
    bsz, seq, _ = x.shape
    for l in range(DEPTH):
        u = rmsnorm(h, norm_mix[l])
        proj = u @ w_in[l]
        u_ssm, q, k, v = jnp.split(proj, [D_SSM, D_SSM + D_ATTN, D_SSM + 2 * D_ATTN], axis=-1)
        y_ssm = s5_branch(u_ssm, A_re[l], A_im[l], log_dt[l], B_re[l], B_im[l], C_re[l], C_im[l],
                          D_skip[l], w_glu[l], b_glu[l])
        y_attn = stick_breaking_attention(q.reshape(bsz, seq, N_HEADS, HEAD_DIM),
                                          k.reshape(bsz, seq, N_HEADS, HEAD_DIM),
                                          v.reshape(bsz, seq, N_HEADS, HEAD_DIM))
        gates = jax.nn.sigmoid((u @ w_gate[l] + b_gate[l]).astype(jnp.float32)).astype(u.dtype)
        g_ssm, g_attn = jnp.split(gates, 2, axis=-1)
        merged = g_ssm * (y_ssm @ w_up_ssm[l]) + g_attn * (y_attn @ w_up_attn[l])
        h = h + merged @ w_out[l]
        hid = jax.nn.relu(rmsnorm(h, norm_mlp[l]) @ w_ff1[l])
        h = h + (hid * hid) @ w_ff2[l]
    return rmsnorm(h, norm_final)


DEPTH_2 = 2

MLA_HEADS = 8
MLA_NOPE = 64
MLA_ROPE = 32
MLA_V = 64
MLA_Q_RANK = 256
MLA_KV_RANK = 128
NSA_HEADS = 8
NSA_KV_HEADS = 2
NSA_HPG = NSA_HEADS // NSA_KV_HEADS
NSA_HD = 64
NSA_ROT = NSA_HD // 4
L_CMP = 32
S_CMP = 16
CMP_HIDDEN = 128
L_SLC = 64
N_SEL = 16
WINDOW = 512
ROPE_THETA = 500000.0
D_FF_2 = 2816
ALPHA = (2 * DEPTH_2) ** 0.25
BETA = (8 * DEPTH_2) ** -0.25
LN_EPS = 1e-5
RMS_EPS = 1e-6
NEG = -1e30
BIG = 1e30
SPLITS = (MLA_Q_RANK, MLA_KV_RANK, MLA_ROPE, NSA_HEADS * NSA_HD, 6 * NSA_KV_HEADS * NSA_HD, 3 * NSA_HEADS, D_MODEL, D_MODEL)
D_IN_2 = sum(SPLITS)


def layer_norm(x, g, b):
    xf = x.astype(jnp.float32)
    mu = jnp.mean(xf, -1, keepdims=True)
    var = jnp.mean(jnp.square(xf - mu), -1, keepdims=True)
    return ((xf - mu) * lax.rsqrt(var + LN_EPS) * g + b).astype(x.dtype)

def rms_norm(x, g):
    xf = x.astype(jnp.float32)
    return (xf * lax.rsqrt(jnp.mean(xf * xf, -1, keepdims=True) + RMS_EPS) * g).astype(x.dtype)

def swiglu(x, wg, wu, wd):
    return (jax.nn.silu(x @ wg) * (x @ wu)) @ wd

def rope_tables(rot_dim, T):
    inv = 1.0 / (ROPE_THETA ** (jnp.arange(0, rot_dim, 2, dtype=jnp.float32) / rot_dim))
    ang = jnp.arange(T, dtype=jnp.float32)[:, None] * inv[None, :]
    return jnp.cos(ang), jnp.sin(ang)

def apply_rope(x, cos, sin):
    x1, x2 = jnp.split(x, 2, axis=-1)
    c, s = cos[:, None, :], sin[:, None, :]
    return jnp.concatenate([x1 * c - x2 * s, x2 * c + x1 * s], -1).astype(x.dtype)

def partial_rope(x, cos, sin):
    return jnp.concatenate([apply_rope(x[..., :NSA_ROT], cos, sin), x[..., NSA_ROT:]], -1)

def to_blocks(a):
    B, T = a.shape[:2]
    return a.reshape((B, T // Q_BLOCK, Q_BLOCK) + a.shape[2:]).swapaxes(0, 1)

def from_blocks(a):
    nblk, B, Q = a.shape[:3]
    return a.swapaxes(0, 1).reshape((B, nblk * Q) + a.shape[3:])

def mla_attention(q_nope, q_pe, k_nope, k_pe, v):
    T = q_nope.shape[1]
    scale = (MLA_NOPE + MLA_ROPE) ** -0.5
    kpos = jnp.arange(T)

    def one_block(args):
        qs, qn, qp = args
        s = (jnp.einsum('bqhd,bkhd->bhqk', qn, k_nope, preferred_element_type=jnp.float32)
             + jnp.einsum('bqhd,bkd->bhqk', qp, k_pe, preferred_element_type=jnp.float32)) * scale
        qpos = qs + jnp.arange(Q_BLOCK)
        s = jnp.where(kpos[None, :] <= qpos[:, None], s, NEG)
        p = jax.nn.softmax(s, axis=-1).astype(v.dtype)
        return jnp.einsum('bhqk,bkhd->bqhd', p, v)

    starts = jnp.arange(T // Q_BLOCK) * Q_BLOCK
    return from_blocks(lax.map(one_block, (starts, to_blocks(q_nope), to_blocks(q_pe))))

def compress(kv, pe, w1, b1, w2):
    B, T, G, D = kv.shape
    n_cmp = (T - L_CMP) // S_CMP + 1
    idx = np.arange(n_cmp)[:, None] * S_CMP + np.arange(L_CMP)[None, :]
    blk = kv[:, idx] + pe[:, None, :]
    blk = blk.transpose(0, 1, 3, 2, 4).reshape(B, n_cmp, G, L_CMP * D)
    return jax.nn.gelu(blk @ w1 + b1) @ w2

def nsa_attention(q, k_c, v_c, k_s, v_s, k_w, v_w, gates,
                  pe_k, k_w1, k_b1, k_w2, pe_v, v_w1, v_b1, v_w2):
    B, T = q.shape[:2]
    G, HPG, D = NSA_KV_HEADS, NSA_HPG, NSA_HD
    scale = D ** -0.5
    qg = q.reshape(B, T, G, HPG, D)
    tpos = jnp.arange(T)
    n_cmp = (T - L_CMP) // S_CMP + 1
    n_slc = T // L_SLC
    n_sel = min(N_SEL, n_slc)

    kc = compress(k_c, pe_k, k_w1, k_b1, k_w2)
    vc = compress(v_c, pe_v, v_w1, v_b1, v_w2)
    cmp_start = np.arange(n_cmp) * S_CMP
    valid = jnp.asarray(cmp_start + L_CMP - 1)[None, :] <= tpos[:, None]
    s = jnp.einsum('btghd,bcgd->bghtc', qg, kc, preferred_element_type=jnp.float32) * scale
    p_cmp = jax.nn.softmax(jnp.where(valid, s, NEG), axis=-1) * valid
    o_c = jnp.einsum('bghtc,bcgd->btghd', p_cmp.astype(vc.dtype), vc)

    blk = np.arange(n_slc)
    overlap = ((cmp_start[:, None] < (blk[None, :] + 1) * L_SLC)
               & (cmp_start[:, None] + L_CMP > blk[None, :] * L_SLC)).astype(np.float32)
    imp = jnp.einsum('bghtc,cj->btgj', p_cmp, jnp.asarray(overlap))
    cur = (tpos // L_SLC)[:, None]
    jb = jnp.arange(n_slc)[None, :]
    forced = (jb == 0) | (jb == cur) | (jb == cur - 1)
    causal = jb <= cur
    imp = jnp.where(forced[:, None], BIG, jnp.where(causal[:, None], imp, NEG))
    _, sel = lax.top_k(imp, n_sel)

    k_sb = k_s.reshape(B, n_slc, L_SLC, G, D).transpose(0, 3, 1, 2, 4)
    v_sb = v_s.reshape(B, n_slc, L_SLC, G, D).transpose(0, 3, 1, 2, 4)
    k_wp = jnp.pad(k_w, ((0, 0), (WINDOW, 0), (0, 0), (0, 0)))
    v_wp = jnp.pad(v_w, ((0, 0), (WINDOW, 0), (0, 0), (0, 0)))
    span = WINDOW + Q_BLOCK
    bi = jnp.arange(B)[:, None, None, None]
    gi = jnp.arange(G)[None, None, :, None]
    n_keys = n_sel * L_SLC

    def one_block(args):
        qs, qb, sb = args
        qpos = qs + jnp.arange(Q_BLOCK)
        ks = k_sb[bi, gi, sb].reshape(B, Q_BLOCK, G, n_keys, D)
        vs = v_sb[bi, gi, sb].reshape(B, Q_BLOCK, G, n_keys, D)
        kpos = (sb[..., None] * L_SLC + jnp.arange(L_SLC)).reshape(B, Q_BLOCK, G, n_keys)
        m_s = (kpos <= qpos[None, :, None, None]).transpose(0, 2, 1, 3)[:, :, None]
        s_s = jnp.einsum('bqghd,bqgkd->bghqk', qb, ks, preferred_element_type=jnp.float32) * scale
        p_s = jax.nn.softmax(jnp.where(m_s, s_s, NEG), axis=-1).astype(vs.dtype)
        o_s = jnp.einsum('bghqk,bqgkd->bqghd', p_s, vs)
        kw = lax.dynamic_slice_in_dim(k_wp, qs, span, axis=1)
        vw = lax.dynamic_slice_in_dim(v_wp, qs, span, axis=1)
        kpos_w = qs - WINDOW + jnp.arange(span)
        m_w = ((kpos_w[None, :] <= qpos[:, None]) & (kpos_w[None, :] > qpos[:, None] - WINDOW)
               & (kpos_w[None, :] >= 0))
        s_w = jnp.einsum('bqghd,bkgd->bghqk', qb, kw, preferred_element_type=jnp.float32) * scale
        p_w = jax.nn.softmax(jnp.where(m_w, s_w, NEG), axis=-1).astype(vw.dtype)
        o_w = jnp.einsum('bghqk,bkgd->bqghd', p_w, vw)
        return o_s, o_w

    starts = jnp.arange(T // Q_BLOCK) * Q_BLOCK
    o_s, o_w = lax.map(one_block, (starts, to_blocks(qg), to_blocks(sel)))
    o_s, o_w = from_blocks(o_s), from_blocks(o_w)
    g = gates.reshape(B, T, G, HPG, 3)
    o = g[..., 0:1] * o_c + g[..., 1:2] * o_s + g[..., 2:3] * o_w
    return o.reshape(B, T, NSA_HEADS * D)

def token_mixer(x, w_in, q_norm_g, w_uq, kv_norm_g, w_ukv,
                cmp_pe_k, cmp_k_w1, cmp_k_b1, cmp_k_w2, cmp_pe_v, cmp_v_w1, cmp_v_b1, cmp_v_w2,
                w_proj_mla, w_proj_nsa, w_out, cos_m, sin_m, cos_n, sin_n):
    B, T, _ = x.shape
    offsets = np.cumsum(SPLITS)[:-1].tolist()
    c_q, c_kv, k_pe, q_n, kv_n, g_n, gate_m, gate_n = jnp.split(x @ w_in, offsets, axis=-1)

    q = (rms_norm(c_q, q_norm_g) @ w_uq).reshape(B, T, MLA_HEADS, MLA_NOPE + MLA_ROPE)
    q_nope, q_pe = q[..., :MLA_NOPE], apply_rope(q[..., MLA_NOPE:], cos_m, sin_m)
    kv = (rms_norm(c_kv, kv_norm_g) @ w_ukv).reshape(B, T, MLA_HEADS, MLA_NOPE + MLA_V)
    k_nope, v_m = kv[..., :MLA_NOPE], kv[..., MLA_NOPE:]
    k_pe = apply_rope(k_pe[:, :, None, :], cos_m, sin_m)[:, :, 0]
    o_m = mla_attention(q_nope, q_pe, k_nope, k_pe, v_m).reshape(B, T, MLA_HEADS * MLA_V)

    qn = partial_rope(q_n.reshape(B, T, NSA_HEADS, NSA_HD), cos_n, sin_n)
    kvs = kv_n.reshape(B, T, 6, NSA_KV_HEADS, NSA_HD)
    k_c = partial_rope(kvs[:, :, 0], cos_n, sin_n)
    k_s = partial_rope(kvs[:, :, 2], cos_n, sin_n)
    k_w = partial_rope(kvs[:, :, 4], cos_n, sin_n)
    gates = jax.nn.sigmoid(g_n.reshape(B, T, NSA_HEADS, 3))
    o_n = nsa_attention(qn, k_c, kvs[:, :, 1], k_s, kvs[:, :, 3], k_w, kvs[:, :, 5], gates,
                        cmp_pe_k, cmp_k_w1, cmp_k_b1, cmp_k_w2, cmp_pe_v, cmp_v_w1, cmp_v_b1, cmp_v_w2)

    y = jax.nn.sigmoid(gate_m) * (o_m @ w_proj_mla) + jax.nn.sigmoid(gate_n) * (o_n @ w_proj_nsa)
    return y @ w_out

def second_inputs(seed: int = 0) -> dict:
    key = jax.random.key(seed)
    ks = iter(jax.random.split(key, 64))

    def w(shape, fan_in, scale=1.0):
        return jax.random.normal(next(ks), (DEPTH_2,) + shape, jnp.float32) * (scale * fan_in ** -0.5)

    def gain(n):
        return 1.0 + 0.02 * jax.random.normal(next(ks), (DEPTH_2, n), jnp.float32)

    def small(shape, s=0.02):
        return s * jax.random.normal(next(ks), (DEPTH_2,) + shape, jnp.float32)

    return {
        'x': jax.random.normal(next(ks), (BATCH, SEQ, D_MODEL), jnp.float32),
        'ln_f1_g': gain(D_MODEL), 'ln_f1_b': small((D_MODEL,)),
        'ffn1_wg': w((D_MODEL, D_FF_2), D_MODEL), 'ffn1_wu': w((D_MODEL, D_FF_2), D_MODEL),
        'ffn1_wd': w((D_FF_2, D_MODEL), D_FF_2, BETA),
        'w_in': w((D_MODEL, D_IN_2), D_MODEL),
        'q_norm_g': gain(MLA_Q_RANK), 'w_uq': w((MLA_Q_RANK, MLA_HEADS * (MLA_NOPE + MLA_ROPE)), MLA_Q_RANK),
        'kv_norm_g': gain(MLA_KV_RANK), 'w_ukv': w((MLA_KV_RANK, MLA_HEADS * (MLA_NOPE + MLA_V)), MLA_KV_RANK),
        'cmp_pe_k': small((L_CMP, NSA_HD), 0.1), 'cmp_k_w1': w((L_CMP * NSA_HD, CMP_HIDDEN), L_CMP * NSA_HD),
        'cmp_k_b1': small((CMP_HIDDEN,)), 'cmp_k_w2': w((CMP_HIDDEN, NSA_HD), CMP_HIDDEN),
        'cmp_pe_v': small((L_CMP, NSA_HD), 0.1), 'cmp_v_w1': w((L_CMP * NSA_HD, CMP_HIDDEN), L_CMP * NSA_HD),
        'cmp_v_b1': small((CMP_HIDDEN,)), 'cmp_v_w2': w((CMP_HIDDEN, NSA_HD), CMP_HIDDEN),
        'w_proj_mla': w((MLA_HEADS * MLA_V, D_MODEL), MLA_HEADS * MLA_V),
        'w_proj_nsa': w((NSA_HEADS * NSA_HD, D_MODEL), NSA_HEADS * NSA_HD),
        'w_out': w((D_MODEL, D_MODEL), D_MODEL, BETA),
        'ln_mix_g': gain(D_MODEL), 'ln_mix_b': small((D_MODEL,)),
        'ffn2_wg': w((D_MODEL, D_FF_2), D_MODEL), 'ffn2_wu': w((D_MODEL, D_FF_2), D_MODEL),
        'ffn2_wd': w((D_FF_2, D_MODEL), D_FF_2, BETA),
        'ln_f2_g': gain(D_MODEL), 'ln_f2_b': small((D_MODEL,)),
    }

def second_block(x, ln_f1_g, ln_f1_b, ffn1_wg, ffn1_wu, ffn1_wd, w_in, q_norm_g, w_uq, kv_norm_g, w_ukv,
              cmp_pe_k, cmp_k_w1, cmp_k_b1, cmp_k_w2, cmp_pe_v, cmp_v_w1, cmp_v_b1, cmp_v_w2,
              w_proj_mla, w_proj_nsa, w_out, ln_mix_g, ln_mix_b,
              ffn2_wg, ffn2_wu, ffn2_wd, ln_f2_g, ln_f2_b):
    T = x.shape[1]
    cos_m, sin_m = rope_tables(MLA_ROPE, T)
    cos_n, sin_n = rope_tables(NSA_ROT, T)
    for l in range(DEPTH_2):
        x = layer_norm(ALPHA * x + 0.5 * swiglu(x, ffn1_wg[l], ffn1_wu[l], ffn1_wd[l]), ln_f1_g[l], ln_f1_b[l])
        mix = token_mixer(x, w_in[l], q_norm_g[l], w_uq[l], kv_norm_g[l], w_ukv[l],
                          cmp_pe_k[l], cmp_k_w1[l], cmp_k_b1[l], cmp_k_w2[l],
                          cmp_pe_v[l], cmp_v_w1[l], cmp_v_b1[l], cmp_v_w2[l],
                          w_proj_mla[l], w_proj_nsa[l], w_out[l], cos_m, sin_m, cos_n, sin_n)
        x = layer_norm(ALPHA * x + mix, ln_mix_g[l], ln_mix_b[l])
        x = layer_norm(ALPHA * x + 0.5 * swiglu(x, ffn2_wg[l], ffn2_wu[l], ffn2_wd[l]), ln_f2_g[l], ln_f2_b[l])
    return x


def setup_inputs(seed=0):
    out = dict(first_inputs(seed))
    for name, value in second_inputs(seed + 1).items():
        if name != "x":
            out[name + "_2"] = value
    return out


def reference(
    x, norm_mix, w_in, A_re, A_im, log_dt, B_re, B_im, C_re, C_im, D_skip, w_glu, b_glu,
    w_up_ssm, w_up_attn, w_gate, b_gate, w_out, norm_mlp, w_ff1, w_ff2, norm_final, ln_f1_g_2,
    ln_f1_b_2, ffn1_wg_2, ffn1_wu_2, ffn1_wd_2, w_in_2, q_norm_g_2, w_uq_2, kv_norm_g_2,
    w_ukv_2, cmp_pe_k_2, cmp_k_w1_2, cmp_k_b1_2, cmp_k_w2_2, cmp_pe_v_2, cmp_v_w1_2, cmp_v_b1_2,
    cmp_v_w2_2, w_proj_mla_2, w_proj_nsa_2, w_out_2, ln_mix_g_2, ln_mix_b_2, ffn2_wg_2,
    ffn2_wu_2, ffn2_wd_2, ln_f2_g_2, ln_f2_b_2,
):
    x = first_block(
        x, norm_mix, w_in, A_re, A_im, log_dt, B_re, B_im, C_re, C_im, D_skip, w_glu, b_glu,
        w_up_ssm, w_up_attn, w_gate, b_gate, w_out, norm_mlp, w_ff1, w_ff2, norm_final,
    )
    return second_block(
        x, ln_f1_g_2, ln_f1_b_2, ffn1_wg_2, ffn1_wu_2, ffn1_wd_2, w_in_2, q_norm_g_2, w_uq_2,
        kv_norm_g_2, w_ukv_2, cmp_pe_k_2, cmp_k_w1_2, cmp_k_b1_2, cmp_k_w2_2, cmp_pe_v_2,
        cmp_v_w1_2, cmp_v_b1_2, cmp_v_w2_2, w_proj_mla_2, w_proj_nsa_2, w_out_2, ln_mix_g_2,
        ln_mix_b_2, ffn2_wg_2, ffn2_wu_2, ffn2_wd_2, ln_f2_g_2, ln_f2_b_2,
    )


_drawn_inputs = setup_inputs


def setup_inputs(seed=0):
    import zlib

    import numpy as np

    out = dict(_drawn_inputs(seed))
    spreads = {}
    factors = {'norm_mix': 5.144,
     'A_re': 64.0,
     'A_im': 3.159,
     'log_dt': 3.368,
     'B_re': 4.492,
     'B_im': 4.495,
     'C_re': 4.512,
     'C_im': 4.514,
     'b_glu': 8.0,
     'b_gate': 8.0,
     'norm_mlp': 3.25,
     'norm_final': 2.691,
     'q_norm_g_2': 8.0,
     'kv_norm_g_2': 8.0,
     'cmp_pe_k_2': 8.0,
     'cmp_k_w1_2': 3.432,
     'cmp_k_b1_2': 37.444,
     'cmp_k_w2_2': 3.366,
     'cmp_pe_v_2': 6.732,
     'cmp_v_b1_2': 8.0}
    for name, (base, spread) in spreads.items():
        noise = np.random.default_rng([zlib.crc32(name.encode()), seed]).standard_normal(out[name].shape)
        drawn = base * np.exp(spread * noise) if base else spread * noise
        out[name] = __import__('jax').numpy.asarray(drawn.astype(out[name].dtype))
    for name, factor in factors.items():
        out[name] = (out[name] * factor).astype(out[name].dtype)
    return out
```

```python
from contextlib import ExitStack

import numpy as np

import concourse.bass as bass
from concourse import mybir

F32 = mybir.dt.float32
F32R = mybir.dt.float32r
BF16 = mybir.dt.bfloat16
ALU = mybir.AluOpType
ACT = mybir.ActivationFunctionType
AX = mybir.AxisListType

P = 128
T = 256
NTT = T // P
D = 1024
KD = D // P
DS = 512
KS = DS // P
HEADS = 8
HD = 64
STATES = 64
NG = 32
ST = NG * STATES // P
FF1 = 4096
FF2 = 2816
LAYERS = 2
SLAB = 2048
WCOLS = SLAB // KD
PI = float(np.pi)
ROUND = 12582912.0
NEG = -1e30
ALPHA = (2 * LAYERS) ** 0.25
EPS_RMS = 1e-6
EPS_LN = 1e-5
Q_RANK, KV_RANK, ROPE_M = 256, 128, 32
QK_M = HD + ROPE_M
SCALE_M = QK_M ** -0.5
SCALE_N = HD ** -0.5
ROT_N = HD // 4
THETA = 500000.0
S_CMP, L_CMP = 16, 32
N_CMP = (T - L_CMP) // S_CMP + 1
KVH = 2
HPG = HEADS // KVH
C_Q, C_KV = 0, Q_RANK
C_QN = C_KV + KV_RANK + ROPE_M
C_KVN = C_QN + HEADS * HD
C_GN = C_KVN + 6 * KVH * HD
C_GM = C_GN + 3 * HEADS

ROW1 = {}
_n = 0
for _name, _rows in (("norm_mix", 8), ("norm_mlp", 8), ("norm_final", 8), ("D_skip", 4), ("b_glu", 4),
                     ("b_gate", 16), ("A_re", 16), ("A_im", 16)):
    ROW1[_name] = _n
    _n += _rows
ROWS1 = _n
ROW2 = {}
_n = 0
for _name, _rows in (("ln_f1_g", 8), ("ln_f1_b", 8), ("ln_mix_g", 8), ("ln_mix_b", 8), ("ln_f2_g", 8),
                     ("ln_f2_b", 8), ("q_norm_g", 2), ("kv_norm_g", 1), ("cmp_k_b1", 1), ("cmp_v_b1", 1),
                     ("cmp_pe_k", 16), ("cmp_pe_v", 16)):
    ROW2[_name] = _n
    _n += _rows
ROWS2 = _n


UPTO = 'full'


def shape_tables():
    def rope(rot, rows, at):
        inv = 1.0 / (np.float32(THETA) ** (np.arange(0, rot, 2, dtype=np.float32) / np.float32(rot)))
        ang = np.arange(T, dtype=np.float32)[:, None] * inv[None, :].astype(np.float32)
        cos, sin = np.cos(ang).astype(np.float32), np.sin(ang).astype(np.float32)
        c, s = np.ones((rows, T), np.float32), np.zeros((rows, T), np.float32)
        perm = np.zeros((rows, rows), np.float32)
        half = rot // 2
        for a in at:
            c[a:a + half] = cos.T
            c[a + half:a + rot] = cos.T
            s[a:a + half] = -sin.T
            s[a + half:a + rot] = sin.T
            for r in range(half):
                perm[a + half + r, a + r] = 1.0
                perm[a + r, a + half + r] = 1.0
        return c, s, perm
    cn, sn, pn = rope(ROT_N, P, (0, HD))
    cm, sm, pm = rope(ROPE_M, P, (0, HD))
    steps = np.broadcast_to(np.arange(T, dtype=np.float32), (P, T))
    return np.concatenate([cn, sn, cm, sm, pn, pm, steps], axis=1)


def plan():
    slabs, used, last = [], [0, 0, 0], [2]

    def add(what, part, slot=None):
        if slot is None:
            slot = (last[0] + 1) % 3
        slabs.append((what, part, slot, used[slot]))
        used[slot] += 1
        last[0] = slot

    where = {}

    def mark(name):
        where[name] = len(slabs)

    mark("in1")
    for n in range(8):
        add("in1", n)
    mark("gate1")
    for n in range(8):
        add("gate1", n)
    mark("glu")
    add("glu", 0)
    mark("up1")
    for n, w in enumerate(("up_attn", "up_ssm", "up_attn", "up_ssm")):
        add(w, n // 2)
    mark("out1")
    for n in range(4):
        add("out1", n, {3: 1}.get(n))
    mark("ffn1")
    add("ff1", 0, 2)
    for i in range(1, 16):
        add("ff1", i, 0)
        add("ff2", i - 1, 1)
    add("ff2", 15, 2)

    def ffn(tag, l):
        add(tag + "_g", (l, 0), 0)
        add(tag + "_u", (l, 0), 2)
        for i in range(1, 11):
            add(tag + "_g", (l, i), 0)
            add(tag + "_d", (l, i - 1), 1)
            add(tag + "_u", (l, i), 2)
        add(tag + "_d", (l, 10), 1)

    for l in range(LAYERS):
        mark(("fa", l))
        ffn("fa", l)
        mark(("in2", l))
        for n in range(7):
            add("in2", (l, n))
        mark(("uq", l))
        add("uq", (l, 0))
        mark(("cmp", l))
        add("cmp_k", (l, 0))
        add("cmp_v", (l, 0))
        mark(("ukv", l))
        add("ukv", (l, 0))
        mark(("gate2", l))
        for n in range(8):
            add("gate2", (l, n))
        mark(("proj", l))
        for n, w in enumerate(("proj_m", "proj_n", "proj_m", "proj_n")):
            add(w, (l, n // 2))
        mark(("out2", l))
        for n in range(4):
            add("out2", (l, n))
        mark(("fb", l))
        ffn("fb", l)
    return slabs, where


def hybrid_ssm_attention_kernel(nc, a, out):
    slabs, where = plan()
    if UPTO == "b1":
        slabs = slabs[:where[("fa", 0)]]
    for n, (_, _, slot, _u) in enumerate(slabs):
        assert n == 0 or slabs[n - 1][2] != slot

    def num_loads(what, part):
        return 2 if what == "in2" and part[1] in (1, 2, 3, 5, 6) else 1

    loads_so_far, total = [], [0, 0, 0]
    for what, part, slot, _u in slabs:
        total[slot] += num_loads(what, part)
        loads_so_far.append(total[slot])

    with ExitStack() as ctx:
        def sb(name, shape, dt=F32):
            return ctx.enter_context(nc.sbuf_tensor(name, shape, dt))

        def sem(name):
            return ctx.enter_context(nc.semaphore(name))

        bank = [ctx.enter_context(nc.psum_tensor(f"bank{i}", [P, 512], F32)) for i in range(8)]
        raw = sb("raw", [P, 3, SLAB])
        wh = sb("wh", [P, 3, SLAB], F32R)
        wl = sb("wl", [P, 3, SLAB], F32R)
        res = sb("res", [P, KD, T])
        tmp = sb("tmp", [P, KD, T])
        sq = sb("sq", [P, KD, T])
        uh = sb("uh", [P, KD, T], F32R)
        ul = sb("ul", [P, KD, T], F32R)
        bh = sb("bh", [P, KD, T], F32R)
        bl = sb("bl", [P, KD, T], F32R)
        hh = sb("hh", [P, 2, T], F32R)
        hl = sb("hl", [P, 2, T], F32R)
        ckh = sb("ckh", [P, T], F32R)
        ckl = sb("ckl", [P, T], F32R)
        act_out = sb("act_out", [P, 2, T])
        hid = sb("hid", [P, 2, T])
        stat = sb("stat", [P, 2, T])
        rstd = sb("rstd", [P, T])
        gates = sb("gates", [P, 2 * KD, T])
        shared = sb("shared", [P, 4096])
        small = sb("small", [P, 4096])
        tables = sb("tables", [P, 2560])
        steps_t = sb("steps_t", [P, T])
        vec1 = sb("vec1", [P, ROWS1])
        vec2 = sb("vec2", [P, LAYERS, ROWS2])
        cmp_w2 = sb("cmp_w2", [P, LAYERS, 2, 2, HD])
        ident = sb("ident", [P, P])
        identb = sb("identb", [P, P], BF16)
        causal = sb("causal", [P, P], BF16)
        earlier = sb("earlier", [P, P], BF16)
        suffix = sb("suffix", [P, P])
        minus1 = sb("minus1", [P, P])
        mean_w = sb("mean_w", [P, P])
        zero_w = sb("zero_w", [P, P], F32R)
        cmask = sb("cmask", [P, NTT, N_CMP])
        cvalid = sb("cvalid", [P, NTT, N_CMP])
        cols1 = sb("cols1", [P, 16, 16])
        kcc = sb("kcc", [P, KVH * N_CMP])
        half_b = sb("half_b", [P, 2 * KD])
        quarter = sb("quarter", [P, 4])

        raw_full = [sem(f"raw_full{i}") for i in range(3)]
        rounded = [sem(f"rounded{i}") for i in range(3)]
        split = [sem(f"split{i}") for i in range(3)]
        used = [sem(f"used{i}") for i in range(3)]
        dve_chain, act_chain, pool_chain = sem("dve_chain"), sem("act_chain"), sem("pool_chain")
        dve_n, act_n, pool_n = [0], [0], [0]
        consts = sem("consts")
        vec_in = sem("vec_in")
        x_in = sem("x_in")
        ssm_in = sem("ssm_in")
        tr_ready = sem("tr_ready")
        tr_taken = sem("tr_taken")
        norm_in = sem("norm_in")
        sum_done = sem("sum_done")
        centred = sem("centred")
        squared = sem("squared")
        var_done = sem("var_done")
        root_done = sem("root_done")
        scaled = sem("scaled")
        norm_h = sem("norm_h")
        res_ready = sem("res_ready")
        norm_out = sem("norm_out")
        ffn_act = sem("ffn_act")
        hid_ready = sem("hid_ready")
        hid_step = sem("hid_step")
        lin_free = [sem("lin_free0"), sem("lin_free1")]

        def two(b):
            return b[:, :].rearrange("p (a t) -> p a t", a=2)

        def chain(eng, count, s, ins):
            count[0] += 1
            ins.then_inc(s, 1)
            eng.wait_ge(s, count[0])

        def slab_view(buf, slot, kt, c):
            return buf[:, slot, 0:kt * c].rearrange("p (k c) -> p k c", c=c)

        def cols(w, c0, c):
            return w[:, bass.ds(c0, c)].rearrange("(k p) c -> p k c", p=P)

        def rows(w, k0, kt):
            return w[bass.ds(k0 * P, kt * P), :].rearrange("(k p) c -> p k c", p=P)

        def slab_loads(what, part, slot):
            def one(w_cols, kt, c):
                return [(slab_view(raw, slot, kt, c), w_cols)]
            if what == "in1":
                return one(cols(a["w_in"][0], part * WCOLS, WCOLS), KD, WCOLS)
            if what == "gate1":
                return one(cols(a["w_gate"][0], part * WCOLS, WCOLS), KD, WCOLS)
            if what == "glu":
                return one(cols(a["w_glu"][0], 0, DS), KS, DS)
            if what in ("up_ssm", "up_attn"):
                return one(cols(a["w_" + what][0], part * 512, 512), KS, 512)
            if what == "out1":
                return one(cols(a["w_out"][0], part * WCOLS, WCOLS), KD, WCOLS)
            if what == "ff1":
                return one(cols(a["w_ff1"][0], part * WCOLS, WCOLS), KD, WCOLS)
            if what == "ff2":
                return one(rows(a["w_ff2"][0], part * 2, 2), 2, D)
            l, i = part
            if what[:2] in ("fa", "fb"):
                ffn = "ffn1" if what[:2] == "fa" else "ffn2"
                w = a[f"{ffn}_w{what[3]}_2"][l]
                if what[3] == "d":
                    return one(rows(w, i * 2, 2), 2, D)
                return one(cols(w, i * WCOLS, WCOLS), KD, WCOLS)
            if what == "in2":
                w = a["w_in_2"][l]
                if i == 0:
                    return one(cols(w, C_Q, Q_RANK), KD, Q_RANK)
                if i == 1:
                    n1, n2 = KV_RANK + ROPE_M, 3 * HEADS
                    v = slab_view(raw, slot, KD, n1 + n2)
                    return [(v[:, :, 0:n1], cols(w, C_KV, n1)), (v[:, :, n1:], cols(w, C_GN, n2))]
                if i in (2, 3):
                    v = slab_view(raw, slot, KD, WCOLS)
                    return [(v[:, :, g * 2 * HD:(g + 1) * 2 * HD], cols(w, C_QN + (g * HPG + 2 * (i - 2)) * HD, 2 * HD))
                            for g in range(KVH)]
                if i == 4:
                    return one(cols(w, C_KVN, WCOLS), KD, WCOLS)
                v = slab_view(raw, slot, KD, WCOLS)
                return [(v[:, :, j * P:(j + 1) * P], cols(w, C_KVN + (2 + i - 5 + 2 * j) * P, P)) for j in range(2)]
            if what == "uq":
                return one(cols(a["w_uq_2"][l], 0, HEADS * QK_M), 2, HEADS * QK_M)
            if what == "ukv":
                return one(cols(a["w_ukv_2"][l], 0, 2 * HEADS * HD), 1, 2 * HEADS * HD)
            if what in ("cmp_k", "cmp_v"):
                return one(cols(a[what + "_w1_2"][l], 0, P), 16, P)
            if what == "gate2":
                return one(cols(a["w_in_2"][l], C_GM + i * WCOLS, WCOLS), KD, WCOLS)
            if what in ("proj_m", "proj_n"):
                w = a["w_proj_mla_2" if what == "proj_m" else "w_proj_nsa_2"][l]
                return one(cols(w, i * 512, 512), KS, 512)
            assert what == "out2"
            return one(cols(a["w_out_2"][l], i * WCOLS, WCOLS), KD, WCOLS)

        def slab_words(what, part):
            if what == "in2" and part[1] == 1:
                return KD * (KV_RANK + ROPE_M + 3 * HEADS)
            return {"uq": 2 * HEADS * QK_M, "ukv": 2 * HEADS * HD}.get(what, SLAB)

        def sp_slab(sp, n, part=None, more=0):
            what, p0, slot, u = slabs[n]
            part = p0 if part is None else part
            if not (isinstance(more, int) and u + more == 0):
                sp.wait_ge(split[slot], more + u)
            for dst, src in slab_loads(what, part, slot):
                sp.dma_start(dst, src).then_inc(raw_full[slot], 16)

        def slab_pieces(buf, n, halves):
            what, part, slot, _u = slabs[n]
            if what == "in2" and part[1] in (2, 3):
                v = slab_view(buf, slot, KD, WCOLS)
                if halves:
                    return [v.rearrange("p k (h g d) -> p g k h d", g=KVH, d=HD)[:, g] for g in range(KVH)]
                return [v.rearrange("p k (g h d) -> p g k h d", g=KVH, d=HD)[:, g] for g in range(KVH)]
            return [buf[:, slot, 0:slab_words(what, part)]]

        def act_round(act, n, more=0):
            what, part, slot, u = slabs[n]
            words = slab_words(what, part)
            act.wait_ge(raw_full[slot], more * 16 + 16 * loads_so_far[n])
            if not (isinstance(more, int) and u + more == 0):
                act.wait_ge(used[slot], more + u)
            for src, dst in zip(slab_pieces(raw, n, False), slab_pieces(wh, n, True)):
                ins = act.copy(dst, src)
            ins.then_inc(rounded[slot], 1)

        def dve_split(dve, n, more=0):
            what, part, slot, u = slabs[n]
            words = slab_words(what, part)
            dve.wait_ge(rounded[slot], more + u + 1)
            for src, upper, dst in zip(slab_pieces(raw, n, False), slab_pieces(wh, n, True), slab_pieces(wl, n, True)):
                ins = dve.tensor_tensor(dst, src, upper.bitcast(F32), ALU.subtract)
            ins.then_inc(split[slot], 1)

        def act_round_half(act, n, j):
            _w, _p, slot, u = slabs[n]
            if j == 0:
                act.wait_ge(raw_full[slot], 16 * loads_so_far[n])
                act.wait_ge(used[slot], u)
            c = slice(j * SLAB // 2, (j + 1) * SLAB // 2)
            ins = act.copy(wh[:, slot, c], raw[:, slot, c])
            if j == 1:
                ins.then_inc(rounded[slot], 1)

        def dve_split_quarter(dve, n, j):
            _w, _p, slot, u = slabs[n]
            if j == 0:
                dve.wait_ge(rounded[slot], u + 1)
            c = slice(j * SLAB // 4, (j + 1) * SLAB // 4)
            ins = dve.tensor_tensor(wl[:, slot, c], raw[:, slot, c], wh[:, slot, c].bitcast(F32), ALU.subtract)
            if j == 3:
                ins.then_inc(split[slot], 1)

        def pe_slab(pe, n, more=0):
            slot, u = slabs[n][2:]
            pe.wait_ge(split[slot], more + u + 1)
            return slot

        def mm3(pe, o, wa, wb, xa, xb, start, stop, swap=False):
            for n, (w, x) in enumerate(((wa, xa), (wa, xb), (wb, xa))):
                if swap:
                    w, x = x, w
                mm = pe.matmul(o, w, x, start=start and n == 0, stop=stop and n == 2, skip_group_check=True)
            return mm

        def ffn_pe(pe, tag, n0, iters, has_up, ih0, first_ready):
            for b in range(4):
                for c in range(4):
                    pe.matmul(bank[b][:, c * P:(c + 1) * P], zero_w[:, :], zero_w[:, :], start=c == 0, stop=True,
                              skip_group_check=True)
            per = 3 if has_up else 2

            def up_half(n, more, b, ready=None):
                slot = pe_slab(pe, n, more)
                for f in range(2):
                    for k in range(KD):
                        if ready is not None and f == 0:
                            pe.wait_ge(norm_out, ready + k + 1)
                        mm = mm3(pe, bank[b][:, f * T:(f + 1) * T],
                                 slab_view(wh, slot, KD, WCOLS)[:, k, f * P:(f + 1) * P],
                                 slab_view(wl, slot, KD, WCOLS)[:, k, f * P:(f + 1) * P],
                                 uh[:, k, :], ul[:, k, :], k == 0, k == KD - 1)
                mm.then_inc(used[slot], 1)

            def gate(n, more=0, i=None, ready=None):
                if i is not None:
                    pe.wait_ge(ffn_act, i + ih0)
                up_half(n, more, 4, ready)

            def down(n, i, more=0):
                slot = pe_slab(pe, n, more)
                pe.wait_ge(hid_ready, i + ih0 + 1)
                for m in range(KD):
                    for k in range(2):
                        mm = mm3(pe, bank[m // 2][:, (m % 2) * T:(m % 2 + 1) * T],
                                 slab_view(wh, slot, 2, D)[:, k, m * P:(m + 1) * P],
                                 slab_view(wl, slot, 2, D)[:, k, m * P:(m + 1) * P],
                                 hh[:, k, :], hl[:, k, :], False, False)
                mm.then_inc(used[slot], 1)

            gate(n0, ready=first_ready)
            if has_up:
                up_half(n0 + 1, 0, 5)
            n1 = n0 + (2 if has_up else 1)
            with pe.Fori(1, iters, 1) as i:
                gate(n1, i - 1, i)
                down(n1 + 1, i - 1, i - 1)
                if has_up:
                    up_half(n1 + 2, i - 1, 5)
            down(n1 + per * (iters - 1), iters - 1)

        def ffn_split(eng, do, n0, iters, has_up, epilogue):
            per = 3 if has_up else 2
            n1 = n0 + per - 1

            def step(n, what, i, more=0, i0=0):
                epilogue(what, n, i, more)
                if n + 2 < len(slabs):
                    do(eng, n + 2, more)

            def turn(i, more, at):
                step(at, "gate", i, more)
                step(at + 1, "down", i - 1, more)
                if has_up:
                    step(at + 2, "up", i, more)

            step(n0, "gate", 0)
            if has_up:
                step(n0 + 1, "up", 0)
            with eng.Fori(1, iters - 1, 1) as i:
                turn(i, i - 1, n1)
            last = n1 + per * (iters - 2)
            turn(iters - 1, 0, last)
            step(last + per, "down", iters - 1)

        def ffn_act_engine(act, n0, iters, has_up, ih0):
            def epilogue(what, n, i, more):
                if what != "gate":
                    return
                slot, u = slabs[n][2:]
                if not (isinstance(i, int) and i == 0):
                    act.wait_ge(hid_ready, i + ih0)
                act.wait_ge(used[slot], more + u + 1)
                act.activation(act_out[:, :, :], two(bank[4]), ACT.Silu if has_up else ACT.Relu).then_inc(ffn_act, 1)
            ffn_split(act, act_round, n0, iters, has_up, epilogue)

        def ffn_dve_engine(dve, n0, iters, has_up, ih0):
            def epilogue(what, n, i, more):
                if (has_up and what != "up") or (not has_up and what == "gate" and not (isinstance(i, int) and i == 0)):
                    return
                if not has_up and what == "down":
                    i = i + 1
                    if isinstance(i, int) and i == iters:
                        return
                slot, u = slabs[n][2:]
                dve.wait_ge(used[slot], more + u + 1)
                dve.wait_ge(ffn_act, i + ih0 + 1)
                other = two(bank[5]) if has_up else act_out[:, :, :]
                dve.tensor_tensor(hid[:, :, :], act_out[:, :, :], other, ALU.mult).then_inc(hid_step, 1)
                dve.wait_ge(hid_step, 2 * i + (2 * ih0 + 1))
                dve.tensor_copy(hh[:, :, :], hid[:, :, :]).then_inc(hid_step, 1)
                dve.wait_ge(hid_step, 2 * i + (2 * ih0 + 2))
                dve.tensor_tensor(hl[:, :, :], hid[:, :, :], hh[:, :, :].bitcast(F32), ALU.subtract).then_inc(hid_ready, 1)
            ffn_split(dve, dve_split, n0, iters, has_up, epilogue)

        def norm_pe(pe, idx, ln, tb, kt, src):
            if ln is not None:
                for k in range(kt):
                    pe.wait_ge(norm_in, tb + k + 1)
                    mm = pe.matmul(bank[6][:, 0:T], mean_w[:, :], src(k), start=k == 0, stop=k == kt - 1)
                mm.then_inc(sum_done, 1)
            for k in range(kt):
                pe.wait_ge(squared, tb + k + 1)
                mm = pe.matmul(bank[6][:, T:2 * T], mean_w[:, :], sqbuf(k), start=k == 0, stop=k == kt - 1)
            mm.then_inc(var_done, 1)

        def sqbuf(k):
            return sq[:, k, :]

        def norm_act(act, idx, ln, tb, kt, src, scale, eps, y, bias, o_h):
            for k in range(kt):
                if ln is not None:
                    act.wait_ge(centred, ln * KD + k + 1)
                else:
                    act.wait_ge(norm_in, tb + k + 1)
                act.activation(sqbuf(k), src(k), ACT.Square).then_inc(squared, 1)
            act.wait_ge(var_done, idx + 1)
            act.activation(rstd[:, :], bank[6][:, T:2 * T], ACT.Sqrt, scale=scale, bias=quarter[:, eps:eps + 1]).then_inc(root_done, 1)
            if o_h is None:
                return
            for k in range(kt):
                act.wait_ge(scaled, tb + k + 1)
                if bias is None:
                    ins = act.copy(o_h(k), y(k))
                else:
                    ins = act.activation(o_h(k), y(k), ACT.Identity, bias=bias(k))
                ins.then_inc(norm_h, 1)

        def norm_dve(dve, idx, ln, tb, kt, src, gain, y, bias, o_h, o_l, res_scale=None):
            if ln is not None:
                dve.wait_ge(sum_done, ln + 1)
                chain(dve, dve_n, dve_chain, dve.tensor_copy(stat[:, 0, :], bank[6][:, 0:T]))
                for k in range(kt):
                    dve.tensor_tensor(src(k), src(k), stat[:, 0, :], ALU.subtract).then_inc(centred, 1)
            dve.wait_ge(root_done, idx + 1)
            chain(dve, dve_n, dve_chain, dve.reciprocal(rstd[:, :], rstd[:, :]))
            for k in range(kt + 2):
                if k < kt:
                    dve.scalar_tensor_tensor(out=y(k), in0=src(k), scalar=gain(k), in1=rstd[:, :],
                                             op0=ALU.mult, op1=ALU.mult).then_inc(scaled, 1)
                if k >= 2 and o_h is not None:
                    dve.wait_ge(norm_h, tb + k - 1)
                    if bias is None:
                        ins = dve.tensor_tensor(o_l(k - 2), y(k - 2), o_h(k - 2).bitcast(F32), ALU.subtract)
                    else:
                        ins = dve.scalar_tensor_tensor(out=o_l(k - 2), in0=y(k - 2), scalar=bias(k - 2),
                                                       in1=o_h(k - 2).bitcast(F32), op0=ALU.add, op1=ALU.subtract)
                    ins.then_inc(norm_out, 1)
            if res_scale is not None:
                for k in range(kt):
                    if bias is None:
                        dve.tensor_scalar(res[:, k, :], y(k), res_scale, None, ALU.mult).then_inc(res_ready, 1)
                    else:
                        dve.tensor_scalar(res[:, k, :], y(k), bias(k), res_scale, ALU.add, ALU.mult).then_inc(res_ready, 1)

        norms, n_ln, n_tiles = {}, 0, 0
        for name, is_ln, kt in [("mix1", 0, KD), ("mlp1", 0, KD), ("final1", 0, KD)] + [
                ((w, l), is_ln, kt) for l in range(LAYERS)
                for w, is_ln, kt in (("fa", 1, KD), ("q", 0, 2), ("kv", 0, 1), ("mix", 1, KD), ("fb", 1, KD))]:
            norms[name] = (len(norms), n_ln if is_ln else None, n_tiles)
            n_ln += is_ln
            n_tiles += kt
        tile_u = lambda k: uh[:, k, :]
        tile_l = lambda k: ul[:, k, :]
        tile_tmp = lambda k: tmp[:, k, :]
        tile_res = lambda k: res[:, k, :]

        def v1(name):
            return lambda k: vec1[:, ROW1[name] + k:ROW1[name] + k + 1]

        def v2(l, name):
            return lambda k: vec2[:, l, ROW2[name] + k:ROW2[name] + k + 1]

        gflat = gates[:, :, :].rearrange("p a t -> p (a t)")
        x_tok = gflat[:, 0:2048].rearrange("p (a d) -> p a d", a=NTT)
        flat = lambda t: t[:, :, :].rearrange("p a t -> p (a t)")
        rows_in = flat(act_out)
        b_nat = [gflat[:, 2048 + 256 * i:2304 + 256 * i].rearrange("p (s c) -> p s c", c=16) for i in range(2)]
        b_bar = [gflat[:, 2560 + 256 * i:2816 + 256 * i].rearrange("p (s c) -> p s c", c=16) for i in range(2)]
        b_diag = [gflat[:, 3072 + 512 * i:3584 + 512 * i].rearrange("p (s c) -> p s c", c=32) for i in range(2)]
        c_nat = [flat(hid).rearrange("p (i a s) -> p i a s", i=4, a=2), flat(stat).rearrange("p (i a s) -> p i a s", i=4, a=2)]
        b_t = [tables[:, 512 * i:512 * i + 512].rearrange("p (i m) -> p i m", i=4) for i in range(2)]
        c_t = [tables[:, 1024 + 512 * i:1536 + 512 * i].rearrange("p (s c) -> p s c", c=32) for i in range(3)]
        us = tmp[:, 0:KS, :]
        v_tok = tmp[:, KS:, :].rearrange("p a t -> p (a t)").rearrange("p (a d) -> p a d", a=NTT)
        qT, kT = sq[:, 0:KS, :], sq[:, KS:, :]
        col = lambda i: cols1[:, i, :]
        (DT, ADT, TURNS, WHOLE, FRAC, DECAY, AFRAC, SIN1, COS1, ARE, AIM, INV, FRE, FIM, CT) = range(15)

        def phase(i, which):
            return shared[:, (i % 2) * 2048 + which * 1024:(i % 2) * 2048 + which * 1024 + 1024].rearrange(
                "p (j t) -> p j t", j=4)
        prod = [small[:, i * 1024:(i + 1) * 1024].rearrange("p (a t) -> p a t", a=4) for i in range(2)]
        ATT = 3 * P
        at_abs, at_pos, at_sp, at_w = (small[:, 2048 + ATT * i:2048 + ATT * (i + 1)] for i in range(4))
        merged = small[:, 0:2048].rearrange("p (k t) -> p k t", k=KD)
        gated = small[:, 2048:3072].rearrange("p (k t) -> p k t", k=4)

        mk = lambda *names: [sem(n) for n in names]
        (prep_dve, prep_act, bt_in, bt_taken, ph_ready, ph_done, bu_done, bu_free, prod_done, y_done,
         y_taken, gelu_h, gelu_l, z_done, z_read, ln_done, sp_done, sp_masked, tri_done, w_exp, w_masked, av_done,
         o_half, o_taken, glu_sig, glu_y, glu_h, glu_l, pair_read, merged_sum, merged_h, merged_l, 
         gn_in, gn_t, w2_in, out_x, vec_taken, cd_in) = mk(
            "prep_dve", "prep_act", "bt_in", "bt_taken", "ph_ready", "ph_done", "bu_done", "bu_free",
            "prod_done", "y_done", "y_taken", "gelu_h", "gelu_l", "z_done", "z_read", "ln_done", "sp_done",
            "sp_masked", "tri_done", "w_exp", "w_masked", "av_done", "o_half", "o_taken", "glu_sig",
            "glu_y", "glu_h", "glu_l", "pair_read", "merged_sum", "merged_h", "merged_l", "gn_in", "gn_t", "w2_in",
            "out_x", "vec_taken", "cd_in")

        tiles_at = {g: [g - 2] for g in range(2, 14)}
        tiles_at[14], tiles_at[15] = [12, 13], [14, 15]
        NSTEP = 16

        def used_by(n):
            return slabs[n][2], slabs[n][3] + 1

        def wait_used(eng, n):
            slot, c = used_by(n)
            eng.wait_ge(used[slot], c)

        def lin_pe(pe, n, b, ready=None, kt=KD, c=WCOLS, tiles=2, xa=tile_u, xb=tile_l, inc=True):
            slot = pe_slab(pe, n)
            for f in range(tiles):
                for k in range(kt):
                    if ready is not None and f == 0:
                        ready(k)
                    mm = mm3(pe, bank[b + f // 2][:, (f % 2) * T:(f % 2 + 1) * T],
                             slab_view(wh, slot, kt, c)[:, k, f * P:(f + 1) * P],
                             slab_view(wl, slot, kt, c)[:, k, f * P:(f + 1) * P],
                             xa(k), xb(k), k == 0, k == kt - 1)
            if inc:
                mm.then_inc(used[slot], 1)
            return mm

        def lin_quarter(pe, n, b, j):
            slot = slabs[n][2]
            for q in range(4 * j, 4 * j + 4):
                f, k = divmod(q, KD)
                mm = mm3(pe, bank[b][:, f * T:(f + 1) * T],
                         slab_view(wh, slot, KD, WCOLS)[:, k, f * P:(f + 1) * P],
                         slab_view(wl, slot, KD, WCOLS)[:, k, f * P:(f + 1) * P],
                         uh[:, k, :], ul[:, k, :], k == 0, k == KD - 1)
            if j == 3:
                mm.then_inc(used[slot], 1)

        def lin_tokens(pe, n, b, c0, width, c, kt=KD, at=0, xa=uh, xb=ul):
            slot = slabs[n][2]
            for tt in range(NTT):
                for k in range(kt):
                    mm = mm3(pe, bank[b][:, at + tt * width:at + (tt + 1) * width],
                             xa[:, k, tt * P:(tt + 1) * P], xb[:, k, tt * P:(tt + 1) * P],
                             slab_view(wh, slot, kt, c)[:, k, c0:c0 + width],
                             slab_view(wl, slot, kt, c)[:, k, c0:c0 + width], k == 0, k == kt - 1)
            return mm

        N_IN1, N_GATE1, N_GLU, N_UP1, N_OUT1, N_FFN1 = (where[w] for w in ("in1", "gate1", "glu", "up1", "out1", "ffn1"))

        def b1_sp(sp):
            sp.dma_start(x_tok, a["x"][0].rearrange("(a p) d -> p a d", p=P)).then_inc(x_in, 16)
            for n in range(N_FFN1):
                sp_slab(sp, n)
            n0 = N_FFN1
            sp_slab(sp, n0)
            with sp.Fori(1, 16, 1) as i:
                sp_slab(sp, n0 + 1, i, i - 1)
                sp_slab(sp, n0 + 2, i - 1, i - 1)
            sp_slab(sp, n0 + 31)

        def pool_consts(pool):
            def link(ins):
                chain(pool, pool_n, pool_chain, ins)
            link(pool.memset(ident[:, :], 0.0))
            link(pool.affine_select(out=ident[:, :], in_=ident[:, :], compare_op=ALU.not_equal, fill=1.0, base=0,
                                    pattern=[[-1, P]], channel_multiplier=1))
            pool.tensor_copy(identb[:, :], ident[:, :]).then_inc(consts, 1)
            pool.memset(mean_w[:, :], 1.0 / D).then_inc(consts, 1)
            link(pool.memset(suffix[:, :], -1.0))
            pool.affine_select(out=suffix[:, :], in_=suffix[:, :], compare_op=ALU.is_ge, fill=0.0, base=0,
                               pattern=[[-1, P]], channel_multiplier=1).then_inc(consts, 1)
            pool.memset(minus1[:, :], -1.0).then_inc(consts, 1)
            link(pool.memset(causal[:, :], 0.0))
            pool.affine_select(out=causal[:, :], in_=causal[:, :], compare_op=ALU.is_ge, fill=NEG, base=0,
                               pattern=[[-1, P]], channel_multiplier=1).then_inc(consts, 1)
            link(pool.memset(earlier[:, :], 0.0))
            pool.affine_select(out=earlier[:, :], in_=earlier[:, :], compare_op=ALU.is_gt, fill=NEG, base=0,
                               pattern=[[1, P]], channel_multiplier=-1).then_inc(consts, 1)
            pool.memset(zero_w[:, :].bitcast(F32), 0.0).then_inc(consts, 1)
            for t, v, f in ((cmask, 0.0, NEG), (cvalid, 1.0, 0.0)):
                link(pool.memset(t[:, :, :], v))
                pool.affine_select(out=t[:, :, :], in_=t[:, :, :], compare_op=ALU.is_ge, fill=f, base=1 - L_CMP,
                                   pattern=[[P, NTT], [-S_CMP, N_CMP]], channel_multiplier=1).then_inc(consts, 1)

        def b1_pool(pool):
            def keep_earlier_keys(t):
                v = t.rearrange("p (a b) -> p a b", b=P)[:, 0:3:2, :]
                return pool.affine_select(out=v, in_=v, compare_op=ALU.is_gt, fill=0.0, base=0,
                                          pattern=[[0, 2], [1, P]], channel_multiplier=-1)
            for h in range(HEADS):
                pool.wait_ge(sp_done, h + 1)
                keep_earlier_keys(at_sp).then_inc(sp_masked, 1)

        def start_act_dmas(act):
            for name, (buf, r0) in [(k, (0, r)) for k, r in ROW1.items()]:
                src = a[name]
                if name in ("A_re", "A_im"):
                    src = src[0].rearrange("(s g) p -> s (g p)", g=2)
                else:
                    src = (src if name == "norm_final" else src[0]).rearrange("(k p) -> k p", p=P)
                act.dma_start(rows_in[r0:r0 + src.shape[0], 0:P], src).then_inc(vec_in, 16)
            act.dma_start(small[0:ST, 0:2], a["log_dt"][0].rearrange("(s g) -> s g", g=2)).then_inc(vec_in, 16)
            for l in range(LAYERS):
                for name, r0 in ROW2.items():
                    src = a[name + "_2"][l]
                    if name.startswith("cmp_pe"):
                        src = src.rearrange("(s g) p -> s (g p)", g=2)
                    else:
                        src = src.rearrange("(k p) -> k p", p=P)
                    act.dma_start(rows_in[r0:r0 + src.shape[0], (1 + l) * P:(2 + l) * P], src).then_inc(vec_in, 16)
            for i, nm in enumerate(("B_re", "B_im")):
                act.dma_start(b_nat[i], a[nm][0].rearrange("(s g) p c -> (g p) s c", g=2)).then_inc(ssm_in, 16)
            for i, nm in enumerate(("C_re", "C_im")):
                for d in range(2):
                    act.dma_start(c_nat[i][:, :, d, :], a[nm][0].rearrange("(i g) c p -> (g c) i p", g=8)).then_inc(ssm_in, 16)
            act.dma_start(steps_t[:, :], a["shape_tables"][:, 4 * T + 2 * P:]).then_inc(ssm_in, 16)
            for l in range(LAYERS):
                for i, nm in enumerate(("cmp_k_w2_2", "cmp_v_w2_2")):
                    for d in range(2):
                        act.dma_start(cmp_w2[:, l, i, d, :], a[nm][l]).then_inc(w2_in, 16)
        N_VEC = 16 * (len(ROW1) + 1 + LAYERS * len(ROW2))

        def b1_pe_start(pe):
            pe.wait_ge(consts, 9)
            pe.wait_ge(vec_in, N_VEC)
            pe.transpose(bank[0][:, 0:ROWS1], rows_in[0:ROWS1, 0:P], ident[0:ROWS1, 0:ROWS1])
            for l in range(LAYERS):
                pe.transpose(bank[0][:, P * (l + 1):P * (l + 1) + ROWS2], rows_in[0:ROWS2, P * (l + 1):P * (l + 2)],
                             ident[0:ROWS2, 0:ROWS2])
            pe.wait_ge(prep_dve, 1)
            pe.transpose(bank[0][:, 3 * P:3 * P + ST], rows_in[0:ST, 3 * P:4 * P], ident[0:ST, 0:ST]).then_inc(tr_ready, 1)
            pe.wait_ge(x_in, 16)
            for k in range(KD):
                for tt in range(NTT):
                    mm = pe.transpose(bank[1 + k // 2][:, (k % 2) * T + tt * P:(k % 2) * T + (tt + 1) * P],
                                      x_tok[:, tt, k * P:(k + 1) * P], ident[:, :])
                if k % 2:
                    mm.then_inc(tr_ready, 1)

        def b1_dve_start(dve):
            link = lambda ins: chain(dve, dve_n, dve_chain, ins)
            dve.memset(quarter[:, 0:1], PI / 2)
            dve.memset(quarter[:, 1:2], EPS_RMS)
            dve.memset(quarter[:, 2:3], EPS_LN).then_inc(cd_in, 1)
            for i in range(2):
                link(dve.memset(b_diag[i], 0.0))
            for i in range(3):
                link(dve.memset(c_t[i], 0.0))
            link(dve.memset(kcc[:, :], 0.0))
            dve.wait_ge(vec_in, N_VEC)
            dve.tensor_copy(rows_in[0:ST, 3 * P:4 * P].rearrange("p (g s) -> p g s", g=2),
                            small[0:ST, 0:2].rearrange("p (g o) -> p g o", o=1).to_broadcast([ST, 2, STATES])).then_inc(prep_dve, 1)
            dve.wait_ge(tr_ready, 1)
            link(dve.tensor_copy(vec1[:, :], bank[0][:, 0:ROWS1]))
            for l in range(LAYERS):
                link(dve.tensor_copy(vec2[:, l, :], bank[0][:, P * (l + 1):P * (l + 1) + ROWS2]))
            link(dve.tensor_scalar(half_b[:, :], vec1[:, ROW1["b_gate"]:ROW1["b_gate"] + 2 * KD], 0.5, None, ALU.mult))
            dve.tensor_copy(col(CT), bank[0][:, 3 * P:3 * P + ST]).then_inc(prep_dve, 1)
            for b in range(4):
                dve.wait_ge(tr_ready, b + 2)
                dve.tensor_copy(res[:, 2 * b:2 * b + 2, :], two(bank[1 + b])).then_inc(norm_in, 2)

        def b1_dve_params(dve):
            link = lambda ins: chain(dve, dve_n, dve_chain, ins)
            TT = lambda o, x, y, op: link(dve.tensor_tensor(o, x, y, op))
            lre, lim = vec1[:, ROW1["A_re"]:ROW1["A_re"] + ST], vec1[:, ROW1["A_im"]:ROW1["A_im"] + ST]
            dve.wait_ge(prep_act, 1)
            TT(col(ADT), lre, col(DT), ALU.mult)
            link(dve.scalar_tensor_tensor(out=col(TURNS), in0=lim, scalar=1.0 / (2 * PI), in1=col(DT), op0=ALU.mult, op1=ALU.mult))
            link(dve.tensor_scalar(col(WHOLE), col(TURNS), ROUND, ROUND, ALU.add, ALU.subtract))
            dve.tensor_tensor(col(FRAC), col(TURNS), col(WHOLE), ALU.subtract).then_inc(prep_dve, 1)
            dve.wait_ge(ssm_in, 16 * 7)
            for i in range(2):
                dve_phase(dve, i)
            dve.wait_ge(prep_act, 2)
            TT(col(ARE), col(DECAY), col(COS1), ALU.mult)
            link(dve.tensor_scalar(col(ARE), col(ARE), 1.0, None, ALU.subtract))
            TT(col(AIM), col(DECAY), col(SIN1), ALU.mult)
            TT(col(INV), lre, lre, ALU.mult)
            TT(col(CT), lim, lim, ALU.mult)
            TT(col(INV), col(INV), col(CT), ALU.add)
            link(dve.reciprocal(col(INV), col(INV)))
            TT(col(FRE), col(ARE), lre, ALU.mult)
            TT(col(CT), col(AIM), lim, ALU.mult)
            TT(col(FRE), col(FRE), col(CT), ALU.add)
            TT(col(FRE), col(FRE), col(INV), ALU.mult)
            TT(col(FIM), col(AIM), lre, ALU.mult)
            TT(col(CT), col(ARE), lim, ALU.mult)
            TT(col(FIM), col(FIM), col(CT), ALU.subtract)
            TT(col(FIM), col(FIM), col(INV), ALU.mult)
            fre, fim = (col(i).rearrange("p (s o) -> p s o", o=1).to_broadcast([P, ST, 16]) for i in (FRE, FIM))
            t0 = flat(act_out)[:, 0:256].rearrange("p (s c) -> p s c", c=16)
            TT(b_bar[0], b_nat[0], fre, ALU.mult)
            TT(t0, b_nat[1], fim, ALU.mult)
            TT(b_bar[0], b_bar[0], t0, ALU.subtract)
            TT(b_bar[1], b_nat[1], fre, ALU.mult)
            TT(t0, b_nat[0], fim, ALU.mult)
            TT(b_bar[1], b_bar[1], t0, ALU.add)
            for i in range(2):
                for g in range(2):
                    ins = dve.tensor_copy(b_diag[i][64 * g:64 * g + 64, :, 16 * g:16 * g + 16], b_bar[i][64 * g:64 * g + 64, :, :])
                    ins.then_inc(bt_in, 1)
            dve.wait_ge(bt_taken, 1)
            for i in range(2):
                link(dve.tensor_copy(b_t[i], bank[i][:, :].rearrange("p (i m) -> p i m", i=4)))
            for i, (src, sign) in enumerate(((2, 1.0), (2, -1.0), (3, -1.0))):
                for g in range(2):
                    o = c_t[i][64 * g:64 * g + 64, :, 16 * g:16 * g + 16]
                    s_ = bank[src][64 * g:64 * g + 64, :].rearrange("p (s c) -> p s c", c=32)[:, :, 16 * g:16 * g + 16]
                    ins = dve.tensor_scalar(o, s_, sign, None, ALU.mult)
                    if i == 2 and g == 1:
                        ins.then_inc(cd_in, 1)
                    else:
                        link(ins)

        def b1_pe_params(pe):
            pe.wait_ge(bt_in, 4)
            for i in range(2):
                for q in range(4):
                    pe.transpose(bank[i][:, q * P:(q + 1) * P], b_diag[i][:, 4 * q:4 * q + 4, :].rearrange("p s c -> p (s c)"), ident[:, :])
            for i in range(2):
                for q in range(4):
                    mm = pe.transpose(bank[2 + i][:, q * P:(q + 1) * P], c_nat[i][:, q, :, :].rearrange("p a s -> p (a s)"), ident[:, :])
            mm.then_inc(bt_taken, 1)
            pe.wait_ge(cd_in, 2)

        def dve_phase(dve, i):
            c, s = phase(i, 0), phase(i, 1)
            for j in range(4):
                ins = dve.tensor_scalar(s[:, j, :], steps_t[:, :], col(TURNS)[:, 4 * i + j:4 * i + j + 1], None, ALU.mult)
            chain(dve, dve_n, dve_chain, ins)
            chain(dve, dve_n, dve_chain, dve.tensor_scalar(c, s, ROUND, ROUND, ALU.add, ALU.subtract))
            dve.tensor_tensor(s, s, c, ALU.subtract).then_inc(ph_ready, 1)

        def act_phase(act, i):
            c, s = phase(i, 0), phase(i, 1)
            act.wait_ge(ph_ready, i + 1)
            chain(act, act_n, act_chain, act.activation(c, s, ACT.Abs))
            chain(act, act_n, act_chain, act.activation(s, s, ACT.Sin, scale=2 * PI))
            act.activation(c, c, ACT.Sin, scale=-2 * PI, bias=quarter[:, 0:1]).then_inc(ph_done, 1)

        def pe_bu(pe, s):
            i, j = s // 4, s % 4
            if s >= 2:
                pe.wait_ge(bu_free, s - 1)
            pe.wait_ge(lin_free[i // 2], 1)
            r = slice(32 * j, 32 * j + 32)
            pe.matmul(bank[s % 2][:, 0:T], b_t[0][r, i, :], us[r, i, :], start=True, stop=True)
            pe.matmul(bank[s % 2][:, T:2 * T], b_t[1][r, i, :], us[r, i, :], start=True, stop=True).then_inc(bu_done, 1)

        def pe_y(pe, s):
            i, j = s // 4, s % 4
            if j == 0 and i >= 1:
                pe.wait_ge(y_taken, i)
            pe.wait_ge(prod_done, s + 1)
            p = prod[s % 2]
            for n, (c, q) in enumerate(((0, 0), (1, 3), (2, 2), (2, 1))):
                mm = pe.matmul(bank[3][32 * j:32 * j + 32, 0:T], c_t[c][:, s, :], p[:, q, :], start=n == 0, stop=n == 3)
            mm.then_inc(y_done, 1)

        def dve_state(dve, s):
            i, j = s // 4, s % 4
            link = lambda ins: chain(dve, dve_n, dve_chain, ins)
            cos2 = phase(i, 0)[:, j:j + 1, :].to_broadcast([P, 2, T])
            sin2 = phase(i, 1)[:, j:j + 1, :].to_broadcast([P, 2, T])
            dve.wait_ge(bu_done, s + 1)
            if s >= 1:
                dve.wait_ge(prod_done, s)
            if j == 0:
                dve.wait_ge(ph_done, i + 1)
            dve.tensor_tensor(act_out[:, :, :], two(bank[s % 2]), cos2, ALU.mult)
            dve.tensor_tensor(hid[:, :, :], two(bank[s % 2]), sin2, ALU.mult).then_inc(bu_free, 1)
            dve.wait_ge(bu_free, s + 1)
            dve.tensor_tensor(stat[:, 0, :], act_out[:, 0, :], hid[:, 1, :], ALU.add)
            link(dve.tensor_tensor(stat[:, 1, :], act_out[:, 1, :], hid[:, 0, :], ALU.subtract))
            decay = col(DECAY)[:, s:s + 1].to_broadcast([P, T])
            dve.tensor_tensor_scan(act_out[:, 0, :], decay, stat[:, 0, :], 0.0, ALU.mult, ALU.add)
            link(dve.tensor_tensor_scan(act_out[:, 1, :], decay, stat[:, 1, :], 0.0, ALU.mult, ALU.add))
            if s >= 2:
                dve.wait_ge(y_done, s - 1)
            p = prod[s % 2]
            dve.tensor_tensor(p[:, 0:2, :], act_out[:, :, :], cos2, ALU.mult)
            dve.tensor_tensor(p[:, 2:4, :], act_out[:, :, :], sin2, ALU.mult).then_inc(prod_done, 1)

        def dve_y(dve, i):
            dve.wait_ge(y_done, 4 * i + 4)
            dve.scalar_tensor_tensor(out=us[:, i, :], in0=us[:, i, :], scalar=v1("D_skip")(i), in1=bank[3][:, 0:T],
                                     op0=ALU.mult, op1=ALU.add).then_inc(y_taken, 1)

        def head(h):
            r = slice(64 * (h % 2), 64 * (h % 2) + 64)
            return h // 2, r, (2, 7)[h % 2]

        def pe_z(pe, h):
            j, r, b = head(h)
            if h == 0:
                for b_ in range(2):
                    pe.wait_ge(lin_free[b_], 4)
            if h >= 2:
                pe.wait_ge(w_exp, h - 1)
            pe.matmul(bank[b][:, 0:T], kT[r, j, 0:P], qT[r, j, :], start=True, stop=True, skip_group_check=True)
            pe.matmul(bank[b][:, T:T + P], kT[r, j, P:T], qT[r, j, P:T], start=False, stop=True,
                      skip_group_check=True).then_inc(z_done, 1)

        def pe_tri(pe, h):
            j, r, b = head(h)
            pe.wait_ge(sp_masked, h + 1)
            pe.matmul(bank[b][:, 0:T], suffix[:, :], at_sp[:, 0:T], start=False, stop=True, skip_group_check=True)
            pe.matmul(bank[b][:, P:T], minus1[:, :], at_sp[:, T:T + P], start=False, stop=True, skip_group_check=True)
            pe.matmul(bank[b][:, T:T + P], suffix[:, :], at_sp[:, T:T + P], start=False, stop=True, skip_group_check=True)
            for c in (0, T):
                mm = pe.matmul(bank[b][:, c:c + P], identb[:, :], earlier[:, :], start=False, stop=True,
                               skip_group_check=True)
            mm.then_inc(tri_done, 1)

        def pe_av(pe, h):
            j, r, b = head(h)
            pe.wait_ge(w_exp, h + 1)
            if h % 2 == 0 and j >= 1:
                pe.wait_ge(o_taken, j)
            c = slice(h * HD, h * HD + HD)
            pe.matmul(bank[6][r, 0:T], v_tok[:, 0, c], at_w[:, 0:T], start=True, stop=True, skip_group_check=True)
            pe.matmul(bank[6][r, P:T], v_tok[:, 1, c], at_w[:, T:T + P], start=False, stop=True,
                      skip_group_check=True).then_inc(av_done, 1)

        def act_softplus(act, h):
            link = lambda ins: chain(act, act_n, act_chain, ins)
            b = head(h)[2]
            act.wait_ge(z_done, h + 1)
            if h >= 1:
                act.wait_ge(sp_done, h)
            link(act.activation(at_abs, bank[b][:, 0:ATT], ACT.Abs))
            act.activation(at_pos, bank[b][:, 0:ATT], ACT.Relu).then_inc(z_read, 1)
            link(act.activation(at_abs, at_abs, ACT.Exp, scale=-1.0))
            act.activation(at_abs, at_abs, ACT.Ln, bias=1.0).then_inc(ln_done, 1)

        def act_weights(act, h):
            act.wait_ge(tri_done, h + 1)
            if h >= 1:
                act.wait_ge(av_done, h)
            act.activation(at_w, bank[head(h)[2]][:, 0:ATT], ACT.Exp).then_inc(w_exp, 1)

        def act_o(act, j):
            act.wait_ge(av_done, 2 * j + 2)
            act.copy(bh[:, KS + j, :], bank[6][:, 0:T]).then_inc(o_half, 1)

        def dve_o(dve, j):
            dve.wait_ge(o_half, j + 1)
            dve.tensor_tensor(bl[:, KS + j, :], bank[6][:, 0:T], bh[:, KS + j, :].bitcast(F32), ALU.subtract).then_inc(o_taken, 1)

        def b1_pe(pe):
            idx, ln, tb = norms["mix1"]
            b1_pe_start(pe)
            norm_pe(pe, idx, ln, tb, KD, tile_res)
            for g in range(NSTEP):
                n = N_IN1 + g
                if g >= 8:
                    pe_z(pe, g - 8)
                if g >= 2:
                    pe.wait_ge(lin_free[g % 2], g // 2)
                b = 4 + g % 2
                if g in (6, 7):
                    pe_slab(pe, n)
                    lin_tokens(pe, n, b, 0, WCOLS, WCOLS).then_inc(used[slabs[n][2]], 1)
                else:
                    ready = (lambda k: pe.wait_ge(norm_out, tb + k + 1)) if g == 0 else None
                    lin_pe(pe, n, b, ready)
                if g == 1:
                    b1_pe_params(pe)
                if g >= 8:
                    pe_tri(pe, g - 8)
                for s in tiles_at.get(g - 1, []):
                    pe_y(pe, s)
                for s in tiles_at.get(g + 1, []):
                    pe_bu(pe, s)
                if g >= 9:
                    pe_av(pe, g - 9)
            for s in tiles_at[NSTEP - 1]:
                pe_y(pe, s)
            pe_av(pe, HEADS - 1)
            pe.wait_ge(gelu_l, 1)
            lin_pe(pe, N_GLU, 0, None, KS, DS, 4, lambda k: bh[:, k, :], lambda k: bl[:, k, :])
            pe_up(pe, N_UP1, 0, lambda: pe.wait_ge(o_taken, 4), lambda: pe.wait_ge(glu_l, 1), 1)
            idx, ln, tb = norms["mlp1"]
            pe_out(pe, N_OUT1, 0, tb)
            norm_pe(pe, idx, ln, tb, KD, tile_res)
            ffn_pe(pe, "ff", N_FFN1, 16, False, 0, tb)
            idx, ln, tb = norms["final1"]
            norm_pe(pe, idx, ln, tb, KD, tile_res)

        def pe_up(pe, n0, r, ready_b, ready_a, extra=0, order="BA"):
            for q in range(4):
                p, which = q // 2, order[q % 2]
                off = KS if which == "B" else 0
                (ready_b if which == "B" else ready_a)()
                if q == 0 and extra:
                    pe.wait_ge(glu_sig, 1)
                if q >= 2:
                    pe.wait_ge(pair_read, 4 * r + q - 1)
                lin_pe(pe, n0 + q, 2 * (q % 2), None, KS, 512, 4,
                       lambda k, off=off: bh[:, off + k, :], lambda k, off=off: bl[:, off + k, :])

        def pe_out(pe, n0, r, tb):
            for q in range(4):
                def ready(k):
                    if k % 4 == 0:
                        pe.wait_ge(merged_l, 2 * r + k // 4 + 1)
                if q >= 2:
                    pe.wait_ge(norm_in, tb + 2 * (q - 1))
                lin_pe(pe, n0 + q, 4 + q % 2, ready if q == 0 else None)

        def act_up(act, n0, r, q):
            p = q // 2
            if q % 2:
                act.wait_ge(merged_sum, 2 * r + p + 1)
                act.copy(uh[:, 4 * p:4 * p + 4, :], merged[:, 4 * p:4 * p + 4, :]).then_inc(merged_h, 1)

        def dve_up(dve, n0, r, q, order="BA"):
            link = lambda ins: chain(dve, dve_n, dve_chain, ins)
            p, which = q // 2, order[q % 2]
            wait_used(dve, n0 + q)
            g0 = (KD if which == "B" else 0) + 4 * p
            o = merged[:, 4 * p:4 * p + 4, :] if q % 2 == 0 else gated
            for f in range(2):
                ins = dve.scalar_tensor_tensor(out=o[:, 2 * f:2 * f + 2, :], in0=gates[:, g0 + 2 * f:g0 + 2 * f + 2, :], scalar=1.0,
                                               in1=two(bank[2 * (q % 2) + f]), op0=ALU.add, op1=ALU.mult)
            ins.then_inc(pair_read, 1)
            if q % 2:
                dve.wait_ge(pair_read, 4 * r + q + 1)
                m = merged[:, 4 * p:4 * p + 4, :]
                dve.tensor_tensor(m, m, gated, ALU.add).then_inc(merged_sum, 1)
                dve.wait_ge(merged_h, 2 * r + p + 1)
                dve.tensor_tensor(ul[:, 4 * p:4 * p + 4, :], m, uh[:, 4 * p:4 * p + 4, :].bitcast(F32), ALU.subtract).then_inc(merged_l, 1)

        def dve_out(dve, n0, q, o):
            wait_used(dve, n0 + q)
            dve.scalar_tensor_tensor(out=o[:, 2 * q:2 * q + 2, :], in0=two(bank[4 + q % 2]), scalar=0.5, in1=res[:, 2 * q:2 * q + 2, :],
                                     op0=ALU.mult, op1=ALU.add).then_inc(norm_in, 2)

        def b1_act(act):
            link = lambda ins: chain(act, act_n, act_chain, ins)
            start_act_dmas(act)
            act_round(act, 0)
            act_round(act, 1)
            act.wait_ge(cd_in, 1)
            act.wait_ge(prep_dve, 2)
            act.activation(col(DT), col(CT), ACT.Exp).then_inc(prep_act, 1)
            idx, ln, tb = norms["mix1"]
            norm_act(act, idx, ln, tb, KD, tile_res, 1.0, 1, tile_tmp, None, tile_u)
            act.wait_ge(prep_dve, 3)
            act.activation(col(DECAY), col(ADT), ACT.Exp)
            link(act.activation(col(AFRAC), col(FRAC), ACT.Abs))
            act.activation(col(SIN1), col(FRAC), ACT.Sin, scale=2 * PI)
            act.activation(col(COS1), col(AFRAC), ACT.Sin, scale=-2 * PI, bias=quarter[:, 0:1]).then_inc(prep_act, 1)
            for i in range(2):
                act_phase(act, i)
            for g in range(NSTEP):
                n = N_IN1 + g
                if g >= 8:
                    act_softplus(act, g - 8)
                act_round(act, n + 2)
                for s in tiles_at.get(g, []):
                    if s in (4, 8):
                        act_phase(act, s // 4 + 1)
                wait_used(act, n)
                b = bank[4 + g % 2]
                if g < 2:
                    act.copy(us[:, 2 * g:2 * g + 2, :], two(b)).then_inc(lin_free[g % 2], 1)
                elif g < 8:
                    o = (qT[:, 2 * (g - 2):2 * (g - 2) + 2, :] if g < 4 else kT[:, 2 * (g - 4):2 * (g - 4) + 2, :] if g < 6
                         else v_tok[:, :, (g - 6) * WCOLS:(g - 5) * WCOLS])
                    act.activation(o, two(b), ACT.Copy, scale=SCALE_N if g < 4 else 1.0).then_inc(lin_free[g % 2], 1)
                else:
                    for f in range(2):
                        k = 2 * (g - 8) + f
                        ins = act.activation(gates[:, k, :], b[:, f * T:(f + 1) * T], ACT.Tanh, scale=0.5, bias=half_b[:, k:k + 1])
                    ins.then_inc(lin_free[g % 2], 1)
                if g >= 8:
                    act_weights(act, g - 8)
                if g >= 9 and g % 2 == 0:
                    act_o(act, (g - 10) // 2)
            act_o(act, 3)
            act.wait_ge(y_taken, 4)
            link(act.activation(us[:, :, :], us[:, :, :], ACT.Gelu_apprx_tanh))
            act.copy(bh[:, 0:KS, :], us[:, :, :]).then_inc(gelu_h, 1)
            act_round(act, N_GLU + 2)
            wait_used(act, N_GLU)
            for f in range(KS):
                ins = act.activation(gated[:, f, :], bank[f // 2][:, (f % 2) * T:(f % 2 + 1) * T], ACT.Sigmoid,
                                     bias=v1("b_glu")(f))
            ins.then_inc(glu_sig, 1)
            act.wait_ge(glu_y, 1)
            act.copy(bh[:, 0:KS, :], us[:, :, :]).then_inc(glu_h, 1)
            for q in range(4):
                act_up(act, N_UP1, 0, q)
                act_round(act, N_UP1 + q + 2)
            for q in range(4):
                act_round(act, N_OUT1 + q + 2)
            idx, ln, tb = norms["mlp1"]
            norm_act(act, idx, ln, tb, KD, tile_res, 1.0, 1, tile_tmp, None, tile_u)
            ffn_act_engine(act, N_FFN1, 16, False, 0)
            idx, ln, tb = norms["final1"]
            norm_act(act, idx, ln, tb, KD, tile_res, 1.0, 1, tile_tmp, None, tile_u)

        def b1_dve(dve):
            link = lambda ins: chain(dve, dve_n, dve_chain, ins)
            b1_dve_start(dve)
            dve_split(dve, 0)
            dve_split(dve, 1)
            idx, ln, tb = norms["mix1"]
            norm_dve(dve, idx, ln, tb, KD, tile_res, v1("norm_mix"), tile_tmp, None, tile_u, tile_l)
            b1_dve_params(dve)
            for g in range(NSTEP):
                n = N_IN1 + g
                if g >= 8:
                    h = g - 8
                    dve.wait_ge(ln_done, h + 1)
                    if h >= 1:
                        dve.wait_ge(tri_done, h)
                    dve.tensor_tensor(at_sp, at_pos, at_abs, ALU.add).then_inc(sp_done, 1)
                if tiles_at.get(g - 1, [0])[-1] % 4 == 3:
                    dve_y(dve, tiles_at[g - 1][-1] // 4)
                dve_split(dve, n + 2)
                for s in tiles_at.get(g, []):
                    if s in (4, 8):
                        dve_phase(dve, s // 4 + 1)
                    dve_state(dve, s)
                if g >= 9 and g % 2 == 0:
                    dve_o(dve, (g - 10) // 2)
            dve_y(dve, 3)
            dve_o(dve, 3)
            dve.wait_ge(gelu_h, 1)
            dve.tensor_tensor(bl[:, 0:KS, :], us[:, :, :], bh[:, 0:KS, :].bitcast(F32), ALU.subtract).then_inc(gelu_l, 1)
            dve_split(dve, N_GLU + 2)
            dve.wait_ge(glu_sig, 1)
            dve.tensor_tensor(us[:, :, :], us[:, :, :], gated, ALU.mult).then_inc(glu_y, 1)
            dve.wait_ge(glu_h, 1)
            dve.tensor_tensor(bl[:, 0:KS, :], us[:, :, :], bh[:, 0:KS, :].bitcast(F32), ALU.subtract).then_inc(glu_l, 1)
            for b in range(2):
                dve.wait_ge(lin_free[b], 8)
            for q in range(4):
                dve_up(dve, N_UP1, 0, q)
                dve_split(dve, N_UP1 + q + 2)
            for q in range(4):
                dve_out(dve, N_OUT1, q, res)
                dve_split(dve, N_OUT1 + q + 2)
            idx, ln, tb = norms["mlp1"]
            norm_dve(dve, idx, ln, tb, KD, tile_res, v1("norm_mlp"), tile_tmp, None, tile_u, tile_l)
            ffn_dve_engine(dve, N_FFN1, 16, False, 0)
            wait_used(dve, N_FFN1 + 31)
            for b in range(4):
                dve.tensor_tensor(res[:, 2 * b:2 * b + 2, :], two(bank[b]), res[:, 2 * b:2 * b + 2, :], ALU.add).then_inc(norm_in, 2)
            idx, ln, tb = norms["final1"]
            norm_dve(dve, idx, ln, tb, KD, tile_res, v1("norm_final"), tile_tmp, None, tile_u, tile_l, ALPHA)

        cos_n, sin_n, cos_m, sin_m = (tables[:, i * T:(i + 1) * T] for i in range(4))
        perm_n, perm_m = tables[:, 4 * T:4 * T + P], tables[:, 4 * T + P:4 * T + 2 * P]
        q_n = shared[:, 0:1024].rearrange("p (h t) -> p h t", h=HPG)
        kc, vc, ks, kw = (shared[:, 1024 + i * T:1024 + (i + 1) * T] for i in range(4))
        ksw = shared[:, 1024 + 2 * T:1024 + 4 * T].rearrange("p (a t) -> p a t", a=2)
        vsw = shared[:, 2048:2560].rearrange("p (w a d) -> p a w d", w=2, a=NTT)
        vs, vw = (shared[:, 2048 + i * T:2048 + (i + 1) * T].rearrange("p (a d) -> p a d", a=NTT) for i in range(2))
        vm = shared[:, 2560:3584].rearrange("p (a d) -> p a d", a=NTT)
        qm, km = sq, tmp
        cq = small[:, 0:512].rearrange("p (k t) -> p k t", k=2)
        ckv, kpe = small[:, 512:768], small[0:ROPE_M, 768:1024]
        kper = small[0:ROPE_M, 1024:1280]
        gn_f = small[32:56, 768:1024]
        gn = small[:, 1280:1328].rearrange("p (a h c) -> p a h c", a=NTT, c=3)
        rope_raw = [small[:, 1344 + 512 * i:1856 + 512 * i].rearrange("p (a t) -> p a t", a=2) for i in range(2)]
        rope_tmp = small[:, 2368:2880].rearrange("p (a t) -> p a t", a=2)
        c_scores = small[:, 0:240]
        c_sums = small[:, 240:288].rearrange("p (c n) -> p c n", c=3)
        vcc = small[0:N_CMP, 320:448]
        chid = [small[:, 448 + 32 * i:448 + 32 * i + 2 * N_CMP] for i in range(2)]
        ctok = [small[0:2 * N_CMP, 512 + P * i:512 + P * (i + 1)] for i in range(2)]
        probs = [flat(hid)[:, 0:ATT], flat(act_out)[:, 0:ATT]]
        probs_t = [flat(stat)[:, 0:ATT], small[:, 768:768 + ATT]]
        p_cmp_t = small[0:N_CMP, 1344:3392]
        x_f = [flat(act_out)[:, 0:480], flat(hid)[:, 0:480]]
        x_halves = [[flat(t_)[:, 512 * i:512 * i + 480] for t_ in (bh, bl)] for i in range(2)]
        (rope_in, perm_done, rope_done, m_read, m_perm, m_roped, km_k, km_pe, kpe_perm, x_blocks, x_l, chid_in, w2_done, ctok_in, ctok_t, w2_read, cs_done, cs_shift, cs_exp, cs_ready, ct_done, ct_taken, a_done, max_done, exp_done, p_ready, t_done, t_taken, o_done, o2_half, o2_taken, bank7_free, tok_done, final_t, final_copied, out_done) = mk(
            "rope_in", "perm_done", "rope_done", "m_read", "m_perm", "m_roped", "km_k", "km_pe", "kpe_perm", "x_blocks", "x_l", "chid_in", "w2_done", "ctok_in", "ctok_t", "w2_read", "cs_done", "cs_shift", "cs_exp", "cs_ready", "ct_done", "ct_taken", "a_done", "max_done", "exp_done", "p_ready", "t_done", "t_taken", "o_done", "o2_half", "o2_taken", "bank7_free", "tok_done", "final_t", "final_copied", "out_done")
        lin2 = [sem("in_read0"), sem("in_read1")]
        NROPE = 4
        RAW_AT = (1, 2, 2, 3)
        B7 = NROPE + 3
        NU = HEADS + 2 * HEADS
        EARLY = 2
        NQ = 4 * (8 - EARLY)
        C0 = 4

        def unit(m):
            if m < HEADS:
                return (lambda c: qm[0:QK_M, m, c], lambda c: km[0:QK_M, m, c],
                        lambda tt: vm[:, tt, m * HD:(m + 1) * HD], m, None)
            h, w = (m - HEADS) // 2, (m - HEADS) % 2
            g, hp = h // HPG, h % HPG
            r = slice(g * HD, (g + 1) * HD)
            k_, v_ = ((ks, vs), (kw, vw))[w]
            return (lambda c: q_n[r, hp, c], lambda c: k_[r, c], lambda tt: v_[:, tt, r], h, 1 + w)

        def unit_cols(tt):
            return slice(0, P) if tt == 0 else slice(P, 3 * P)

        def b2_ffn_sp(sp, l, tag):
            n0 = where[(tag, l)]
            sp_slab(sp, n0)
            sp_slab(sp, n0 + 1)
            with sp.Fori(1, 11, 1) as i:
                sp_slab(sp, n0 + 2, (l, i), i - 1)
                sp_slab(sp, n0 + 3, (l, i - 1), i - 1)
                sp_slab(sp, n0 + 4, (l, i), i - 1)
            sp_slab(sp, n0 + 32)

        def b2_sp(sp, l):
            if l == 0:
                sp.wait_ge(y_done, ST)
                sp.dma_start(tables[:, 0:4 * T + 2 * P], a["shape_tables"][:, 0:4 * T + 2 * P]).then_inc(rope_in, 16)
            b2_ffn_sp(sp, l, "fa")
            for n in range(where[("in2", l)], where[("fb", l)]):
                sp_slab(sp, n)
            b2_ffn_sp(sp, l, "fb")

        def pe_perm(pe, l, r):
            n = NROPE * l + r
            pe.wait_ge(lin2[r % 2], 8 * l + RAW_AT[r])
            pe.wait_ge(bank7_free, B7 * l + r + 1)
            if n == 0:
                pe.wait_ge(rope_in, 16)
            w = T if r == 2 else 2 * T
            raw_ = rope_raw[r % 2]
            pe.matmul(bank[7][:, 0:w], perm_n, raw_[:, 0:w // T, :], start=True, stop=True).then_inc(perm_done, 1)

        def pe_scores(pe, l, m):
            q_, k_, _, h, _w = unit(m)
            n = NU * l + m
            b = bank[m % 2]
            if m >= 2:
                pe.wait_ge(exp_done, n - 1)
            for tt in range(NTT):
                c = unit_cols(tt)
                pe.matmul(b[:, c], q_(slice(tt * P, (tt + 1) * P)), k_(slice(0, (tt + 1) * P)), start=tt == 0, stop=True,
                          skip_group_check=True)
            for c in (0, 2 * P):
                mm = pe.matmul(b[:, c:c + P], identb[:, :], causal[:, :], start=False, stop=True, skip_group_check=True)
            mm.then_inc(a_done, 1)

        def pe_turn(pe, l, m):
            n = NU * l + m
            pe.wait_ge(p_ready, n + 1)
            if m >= 2:
                pe.wait_ge(t_taken, n - 1)
            b = bank[2 + m % 2]
            for q in range(3):
                mm = pe.transpose(b[:, q * P:(q + 1) * P], probs[m % 2][:, q * P:(q + 1) * P], ident[:, :])
            mm.then_inc(t_done, 1)

        def pe_values(pe, l, m):
            _, _, v_, h, w = unit(m)
            n = NU * l + m
            r = slice(64 * (h % 2), 64 * (h % 2) + 64)
            first = w is None or w == 1
            pair = h // 2 + (0 if w is None else 4)
            if first and h % 2 == 0 and pair > 0:
                pe.wait_ge(o2_taken, 8 * l + pair)
            pe.wait_ge(t_taken, n + 1)
            pt = probs_t[m % 2]
            pe.matmul(bank[6][r, 0:T], v_(0), pt[:, 0:T], start=first, stop=True, skip_group_check=True)
            mm = pe.matmul(bank[6][r, P:T], v_(1), pt[:, T:3 * P], start=False, stop=True, skip_group_check=True)
            if w == 2:
                if h == 0:
                    pe.wait_ge(ct_taken, 4 * l + 4)
                g = h // HPG
                mm = pe.matmul(bank[6][r, 0:T], vcc[:, g * HD:(g + 1) * HD], p_cmp_t[:, h * T:(h + 1) * T], start=False, stop=True,
                               skip_group_check=True)
            mm.then_inc(o_done, 1)

        def b2_pe(pe, l):
            idx, ln, tb = norms["final1"] if l == 0 else norms[("fb", l - 1)]
            ffn_pe(pe, "fa", where[("fa", l)], 11, True, 16 + 22 * l, tb)
            idx, ln, tb = norms[("fa", l)]
            norm_pe(pe, idx, ln, tb, KD, tile_tmp)
            n0 = where[("in2", l)]
            for i in range(7):
                n = n0 + i
                b = 4 + i % 2
                if i == 2:
                    pe.wait_ge(norm_in, norms[("q", l)][2] + 2)
                elif i >= 3:
                    pe.wait_ge(lin2[i % 2], 8 * l + (i - 1) // 2)
                ready = (lambda k: pe.wait_ge(norm_out, tb + k + 1)) if i == 0 else None
                slot = slabs[n][2]
                if i in (0, 2, 3, 4, 5):
                    lin_pe(pe, n, b, ready)
                elif i == 1:
                    pe_slab(pe, n)
                    c = KV_RANK + ROPE_M + 3 * HEADS
                    for k in range(KD):
                        mm3(pe, bank[b][:, 0:T], slab_view(wh, slot, KD, c)[:, k, 0:P], slab_view(wl, slot, KD, c)[:, k, 0:P],
                            uh[:, k, :], ul[:, k, :], k == 0, k == KD - 1)
                    for k in range(KD):
                        mm = mm3(pe, bank[b][0:56, T:2 * T], slab_view(wh, slot, KD, c)[:, k, P:c],
                                 slab_view(wl, slot, KD, c)[:, k, P:c], uh[:, k, :], ul[:, k, :], k == 0, k == KD - 1)
                    mm.then_inc(used[slot], 1)
                else:
                    pe_slab(pe, n)
                    lin_tokens(pe, n, b, 0, WCOLS, WCOLS).then_inc(used[slot], 1)
                if i == 1:
                    qi, _, qt = norms[("q", l)]
                    norm_pe(pe, qi, None, qt, 2, lambda k: cq[:, k, :])
                if i == 2:
                    vi, _, vt = norms[("kv", l)]
                    norm_pe(pe, vi, None, vt, 1, lambda k: ckv)
                if i == 2:
                    pe.wait_ge(gn_in, l + 1)
                    for tt in range(NTT):
                        mm = pe.transpose(bank[7][:, tt * 24:(tt + 1) * 24], gn_f[:, tt * P:(tt + 1) * P], ident[32:56, 32:56])
                    mm.then_inc(gn_t, 1)
                if 3 <= i:
                    pe_perm(pe, l, i - 3)
            n = where[("uq", l)]
            slot = pe_slab(pe, n)
            for k in range(2):
                pe.wait_ge(norm_out, qt + k + 1)
            for h in range(HEADS):
                for k in range(2):
                    mm = mm3(pe, bank[h // 2][0:QK_M, (h % 2) * T:(h % 2 + 1) * T],
                             slab_view(wh, slot, 2, HEADS * QK_M)[:, k, h * QK_M:(h + 1) * QK_M],
                             slab_view(wl, slot, 2, HEADS * QK_M)[:, k, h * QK_M:(h + 1) * QK_M],
                             hh[:, k, :], hl[:, k, :], k == 0, k == 1)
            mm.then_inc(used[slot], 1)
            pe.wait_ge(norm_out, vt + 1)

            def cmp_hidden(i):
                n = where[("cmp", l)] + i
                slot = pe_slab(pe, n)
                pe.wait_ge(x_l, 2 * l + i + 1)
                xh, xl = (t_.rearrange("p (s c) -> p s c", s=16) for t_ in x_halves[i])
                for k in range(16):
                    mm = mm3(pe, bank[6 + i][0:2 * N_CMP, 0:P], slab_view(wh, slot, 16, P)[:, k, :], slab_view(wl, slot, 16, P)[:, k, :],
                             xh[:, k, :], xl[:, k, :], k == 0, k == 15, swap=True)
                mm.then_inc(used[slot], 1)

            def cmp_turn(i):
                pe.wait_ge(ctok_in, 2 * l + i + 1)
                pe.transpose(bank[6 + i][:, T:T + 2 * N_CMP], ctok[i], ident[0:2 * N_CMP, 0:2 * N_CMP]).then_inc(ctok_t, 1)

            cmp_hidden(0)
            for b in range(4):
                pe.wait_ge(m_read, 4 * l + b + 1)
                pe.matmul(bank[b][HD:QK_M, :], perm_m[HD:QK_M, HD:QK_M], qm[HD:QK_M, 2 * b:2 * b + 2, :], start=True,
                          stop=True).then_inc(m_perm, 1)
            pe.wait_ge(bank7_free, B7 * l + NROPE + 1)
            cmp_hidden(1)
            cmp_turn(0)
            n = where[("ukv", l)]
            slot = pe_slab(pe, n)
            wk = lambda w_: slab_view(w_, slot, 1, 2 * HEADS * HD)[:, 0, :].rearrange("p (h c) -> p h c", h=HEADS)
            for tt in range(NTT):
                pe.wait_ge(lin2[tt], 8 * l + 3)
                c = slice(tt * P, (tt + 1) * P)
                mm = mm3(pe, bank[4 + tt][:, :], ckh[:, c], ckl[:, c], wk(wh)[:, :, HD:], wk(wl)[:, :, HD:], True, True)
            mm.then_inc(tok_done, 1)
            cmp_turn(1)
            for h in range(HEADS):
                if h % 2 == 0:
                    pe.wait_ge(m_roped, 4 * l + h // 2 + 1)
                mm = mm3(pe, bank[h // 2][0:HD, (h % 2) * T:(h % 2 + 1) * T], wk(wh)[:, h, 0:HD], wk(wl)[:, h, 0:HD], ckh[:, :], ckl[:, :],
                         True, True)
            mm.then_inc(used[slot], 1)
            pe.wait_ge(lin2[0], 8 * l + 4)
            lin_pe(pe, where[("gate2", l)], 4)
            pe.wait_ge(chid_in, 2 * l + 2)
            pe.matmul(bank[7][0:ROPE_M, 0:T], perm_m[0:ROPE_M, 0:ROPE_M], kpe, start=True, stop=True).then_inc(kpe_perm, 1)
            pe.matmul(bank[6][:, 0:2 * N_CMP], cmp_w2[:, l, 0, :, :].rearrange("p a d -> p (a d)"), chid[0],
                      start=True, stop=True).then_inc(w2_done, 1)
            pe.wait_ge(lin2[1], 8 * l + 4)
            for g in range(KVH):
                mm = pe.matmul(bank[5][0:N_CMP, g * HD:(g + 1) * HD], chid[1][:, g * N_CMP:(g + 1) * N_CMP], cmp_w2[:, l, 1, 0, :],
                               start=True, stop=True)
            mm.then_inc(w2_done, 1)
            pe.wait_ge(w2_read, 2 * l + 2)
            lin_pe(pe, where[("gate2", l)] + 1, 5)
            pe.wait_ge(bank7_free, B7 * l + NROPE + 2)
            pe.wait_ge(rope_done, NROPE * l + NROPE)
            o7 = bank[7][:, 0:NTT * HEADS * N_CMP].rearrange("p (a g h c) -> p a h g c", a=NTT, g=KVH, h=HPG)
            for tt in range(NTT):
                for hp in range(HPG):
                    mm = pe.matmul(o7[:, tt, hp], q_n[:, hp, tt * P:(tt + 1) * P], kcc[:, :].rearrange("p (g c) -> p g c", g=KVH),
                                   start=tt + hp == 0, stop=True, skip_group_check=True)
            mm.then_inc(cs_done, 1)
            pe.wait_ge(km_k, 4 * l + 4)
            pe.wait_ge(km_pe, l + 1)
            for s in range(NU + 2):
                if s < NU:
                    pe_scores(pe, l, s)
                if s < NQ:
                    i, j = divmod(s, 4)
                    i += EARLY
                    n = where[("gate2", l)] + i
                    if j == 0:
                        pe.wait_ge(lin2[i % 2], 8 * l + 4 + i // 2)
                        pe_slab(pe, n)
                    lin_quarter(pe, n, 4 + i % 2, j)
                if 1 <= s <= NU:
                    pe_turn(pe, l, s - 1)
                if C0 <= s < C0 + 4:
                    q = s - C0
                    if q == 0:
                        pe.wait_ge(cs_ready, l + 1)
                        pe.wait_ge(bank7_free, B7 * l + B7)
                    else:
                        pe.wait_ge(ct_taken, 4 * l + q)
                    for h in (2 * q, 2 * q + 1):
                        for tt in range(NTT):
                            mm = pe.transpose(bank[7][0:N_CMP, (h % 2) * T + tt * P:(h % 2) * T + (tt + 1) * P],
                                              c_scores[:, (tt * HEADS + h) * N_CMP:(tt * HEADS + h + 1) * N_CMP], ident[:, :])
                    mm.then_inc(ct_done, 1)
                if s >= 2:
                    pe_values(pe, l, s - 2)
            pe_up(pe, where[("proj", l)], l + 1, lambda: pe.wait_ge(o2_taken, 8 * l + 4), lambda: pe.wait_ge(o2_taken, 8 * l + 8), 0, "AB")
            idx, ln, tb = norms[("mix", l)]
            pe_out(pe, where[("out2", l)], l + 1, tb)
            norm_pe(pe, idx, ln, tb, KD, tile_tmp)
            ffn_pe(pe, "fb", where[("fb", l)], 11, True, 16 + 22 * l + 11, tb)
            idx, ln, tb = norms[("fb", l)]
            norm_pe(pe, idx, ln, tb, KD, tile_tmp)

        def pe_output(pe):
            for tt in range(NTT):
                for k in range(KD):
                    if tt == 0:
                        pe.wait_ge(norm_h, norms[("fb", LAYERS - 1)][2] + k + 1)
                    mm = pe.transpose(bank[2 * tt + k // 4][:, (k % 4) * P:(k % 4 + 1) * P], sq[:, k, tt * P:(tt + 1) * P], ident[:, :])
                    if k % 4 == 3:
                        mm.then_inc(final_t, 1)

        def act_exp(act, l, m):
            n = NU * l + m
            act.wait_ge(max_done, n + 1)
            if m >= 2:
                act.wait_ge(t_done, n - 1)
            for tt in range(NTT):
                c = unit_cols(tt)
                mm = act.activation(probs[m % 2][:, c], bank[m % 2][:, c], ACT.Exp, bias=cols1[:, m % 2, tt:tt + 1],
                                    accum_out=cols1[:, m % 2, 2 + tt:3 + tt])
            mm.then_inc(exp_done, 1)

        def act_turned(act, l, m):
            n = NU * l + m
            act.wait_ge(t_done, n + 1)
            if m >= 2:
                act.wait_ge(o_done, n - 1)
            act.copy(probs_t[m % 2], bank[2 + m % 2][:, 0:ATT]).then_inc(t_taken, 1)

        def last_of_pair(m):
            if m < HEADS:
                return m // 2 if m % 2 else None
            return 4 + (m - HEADS) // 4 if (m - HEADS) % 4 == 3 else None

        def act_blocks(act, l, i):
            if i == 0:
                act.wait_ge(rope_done, NROPE * l + 3)
            src = (kc, vc)[i].rearrange("p (c s q) -> p q s c", s=8, q=2)
            o = x_f[i].rearrange("p (s g c) -> p s g c", s=16, g=KVH)
            for par in range(2):
                for g in range(KVH):
                    for half in range(2):
                        ins = act.copy(o[64 * par:64 * par + 64, 8 * half:8 * half + 8, g, :],
                                       src[64 * g:64 * g + 64, par, :, half:half + N_CMP])
            ins.then_inc(x_blocks, 1)

        def act_gates(act, l, i):
            wait_used(act, where[("gate2", l)] + i)
            act.activation(gates[:, 2 * i:2 * i + 2, :], two(bank[4 + i % 2]), ACT.Tanh, scale=0.5).then_inc(lin2[i % 2], 1)

        def b2_act(act, l):
            link = lambda ins: chain(act, act_n, act_chain, ins)
            ffn_act_engine(act, where[("fa", l)], 11, True, 16 + 22 * l)
            idx, ln, tb = norms[("fa", l)]
            norm_act(act, idx, ln, tb, KD, tile_tmp, 1.0, 2, tile_tmp, v2(l, "ln_f1_b"), tile_u)
            n0 = where[("in2", l)]
            for i in range(7):
                n = n0 + i
                act_round(act, n + 2)
                wait_used(act, n)
                b = bank[4 + i % 2]
                r = i - 2
                if 2 <= r < NROPE:
                    act.wait_ge(rope_done, NROPE * l + r - 1)
                elif r >= 0 and l > 0:
                    act.wait_ge(rope_done, NROPE * l)
                if i == 0:
                    act.copy(cq, two(b)).then_inc(norm_in, 2)
                elif i == 1:
                    act.copy(ckv, b[:, 0:T]).then_inc(norm_in, 1)
                    act.activation(gn_f, b[32:56, T:2 * T], ACT.Tanh, scale=0.5).then_inc(gn_in, 1)
                    act.copy(kpe, b[0:ROPE_M, T:2 * T]).then_inc(lin2[1], 1)
                    idx, ln, tb = norms[("q", l)]
                    norm_act(act, idx, ln, tb, 2, lambda k: cq[:, k, :], float(D // Q_RANK), 1, lambda k: cq[:, k, :], None,
                             lambda k: hh[:, k, :])
                elif i in (2, 3):
                    act.activation(rope_raw[r % 2], two(b), ACT.Copy, scale=SCALE_N).then_inc(lin2[i % 2], 1)
                    if i == 2:
                        idx, ln, tb = norms[("kv", l)]
                        norm_act(act, idx, ln, tb, 1, lambda k: ckv, float(D // KV_RANK), 1, lambda k: ckv, None, lambda k: ckh[:, :])
                elif i == 4:
                    act.copy(rope_raw[r % 2][:, 0, :], b[:, 0:T])
                    act.copy(vc, b[:, T:2 * T]).then_inc(lin2[0], 1)
                elif i == 5:
                    act.copy(rope_raw[r % 2], two(b)).then_inc(lin2[1], 1)
                    act_blocks(act, l, 0)
                else:
                    act.copy(vsw, b[:, :].rearrange("p (a w d) -> p a w d", a=NTT, w=2)).then_inc(lin2[0], 1)
                    act_blocks(act, l, 1)
            n = where[("uq", l)]
            act_round(act, n + 2)
            wait_used(act, n)
            for b in range(4):
                act.activation(qm[0:QK_M, 2 * b:2 * b + 2, :], two(bank[b])[0:QK_M], ACT.Copy, scale=SCALE_M).then_inc(m_read, 1)
            for i in range(2):
                n = where[("cmp", l)] + i
                act_round(act, n + 2)
                wait_used(act, n)
                act.copy(ctok[i], bank[6 + i][0:2 * N_CMP, 0:P]).then_inc(ctok_in, 1)
            act_round(act, where[("ukv", l)] + 2)
            act.wait_ge(tok_done, l + 1)
            for tt in range(NTT):
                act.copy(vm[:, tt, :], bank[4 + tt][:, :]).then_inc(lin2[tt], 1)
            for i in range(2):
                act.wait_ge(ctok_t, 2 * l + i + 1)
                act.activation(chid[i], bank[6 + i][:, T:T + 2 * N_CMP], ACT.Gelu_apprx_tanh,
                               bias=v2(l, ("cmp_k_b1", "cmp_v_b1")[i])(0)).then_inc(chid_in, 1)
            wait_used(act, where[("ukv", l)])
            for b in range(4):
                act.copy(km[0:HD, 2 * b:2 * b + 2, :], two(bank[b])[0:HD]).then_inc(km_k, 1)
            for i in range(EARLY):
                act_round(act, where[("gate2", l)] + i + 2)
                act_gates(act, l, i)
            act.wait_ge(cs_shift, l + 1)
            act.activation(c_scores, c_scores, ACT.Exp).then_inc(cs_exp, 1)
            for s in range(NU + 2):
                if s < NU:
                    act_exp(act, l, s)
                if s < NQ and s % 4 < 2:
                    act_round_half(act, where[("gate2", l)] + EARLY + s // 4 + 2, s % 4)
                if 1 <= s <= NU:
                    act_turned(act, l, s - 1)
                if 4 <= s <= NQ and s % 4 == 0:
                    act_gates(act, l, EARLY + s // 4 - 1)
                pair = last_of_pair(s - 2) if s >= 2 else None
                if pair is not None:
                    act.wait_ge(o_done, NU * l + s - 1)
                    act.copy(bh[:, pair, :], bank[6][:, 0:T]).then_inc(o2_half, 1)
            for q in range(4):
                act_up(act, where[("proj", l)], l + 1, q)
                act_round(act, where[("proj", l)] + q + 2)
            for q in range(4):
                act_round(act, where[("out2", l)] + q + 2)
            idx, ln, tb = norms[("mix", l)]
            norm_act(act, idx, ln, tb, KD, tile_tmp, 1.0, 2, tile_tmp, v2(l, "ln_mix_b"), tile_u)
            ffn_act_engine(act, where[("fb", l)], 11, True, 16 + 22 * l + 11)
            idx, ln, tb = norms[("fb", l)]
            norm_act(act, idx, ln, tb, KD, tile_tmp, 1.0, 2, tile_tmp, v2(l, "ln_f2_b"), tile_u if l < LAYERS - 1 else (lambda k: sq[:, k, :]))

        def dve_rope(dve, l, r):
            n = NROPE * l + r
            w = 1 if r == 2 else 2
            link = lambda ins: chain(dve, dve_n, dve_chain, ins)
            o = (q_n[:, 0:2, :], q_n[:, 2:4, :], kc.rearrange("p (a t) -> p a t", a=1), ksw)[r]
            bc = lambda t_: t_.rearrange("p (a t) -> p a t", a=1).to_broadcast([P, w, T])
            dve.wait_ge(perm_done, n + 1)
            dve.tensor_tensor(rope_tmp[:, 0:w, :], two(bank[7])[:, 0:w, :], bc(sin_n), ALU.mult).then_inc(bank7_free, 1)
            link(dve.tensor_tensor(o, rope_raw[r % 2][:, 0:w, :], bc(cos_n), ALU.mult))
            dve.wait_ge(bank7_free, B7 * l + r + 2)
            dve.tensor_tensor(o, o, rope_tmp[:, 0:w, :], ALU.add).then_inc(rope_done, 1)
            dve.wait_ge(rope_done, n + 1)

        def dve_ffn_end(dve, l, tag):
            wait_used(dve, where[(tag, l)] + 32)
            for b in range(4):
                dve.scalar_tensor_tensor(out=tmp[:, 2 * b:2 * b + 2, :], in0=two(bank[b]), scalar=0.5, in1=res[:, 2 * b:2 * b + 2, :],
                                         op0=ALU.mult, op1=ALU.add).then_inc(norm_in, 2)

        def dve_max(dve, l, m):
            n = NU * l + m
            dve.wait_ge(a_done, n + 1)
            for tt in range(NTT):
                ins = dve.tensor_reduce(cols1[:, m % 2, tt:tt + 1], bank[m % 2][:, unit_cols(tt)], AX.X, ALU.max, negate=True)
            ins.then_inc(max_done, 1)

        def dve_weigh(dve, l, m):
            link = lambda ins: chain(dve, dve_n, dve_chain, ins)
            n = NU * l + m
            _, _, _, h, w = unit(m)
            inv = cols1[:, m % 2, 4:6]
            dve.wait_ge(exp_done, n + 1)
            link(dve.reciprocal(inv, cols1[:, m % 2, 2:4]))
            if w is not None:
                link(dve.tensor_tensor(inv, inv, gn[:, :, h, w], ALU.mult))
            for tt in range(NTT):
                c = unit_cols(tt)
                ins = dve.tensor_scalar(probs[m % 2][:, c], probs[m % 2][:, c], inv[:, tt:tt + 1], None, ALU.mult)
            ins.then_inc(p_ready, 1)

        def b2_dve(dve, l):
            link = lambda ins: chain(dve, dve_n, dve_chain, ins)
            TT = lambda o, x, y, op: link(dve.tensor_tensor(o, x, y, op))
            ffn_dve_engine(dve, where[("fa", l)], 11, True, 16 + 22 * l)
            dve_ffn_end(dve, l, "fa")
            idx, ln, tb = norms[("fa", l)]
            norm_dve(dve, idx, ln, tb, KD, tile_tmp, v2(l, "ln_f1_g"), tile_tmp, v2(l, "ln_f1_b"), tile_u, tile_l, ALPHA)
            n0 = where[("in2", l)]
            for i in range(7):
                dve_split(dve, n0 + i + 2)
                if i == 1:
                    idx, ln, tb = norms[("q", l)]
                    norm_dve(dve, idx, ln, tb, 2, lambda k: cq[:, k, :], v2(l, "q_norm_g"), lambda k: cq[:, k, :], None,
                             lambda k: hh[:, k, :], lambda k: hl[:, k, :])
                if i == 2:
                    idx, ln, tb = norms[("kv", l)]
                    norm_dve(dve, idx, ln, tb, 1, lambda k: ckv, v2(l, "kv_norm_g"), lambda k: ckv, None,
                             lambda k: ckh[:, :], lambda k: ckl[:, :])
                    dve.wait_ge(gn_t, l + 1)
                    dve.tensor_scalar(gn.rearrange("p a h c -> p (a h c)"), bank[7][:, 0:NTT * 3 * HEADS], 0.5, 0.5,
                                      ALU.mult, ALU.add).then_inc(bank7_free, 1)
                if i >= 3:
                    dve_rope(dve, l, i - 3)
                if i >= 5:
                    j = i - 5
                    dve.wait_ge(x_blocks, 2 * l + j + 1)
                    pe_rows = vec2[:, l, ROW2[("cmp_pe_k", "cmp_pe_v")[j]]:ROW2[("cmp_pe_k", "cmp_pe_v")[j]] + 16]
                    x3 = x_f[j].rearrange("p (s c) -> p s c", s=16)
                    TT(x3, x3, pe_rows.rearrange("p (s o) -> p s o", o=1).to_broadcast([P, 16, 2 * N_CMP]), ALU.add)
                    link(dve.tensor_copy(x_halves[j][0], x_f[j]))
                    dve.tensor_tensor(x_halves[j][1], x_f[j], x_halves[j][0].bitcast(F32), ALU.subtract).then_inc(x_l, 1)
            dve_split(dve, where[("uq", l)] + 2)
            dve_split(dve, where[("cmp", l)] + 2)
            bc = lambda t_, r: t_[r].rearrange("p (a t) -> p a t", a=1).to_broadcast([ROPE_M, 2, T])
            r = slice(HD, QK_M)
            for b in range(4):
                dve.wait_ge(m_perm, 4 * l + b + 1)
                q_ = qm[r, 2 * b:2 * b + 2, :]
                link(dve.tensor_tensor(rope_tmp[r, :, :], two(bank[b])[r], bc(sin_m, r), ALU.mult))
                TT(q_, q_, bc(cos_m, r), ALU.mult)
                dve.tensor_tensor(q_, q_, rope_tmp[r, :, :], ALU.add).then_inc(m_roped, 1)
                dve.wait_ge(m_roped, 4 * l + b + 1)
            dve_split(dve, where[("cmp", l)] + 3)
            dve_split(dve, where[("ukv", l)] + 2)
            r = slice(0, ROPE_M)
            dve.wait_ge(kpe_perm, l + 1)
            dve.tensor_tensor(rope_tmp[r, 0, :], bank[7][r, 0:T], sin_m[r], ALU.mult).then_inc(bank7_free, 1)
            TT(kper, kpe, cos_m[r], ALU.mult)
            dve.wait_ge(bank7_free, B7 * l + NROPE + 2)
            TT(kper, kper, rope_tmp[r, 0, :], ALU.add)
            dve.tensor_copy(km[HD:QK_M, :, :], kper.rearrange("p (a t) -> p a t", a=1).to_broadcast([ROPE_M, HEADS, T])).then_inc(km_pe, 1)
            dve.wait_ge(w2_done, 2 * l + 1)
            for g in range(KVH):
                r = slice(g * HD, (g + 1) * HD)
                ins = dve.tensor_copy(kcc[r, g * N_CMP:(g + 1) * N_CMP], bank[6][r, g * N_CMP:(g + 1) * N_CMP])
            ins.then_inc(w2_read, 1)
            dve.wait_ge(w2_done, 2 * l + 2)
            dve.tensor_copy(vcc, bank[5][0:N_CMP, 0:P]).then_inc(w2_read, 1)
            dve_split(dve, where[("gate2", l)] + 2)
            dve_split(dve, where[("gate2", l)] + 3)
            dve.wait_ge(cs_done, l + 1)
            s4 = lambda t_: t_.rearrange("p (a h c) -> p a h c", a=NTT, c=N_CMP)
            s3 = c_scores.rearrange("p (n c) -> p n c", c=N_CMP)
            bc4 = lambda t_: t_[:, :, :].rearrange("p a (h c) -> p a h c", h=1).to_broadcast([P, NTT, HEADS, N_CMP])
            bc3 = lambda t_: t_.rearrange("p (n o) -> p n o", o=1).to_broadcast([P, NTT * HEADS, N_CMP])
            dve.tensor_tensor(s4(c_scores), s4(bank[7][:, 0:240]), bc4(cmask), ALU.add).then_inc(bank7_free, 1)
            dve.wait_ge(bank7_free, B7 * (l + 1))
            link(dve.tensor_reduce(c_sums[:, 0, :], s3, AX.X, ALU.max))
            dve.tensor_tensor(s3, s3, bc3(c_sums[:, 0, :]), ALU.subtract).then_inc(cs_shift, 1)
            dve.wait_ge(cs_exp, l + 1)
            link(dve.tensor_reduce(c_sums[:, 1, :], s3, AX.X, ALU.add))
            link(dve.reciprocal(c_sums[:, 2, :], c_sums[:, 1, :]))
            g3 = c_sums[:, 2, :].rearrange("p (a h) -> p a h", a=NTT)
            TT(g3, g3, gn[:, :, :, 0], ALU.mult)
            TT(s3, s3, bc3(c_sums[:, 2, :]), ALU.mult)
            dve.tensor_tensor(s4(c_scores), s4(c_scores), bc4(cvalid), ALU.mult).then_inc(cs_ready, 1)
            for s in range(NU + 2):
                if s < NU:
                    dve_max(dve, l, s)
                if 2 <= s < NQ + 2:
                    dve_split_quarter(dve, where[("gate2", l)] + EARLY + (s - 2) // 4 + 2, (s - 2) % 4)
                if s < NU:
                    dve_weigh(dve, l, s)
                if C0 <= s < C0 + 4:
                    q = s - C0
                    dve.wait_ge(ct_done, 4 * l + q + 1)
                    dve.tensor_copy(p_cmp_t[:, 2 * T * q:2 * T * (q + 1)], bank[7][0:N_CMP, :]).then_inc(ct_taken, 1)
                pair = last_of_pair(s - 2) if s >= 2 else None
                if pair is not None:
                    dve.wait_ge(o2_half, 8 * l + pair + 1)
                    dve.tensor_tensor(bl[:, pair, :], bank[6][:, 0:T], bh[:, pair, :].bitcast(F32), ALU.subtract).then_inc(o2_taken, 1)
            for b in range(2):
                dve.wait_ge(lin2[b], 8 * (l + 1))
            for q in range(4):
                dve_up(dve, where[("proj", l)], l + 1, q, "AB")
                dve_split(dve, where[("proj", l)] + q + 2)
            for q in range(4):
                dve_out(dve, where[("out2", l)], q, tmp)
                dve_split(dve, where[("out2", l)] + q + 2)
            idx, ln, tb = norms[("mix", l)]
            norm_dve(dve, idx, ln, tb, KD, tile_tmp, v2(l, "ln_mix_g"), tile_tmp, v2(l, "ln_mix_b"), tile_u, tile_l, ALPHA)
            ffn_dve_engine(dve, where[("fb", l)], 11, True, 16 + 22 * l + 11)
            dve_ffn_end(dve, l, "fb")
            idx, ln, tb = norms[("fb", l)]
            last = l == LAYERS - 1
            norm_dve(dve, idx, ln, tb, KD, tile_tmp, v2(l, "ln_f2_g"), tile_tmp, v2(l, "ln_f2_b"), None if last else tile_u,
                     None if last else tile_l, None if last else ALPHA)

        out_tok = gflat[:, 0:NTT * D].rearrange("p (a d) -> p a d", a=NTT)

        def dve_output(dve):
            for tt in range(NTT):
                for b in range(2):
                    dve.wait_ge(final_t, 2 * tt + b + 1)
                    dve.tensor_copy(out_tok[:, tt, b * 512:(b + 1) * 512], bank[2 * tt + b][:, :]).then_inc(final_copied, 1)

        def sp_output(sp):
            for tt in range(NTT):
                sp.wait_ge(final_copied, 2 * tt + 2)
                sp.dma_start(out[0].rearrange("(a p) d -> p a d", p=P)[:, tt, :], out_tok[:, tt, :]).then_inc(out_done, 16)
            sp.wait_ge(out_done, 16 * NTT)

        block = ctx.enter_context(nc.Block())
        layers = range(LAYERS if UPTO == "full" else 0)

        @block.sync
        def _(sp):
            b1_sp(sp)
            for l in layers:
                b2_sp(sp, l)
            if UPTO == "full":
                sp_output(sp)

        @block.gpsimd
        def _(pool):
            pool_consts(pool)
            b1_pool(pool)

        @block.scalar
        def _(act):
            b1_act(act)
            for l in layers:
                b2_act(act, l)

        @block.vector
        def _(dve):
            b1_dve(dve)
            for l in layers:
                b2_dve(dve, l)
            if UPTO == "full":
                dve_output(dve)

        @block.tensor
        def _(pe):
            b1_pe(pe)
            pe.wait_ge(w2_in, 16 * 4 * LAYERS)
            for l in layers:
                b2_pe(pe, l)
            if UPTO == "full":
                pe_output(pe)


_INS = ["x", "norm_mix", "w_in", "A_re", "A_im", "log_dt", "B_re", "B_im", "C_re", "C_im", "D_skip", "w_glu", "b_glu",
        "w_up_ssm", "w_up_attn", "w_gate", "b_gate", "w_out", "norm_mlp", "w_ff1", "w_ff2", "norm_final", "ln_f1_g_2",
        "ln_f1_b_2", "ffn1_wg_2", "ffn1_wu_2", "ffn1_wd_2", "w_in_2", "q_norm_g_2", "w_uq_2", "kv_norm_g_2",
        "w_ukv_2", "cmp_pe_k_2", "cmp_k_w1_2", "cmp_k_b1_2", "cmp_k_w2_2", "cmp_pe_v_2", "cmp_v_w1_2", "cmp_v_b1_2",
        "cmp_v_w2_2", "w_proj_mla_2", "w_proj_nsa_2", "w_out_2", "ln_mix_g_2", "ln_mix_b_2", "ffn2_wg_2", "ffn2_wu_2",
        "ffn2_wd_2", "ln_f2_g_2", "ln_f2_b_2"]


def kernel(**inputs):
    import concourse.bacc as bacc
    from concourse.bass_utils import run_bass_kernel_spmd

    nc = bacc.Bacc("TRN2", target_bir_lowering=False, num_devices=1)
    arrays = {name: np.ascontiguousarray(inputs[name]) for name in _INS}
    arrays["shape_tables"] = shape_tables()
    a = {name: nc.dram_tensor(name, v.shape, mybir.dt.from_np(v.dtype), kind="ExternalInput").ap()
         for name, v in arrays.items()}
    out = nc.dram_tensor("out", (1, T, D), F32, kind="ExternalOutput").ap()
    hybrid_ssm_attention_kernel(nc, a, out)
    r = run_bass_kernel_spmd(nc, [arrays], core_ids=[0])
    return r.results[0]["out"]
```

```python
from contextlib import ExitStack

import numpy as np

import concourse.bass as bass
from concourse import mybir

F32 = mybir.dt.float32
F32R = mybir.dt.float32r
BF16 = mybir.dt.bfloat16
ALU = mybir.AluOpType
ACT = mybir.ActivationFunctionType
AX = mybir.AxisListType

P = 128
T = 256
NTT = T // P
D = 1024
KD = D // P
DS = 512
KS = DS // P
HEADS = 8
HD = 64
STATES = 64
NG = 32
ST = NG * STATES // P
FF1 = 4096
FF2 = 2816
LAYERS = 2
SLAB = 2048
WCOLS = SLAB // KD
PI = float(np.pi)
ROUND = 12582912.0
NEG = -1e30
ALPHA = (2 * LAYERS) ** 0.25
EPS_RMS = 1e-6
EPS_LN = 1e-5
Q_RANK, KV_RANK, ROPE_M = 256, 128, 32
QK_M = HD + ROPE_M
SCALE_M = QK_M ** -0.5
SCALE_N = HD ** -0.5
ROT_N = HD // 4
THETA = 500000.0
S_CMP, L_CMP = 16, 32
N_CMP = (T - L_CMP) // S_CMP + 1
KVH = 2
HPG = HEADS // KVH
C_Q, C_KV = 0, Q_RANK
C_QN = C_KV + KV_RANK + ROPE_M
C_KVN = C_QN + HEADS * HD
C_GN = C_KVN + 6 * KVH * HD
C_GM = C_GN + 3 * HEADS

ROW1 = {}
_n = 0
for _name, _rows in (("norm_mix", 8), ("norm_mlp", 8), ("norm_final", 8), ("D_skip", 4), ("b_glu", 4),
                     ("b_gate", 16), ("A_re", 16), ("A_im", 16)):
    ROW1[_name] = _n
    _n += _rows
ROWS1 = _n
ROW2 = {}
_n = 0
for _name, _rows in (("ln_f1_g", 8), ("ln_f1_b", 8), ("ln_mix_g", 8), ("ln_mix_b", 8), ("ln_f2_g", 8),
                     ("ln_f2_b", 8), ("q_norm_g", 2), ("kv_norm_g", 1), ("cmp_k_b1", 1), ("cmp_v_b1", 1),
                     ("cmp_pe_k", 16), ("cmp_pe_v", 16)):
    ROW2[_name] = _n
    _n += _rows
ROWS2 = _n


SLABS1 = FF1 // (2 * P)
SLABS2 = FF2 // (2 * P)
KC1, KC2 = 8, 30


def shape_tables():
    def rope(rot, rows, at):
        inv = 1.0 / (np.float32(THETA) ** (np.arange(0, rot, 2, dtype=np.float32) / np.float32(rot)))
        ang = np.arange(T, dtype=np.float32)[:, None] * inv[None, :].astype(np.float32)
        cos, sin = np.cos(ang).astype(np.float32), np.sin(ang).astype(np.float32)
        c, s = np.ones((rows, T), np.float32), np.zeros((rows, T), np.float32)
        perm = np.zeros((rows, rows), np.float32)
        half = rot // 2
        for a in at:
            c[a:a + half] = cos.T
            c[a + half:a + rot] = cos.T
            s[a:a + half] = -sin.T
            s[a + half:a + rot] = sin.T
            for r in range(half):
                perm[a + half + r, a + r] = 1.0
                perm[a + r, a + half + r] = 1.0
        return c, s, perm
    cn, sn, pn = rope(ROT_N, P, (0, HD))
    cm, sm, pm = rope(ROPE_M, P, (0, HD))
    steps = np.broadcast_to(np.arange(T, dtype=np.float32), (P, T))
    return np.concatenate([cn, sn, cm, sm, pn, pm, steps], axis=1)


def plan():
    slabs, used, last = [], [0, 0, 0], [1, 2]

    def oldest():
        return 3 - sum(last)

    def add(what, part, slot=None):
        if slot is None:
            slot = oldest()
        slabs.append((what, part, slot, used[slot]))
        used[slot] += 1
        if slot != last[1]:
            last[:] = [last[1], slot]

    where = {}

    def mark(name):
        where[name] = len(slabs)

    mark("in1")
    for n in range(8):
        add("in1", n)
    mark("gate1")
    for n in range(8):
        add("gate1", n)
    mark("glu")
    add("glu", 0)
    mark("up1")
    for n, w in enumerate(("up_attn", "up_ssm", "up_attn", "up_ssm")):
        add(w, n // 2)
    mark("out1")
    for n in range(4):
        add("out1", n)
    mark("ffn1")
    g, s, d = oldest(), last[0], last[1]
    add("ff1", 0, g)
    for i in range(1, SLABS1):
        add("ff1", i, s)
        add("ff2", i - 1, d)
    add("ff2", SLABS1 - 1)

    def ffn(tag, l):
        g, d, u = oldest(), last[1], last[0]
        add(tag + "_g", (l, 0), g)
        add(tag + "_u", (l, 0), u)
        for i in range(1, SLABS2 - 1):
            add(tag + "_g", (l, i), g)
            add(tag + "_d", (l, i - 1), d)
            add(tag + "_u", (l, i), u)
        add(tag + "_g", (l, SLABS2 - 1), g)
        add(tag + "_u", (l, SLABS2 - 1), u)
        add(tag + "_d", (l, SLABS2 - 2), d)
        add(tag + "_d", (l, SLABS2 - 1))

    for l in range(LAYERS):
        mark(("fa", l))
        ffn("fa", l)
        mark(("in2", l))
        for n in range(7):
            add("in2", (l, n))
        mark(("uq", l))
        add("uq", (l, 0))
        mark(("cmp", l))
        add("cmp_k", (l, 0))
        add("cmp_v", (l, 0))
        mark(("ukv", l))
        add("ukv", (l, 0))
        mark(("gate2", l))
        for n in range(8):
            add("gate2", (l, n))
        mark(("proj", l))
        for n, w in enumerate(("proj_m", "proj_n", "proj_m", "proj_n")):
            add(w, (l, n // 2))
        mark(("out2", l))
        for n in range(4):
            add("out2", (l, n))
        mark(("fb", l))
        ffn("fb", l)
    return slabs, where


def hybrid_ssm_attention_kernel(nc, a, out):
    slabs, where = plan()
    for n, (_, _, slot, _u) in enumerate(slabs):
        assert n == 0 or slabs[n - 1][2] != slot

    def num_loads(what, part):
        return 2 if what == "in2" and part[1] in (1, 2, 3, 5, 6) else 1

    loads_so_far, total = [], [0, 0, 0]
    for what, part, slot, _u in slabs:
        total[slot] += num_loads(what, part)
        loads_so_far.append(total[slot])

    with ExitStack() as ctx:
        def sb(name, shape, dt=F32):
            return ctx.enter_context(nc.sbuf_tensor(name, shape, dt))

        def sem(name):
            return ctx.enter_context(nc.semaphore(name))

        bank = [ctx.enter_context(nc.psum_tensor(f"bank{i}", [P, 512], F32)) for i in range(8)]
        raw = sb("raw", [P, 3, SLAB])
        wh = sb("wh", [P, 3, SLAB], F32R)
        wl = sb("wl", [P, 3, SLAB], F32R)
        res = sb("res", [P, KD, T])
        tmp = sb("tmp", [P, KD, T])
        sq = sb("sq", [P, KD, T])
        uh = sb("uh", [P, KD, T], F32R)
        ul = sb("ul", [P, KD, T], F32R)
        bh = sb("bh", [P, KD, T], F32R)
        bl = sb("bl", [P, KD, T], F32R)
        hh = sb("hh", [P, 2, T], F32R)
        hl = sb("hl", [P, 2, T], F32R)
        ckh = sb("ckh", [P, T], F32R)
        ckl = sb("ckl", [P, T], F32R)
        act_out = sb("act_out", [P, 2, T])
        hid = sb("hid", [P, 2, T])
        stat = sb("stat", [P, 2, T])
        rstd = sb("rstd", [P, T])
        gates = sb("gates", [P, 2 * KD, T])
        shared = sb("shared", [P, 4096])
        small = sb("small", [P, 4096])
        tables = sb("tables", [P, 2560])
        steps_t = sb("steps_t", [P, T])
        vec1 = sb("vec1", [P, ROWS1])
        vec2 = sb("vec2", [P, LAYERS, ROWS2])
        cmp_w2 = sb("cmp_w2", [P, LAYERS, 2, 2, HD])
        ident = sb("ident", [P, P])
        identb = sb("identb", [P, P], BF16)
        causal = sb("causal", [P, P], BF16)
        earlier = sb("earlier", [P, P], BF16)
        suffix = sb("suffix", [P, P])
        minus1 = sb("minus1", [P, P])
        mean_w = sb("mean_w", [P, P])
        zero_w = sb("zero_w", [P, P], F32R)
        cmask = sb("cmask", [P, NTT, N_CMP])
        cvalid = sb("cvalid", [P, NTT, N_CMP])
        cols1 = sb("cols1", [P, 16, 16])
        kcc = sb("kcc", [P, KVH * N_CMP])
        half_b = sb("half_b", [P, 2 * KD])
        quarter = sb("quarter", [P, 4])

        raw_full = [sem(f"raw_full{i}") for i in range(3)]
        rounded = [sem(f"rounded{i}") for i in range(3)]
        split = [sem(f"split{i}") for i in range(3)]
        used = [sem(f"used{i}") for i in range(3)]
        dve_chain, act_chain, pool_chain = sem("dve_chain"), sem("act_chain"), sem("pool_chain")
        dve_n, act_n, pool_n = [0], [0], [0]
        consts = sem("consts")
        vec_in = sem("vec_in")
        x_in = sem("x_in")
        ssm_in = sem("ssm_in")
        tr_ready = sem("tr_ready")
        norm_in = sem("norm_in")
        summed = sem("summed")
        sum_done = sem("sum_done")
        centred = sem("centred")
        squared = sem("squared")
        var_done = sem("var_done")
        root_done = sem("root_done")
        scaled = sem("scaled")
        norm_h = sem("norm_h")
        res_ready = sem("res_ready")
        norm_out = sem("norm_out")
        ffn_act = sem("ffn_act")
        hid_ready = sem("hid_ready")
        down_bank = sem("down_bank")
        hid_step = sem("hid_step")
        lin_free = [sem("lin_free0"), sem("lin_free1")]

        def two(b):
            return b[:, :].rearrange("p (a t) -> p a t", a=2)

        def chain(eng, count, s, ins):
            count[0] += 1
            ins.then_inc(s, 1)
            eng.wait_ge(s, count[0])

        def slab_view(buf, slot, kt, c):
            return buf[:, slot, 0:kt * c].rearrange("p (k c) -> p k c", c=c)

        def cols(w, c0, c):
            return w[:, bass.ds(c0, c)].rearrange("(k p) c -> p k c", p=P)

        def rows(w, k0, kt):
            return w[bass.ds(k0 * P, kt * P), :].rearrange("(k p) c -> p k c", p=P)

        def slab_loads(what, part, slot):
            def one(w_cols, kt, c):
                return [(slab_view(raw, slot, kt, c), w_cols)]
            if what == "in1":
                return one(cols(a["w_in"][0], part * WCOLS, WCOLS), KD, WCOLS)
            if what == "gate1":
                return one(cols(a["w_gate"][0], part * WCOLS, WCOLS), KD, WCOLS)
            if what == "glu":
                return one(cols(a["w_glu"][0], 0, DS), KS, DS)
            if what in ("up_ssm", "up_attn"):
                return one(cols(a["w_" + what][0], part * 512, 512), KS, 512)
            if what == "out1":
                return one(cols(a["w_out"][0], part * WCOLS, WCOLS), KD, WCOLS)
            if what == "ff1":
                return one(cols(a["w_ff1"][0], part * WCOLS, WCOLS), KD, WCOLS)
            if what == "ff2":
                return one(rows(a["w_ff2"][0], part * 2, 2), 2, D)
            l, i = part
            if what[:2] in ("fa", "fb"):
                ffn = "ffn1" if what[:2] == "fa" else "ffn2"
                w = a[f"{ffn}_w{what[3]}_2"][l]
                if what[3] == "d":
                    return one(rows(w, i * 2, 2), 2, D)
                return one(cols(w, i * WCOLS, WCOLS), KD, WCOLS)
            if what == "in2":
                w = a["w_in_2"][l]
                if i == 0:
                    return one(cols(w, C_Q, Q_RANK), KD, Q_RANK)
                if i == 1:
                    n1, n2 = KV_RANK + ROPE_M, 3 * HEADS
                    v = slab_view(raw, slot, KD, n1 + n2)
                    return [(v[:, :, 0:n1], cols(w, C_KV, n1)), (v[:, :, n1:], cols(w, C_GN, n2))]
                if i in (2, 3):
                    v = slab_view(raw, slot, KD, WCOLS)
                    return [(v[:, :, g * 2 * HD:(g + 1) * 2 * HD], cols(w, C_QN + (g * HPG + 2 * (i - 2)) * HD, 2 * HD))
                            for g in range(KVH)]
                if i == 4:
                    return one(cols(w, C_KVN, WCOLS), KD, WCOLS)
                v = slab_view(raw, slot, KD, WCOLS)
                return [(v[:, :, j * P:(j + 1) * P], cols(w, C_KVN + (2 + i - 5 + 2 * j) * P, P)) for j in range(2)]
            if what == "uq":
                return one(cols(a["w_uq_2"][l], 0, HEADS * QK_M), 2, HEADS * QK_M)
            if what == "ukv":
                return one(cols(a["w_ukv_2"][l], 0, 2 * HEADS * HD), 1, 2 * HEADS * HD)
            if what in ("cmp_k", "cmp_v"):
                return one(cols(a[what + "_w1_2"][l], 0, P), 16, P)
            if what == "gate2":
                return one(cols(a["w_in_2"][l], C_GM + i * WCOLS, WCOLS), KD, WCOLS)
            if what in ("proj_m", "proj_n"):
                w = a["w_proj_mla_2" if what == "proj_m" else "w_proj_nsa_2"][l]
                return one(cols(w, i * 512, 512), KS, 512)
            assert what == "out2"
            return one(cols(a["w_out_2"][l], i * WCOLS, WCOLS), KD, WCOLS)

        def slab_words(what, part):
            if what == "in2" and part[1] == 1:
                return KD * (KV_RANK + ROPE_M + 3 * HEADS)
            return {"uq": 2 * HEADS * QK_M, "ukv": 2 * HEADS * HD}.get(what, SLAB)

        def sp_slab(sp, n, part=None, more=0):
            what, p0, slot, u = slabs[n]
            part = p0 if part is None else part
            if not (isinstance(more, int) and u + more == 0):
                sp.wait_ge(split[slot], more + u)
            for dst, src in slab_loads(what, part, slot):
                sp.dma_start(dst, src).then_inc(raw_full[slot], 16)

        def slab_pieces(buf, n, halves):
            what, part, slot, _u = slabs[n]
            if what == "in2" and part[1] in (2, 3):
                v = slab_view(buf, slot, KD, WCOLS)
                if halves:
                    return [v.rearrange("p k (h g d) -> p g k h d", g=KVH, d=HD)[:, g] for g in range(KVH)]
                return [v.rearrange("p k (g h d) -> p g k h d", g=KVH, d=HD)[:, g] for g in range(KVH)]
            return [buf[:, slot, 0:slab_words(what, part)]]

        def act_round(act, n, more=0):
            what, part, slot, u = slabs[n]
            act.wait_ge(raw_full[slot], more * 16 + 16 * loads_so_far[n])
            if not (isinstance(more, int) and u + more == 0):
                act.wait_ge(used[slot], more + u)
            for src, dst in zip(slab_pieces(raw, n, False), slab_pieces(wh, n, True)):
                ins = act.copy(dst, src)
            ins.then_inc(rounded[slot], 1)

        def dve_split(dve, n, more=0):
            what, part, slot, u = slabs[n]
            dve.wait_ge(rounded[slot], more + u + 1)
            for src, upper, dst in zip(slab_pieces(raw, n, False), slab_pieces(wh, n, True), slab_pieces(wl, n, True)):
                ins = dve.tensor_tensor(dst, src, upper.bitcast(F32), ALU.subtract)
            ins.then_inc(split[slot], 1)

        def act_round_half(act, n, j):
            _w, _p, slot, u = slabs[n]
            if j == 0:
                act.wait_ge(raw_full[slot], 16 * loads_so_far[n])
                act.wait_ge(used[slot], u)
            c = slice(j * SLAB // 2, (j + 1) * SLAB // 2)
            ins = act.copy(wh[:, slot, c], raw[:, slot, c])
            if j == 1:
                ins.then_inc(rounded[slot], 1)

        def dve_split_quarter(dve, n, j):
            _w, _p, slot, u = slabs[n]
            if j == 0:
                dve.wait_ge(rounded[slot], u + 1)
            c = slice(j * SLAB // 4, (j + 1) * SLAB // 4)
            ins = dve.tensor_tensor(wl[:, slot, c], raw[:, slot, c], wh[:, slot, c].bitcast(F32), ALU.subtract)
            if j == 3:
                ins.then_inc(split[slot], 1)

        def pe_slab(pe, n, more=0):
            slot, u = slabs[n][2:]
            pe.wait_ge(split[slot], more + u + 1)
            return slot

        def mm3(pe, o, wa, wb, xa, xb, start, stop, swap=False):
            for n, (w, x) in enumerate(((wa, xa), (wa, xb), (wb, xa))):
                if swap:
                    w, x = x, w
                mm = pe.matmul(o, w, x, start=start and n == 0, stop=stop and n == 2, skip_group_check=True)
            return mm

        zeros_t = zero_w[:, :].rearrange("p (a c) -> p a c", a=1).to_broadcast([P, T // P, P])

        def ffn_pe(pe, n0, iters, has_up, ih0, first_ready):
            for b in range(4):
                for c in range(2):
                    pe.matmul(bank[b][:, c * T:(c + 1) * T], zero_w[:, :], zeros_t, start=c == 0, stop=True,
                              skip_group_check=True)
            per = 3 if has_up else 2

            def up_half(n, more, b, ready=None):
                slot = pe_slab(pe, n, more)
                order = [(f, k) for f in range(2) for k in range(KD)]
                if ready is not None:
                    order.sort(key=lambda x: x[1])
                for f, k in order:
                    if ready is not None and f == 0:
                        pe.wait_ge(norm_out, ready + k + 1)
                    mm = mm3(pe, bank[b][:, f * T:(f + 1) * T],
                             slab_view(wh, slot, KD, WCOLS)[:, k, f * P:(f + 1) * P],
                             slab_view(wl, slot, KD, WCOLS)[:, k, f * P:(f + 1) * P],
                             uh[:, k, :], ul[:, k, :], k == 0 and (f == 0 or ready is None), k == KD - 1)
                mm.then_inc(used[slot], 1)

            def gate(n, more=0, i=None, ready=None):
                if i is not None:
                    pe.wait_ge(ffn_act, i + ih0)
                up_half(n, more, 4, ready)

            def down(n, i, more=0, last=False):
                slot = pe_slab(pe, n, more)
                pe.wait_ge(hid_ready, i + ih0 + 1)
                xh, xl = (bh, bl) if has_up and last else (hh, hl)
                for m in range(KD):
                    for k in range(2):
                        mm = mm3(pe, bank[m // 2][:, (m % 2) * T:(m % 2 + 1) * T],
                                 slab_view(wh, slot, 2, D)[:, k, m * P:(m + 1) * P],
                                 slab_view(wl, slot, 2, D)[:, k, m * P:(m + 1) * P],
                                 xh[:, k, :], xl[:, k, :], False, False)
                    if last and m in (1, 3, 5):
                        mm.then_inc(down_bank, 1)
                mm.then_inc(used[slot], 1)

            gate(n0, ready=first_ready)
            if has_up:
                up_half(n0 + 1, 0, 5)
            n1 = n0 + (2 if has_up else 1)
            with pe.Fori(1, iters - 1, 1) as i:
                gate(n1, i - 1, i)
                down(n1 + 1, i - 1, i - 1)
                if has_up:
                    up_half(n1 + 2, i - 1, 5)
            n1 += per * (iters - 2)
            gate(n1, 0, iters - 1)
            if has_up:
                up_half(n1 + 1, 0, 5)
            down(n1 + per - 1, iters - 2)
            down(n1 + per, iters - 1, last=True)

        def ffn_split(eng, do, n0, iters, has_up, epilogue, leave_last=False):
            per = 3 if has_up else 2
            n1 = n0 + per - 1

            def step(n, what, i, more=0, i0=0):
                epilogue(what, n, i, more)
                if n + 2 < len(slabs):
                    do(eng, n + 2, more)

            def turn(i, more, at):
                step(at, "gate", i, more)
                step(at + 1, "down", i - 1, more)
                if has_up:
                    step(at + 2, "up", i, more)

            step(n0, "gate", 0)
            if has_up:
                step(n0 + 1, "up", 0)
            with eng.Fori(1, iters - 2, 1) as i:
                turn(i, i - 1, n1)
            turn(iters - 2, 0, n1 + per * (iters - 3))
            last = n1 + per * (iters - 2)
            step(last, "gate", iters - 1)
            if has_up:
                step(last + 1, "up", iters - 1)
            step(last + per - 1, "down", iters - 2)
            epilogue("down", last + per, iters - 1, 0)
            if not leave_last and last + per + 2 < len(slabs):
                do(eng, last + per + 2)

        def ffn_act_engine(act, n0, iters, has_up, ih0):
            def epilogue(what, n, i, more):
                if what != "gate":
                    return
                slot, u = slabs[n][2:]
                if not (isinstance(i, int) and i == 0):
                    act.wait_ge(hid_ready, i + ih0)
                act.wait_ge(used[slot], more + u + 1)
                act.activation(act_out[:, :, :], two(bank[4]), ACT.Silu if has_up else ACT.Relu).then_inc(ffn_act, 1)
            ffn_split(act, act_round, n0, iters, has_up, epilogue)

        def ffn_dve_engine(dve, n0, iters, has_up, ih0):
            def epilogue(what, n, i, more):
                if (has_up and what != "up") or (not has_up and what == "gate" and not (isinstance(i, int) and i == 0)):
                    return
                if not has_up and what == "down":
                    i = i + 1
                    if isinstance(i, int) and i == iters:
                        return
                slot, u = slabs[n][2:]
                dve.wait_ge(used[slot], more + u + 1)
                dve.wait_ge(ffn_act, i + ih0 + 1)
                other = two(bank[5]) if has_up else act_out[:, :, :]
                dve.tensor_tensor(hid[:, :, :], act_out[:, :, :], other, ALU.mult).then_inc(hid_step, 1)
                dve.wait_ge(hid_step, 2 * i + (2 * ih0 + 1))
                last = has_up and isinstance(i, int) and i == iters - 1
                xh, xl = (bh[:, 0:2, :], bl[:, 0:2, :]) if last else (hh[:, :, :], hl[:, :, :])
                dve.tensor_copy(xh, hid[:, :, :]).then_inc(hid_step, 1)
                dve.wait_ge(hid_step, 2 * i + (2 * ih0 + 2))
                dve.tensor_tensor(xl, hid[:, :, :], xh.bitcast(F32), ALU.subtract).then_inc(hid_ready, 1)
            ffn_split(dve, dve_split, n0, iters, has_up, epilogue, leave_last=True)

        def norm_pe(pe, idx, ln, tb, kt, src, mean_bank=5):
            if ln is not None:
                pe.wait_ge(summed, ln + 1)
                pe.matmul(bank[mean_bank][:, 0:T], mean_w[:, :], stat[:, 0, :], start=True, stop=False)
                for k in (KD - 2, KD - 1):
                    pe.wait_ge(norm_in, tb + k + 1)
                    mm = pe.matmul(bank[mean_bank][:, 0:T], mean_w[:, :], src(k), start=False, stop=k == KD - 1)
                mm.then_inc(sum_done, 1)
                keep_clock(pe, KC1)
            for k in range(kt):
                pe.wait_ge(squared, tb + k + 1)
                mm = pe.matmul(bank[6][:, T:2 * T], mean_w[:, :], sqbuf(k), start=k == 0, stop=k == kt - 1)
            mm.then_inc(var_done, 1)
            keep_clock(pe, KC2 if kt == KD else 0)

        def keep_clock(pe, n):
            for _ in range(n):
                pe.matmul(bank[7][:, 0:T], zero_w[:, :], zeros_t, start=True, stop=True, skip_group_check=True)

        def sqbuf(k):
            return sq[:, k, :]

        def norm_pool(pool, tb):
            add = lambda o, x, y: pool.tensor_tensor(o, x, y, ALU.add)
            acc, pair = stat[:, 0, :], stat[:, 1, :]
            pool.wait_ge(norm_in, tb + 2)
            chain(pool, pool_n, pool_chain, add(acc, tmp[:, 0, :], tmp[:, 1, :]))
            for k in (2, 4):
                pool.wait_ge(norm_in, tb + k + 2)
                chain(pool, pool_n, pool_chain, add(pair, tmp[:, k, :], tmp[:, k + 1, :]))
                ins = add(acc, acc, pair)
                if k == 2:
                    chain(pool, pool_n, pool_chain, ins)
            ins.then_inc(summed, 1)

        def norm_squares(act, ln, tb, kt, src):
            for k in range(kt):
                if ln is not None:
                    act.wait_ge(centred, ln * KD + k + 1)
                else:
                    act.wait_ge(norm_in, tb + k + 1)
                act.activation(sqbuf(k), src(k), ACT.Square).then_inc(squared, 1)

        def norm_act(act, idx, ln, tb, kt, src, scale, eps, y, bias, o_h, squares=True, meanwhile=None):
            if squares:
                norm_squares(act, ln, tb, kt, src)
            act.wait_ge(var_done, idx + 1)
            act.activation(rstd[:, :], bank[6][:, T:2 * T], ACT.Sqrt, scale=scale, bias=quarter[:, eps:eps + 1]).then_inc(root_done, 1)
            if meanwhile is not None:
                meanwhile()
            if o_h is None:
                return
            for k in range(kt):
                act.wait_ge(scaled, tb + k + 1)
                if bias is None:
                    ins = act.copy(o_h(k), y(k))
                else:
                    ins = act.activation(o_h(k), y(k), ACT.Identity, bias=bias(k))
                ins.then_inc(norm_h, 1)

        def norm_dve(dve, idx, ln, tb, kt, src, gain, y, bias, o_h, o_l, res_scale=None, mean_bank=5):
            if ln is not None:
                dve.wait_ge(sum_done, ln + 1)
                for k in range(kt):
                    dve.tensor_tensor(src(k), src(k), bank[mean_bank][:, 0:T], ALU.subtract).then_inc(centred, 1)
            dve.wait_ge(root_done, idx + 1)
            chain(dve, dve_n, dve_chain, dve.reciprocal(rstd[:, :], rstd[:, :]))
            for k in range(kt + 2):
                if k < kt:
                    dve.scalar_tensor_tensor(out=y(k), in0=src(k), scalar=gain(k), in1=rstd[:, :],
                                             op0=ALU.mult, op1=ALU.mult).then_inc(scaled, 1)
                if k >= 2 and o_h is not None:
                    dve.wait_ge(norm_h, tb + k - 1)
                    if bias is None:
                        ins = dve.tensor_tensor(o_l(k - 2), y(k - 2), o_h(k - 2).bitcast(F32), ALU.subtract)
                    else:
                        ins = dve.scalar_tensor_tensor(out=o_l(k - 2), in0=y(k - 2), scalar=bias(k - 2),
                                                       in1=o_h(k - 2).bitcast(F32), op0=ALU.add, op1=ALU.subtract)
                    ins.then_inc(norm_out, 1)
            if res_scale is not None:
                for k in range(kt):
                    if bias is None:
                        dve.tensor_scalar(res[:, k, :], y(k), res_scale, None, ALU.mult).then_inc(res_ready, 1)
                    else:
                        dve.tensor_scalar(res[:, k, :], y(k), bias(k), res_scale, ALU.add, ALU.mult).then_inc(res_ready, 1)

        norms, n_ln, n_tiles = {}, 0, 0
        for name, is_ln, kt in [("mix1", 0, KD), ("mlp1", 0, KD), ("final1", 0, KD)] + [
                ((w, l), is_ln, kt) for l in range(LAYERS)
                for w, is_ln, kt in (("fa", 1, KD), ("q", 0, 2), ("kv", 0, 1), ("mix", 1, KD), ("fb", 1, KD))]:
            norms[name] = (len(norms), n_ln if is_ln else None, n_tiles)
            n_ln += is_ln
            n_tiles += kt
        tile_u = lambda k: uh[:, k, :]
        tile_l = lambda k: ul[:, k, :]
        tile_tmp = lambda k: tmp[:, k, :]
        tile_res = lambda k: res[:, k, :]

        def v1(name):
            return lambda k: vec1[:, ROW1[name] + k:ROW1[name] + k + 1]

        def v2(l, name):
            return lambda k: vec2[:, l, ROW2[name] + k:ROW2[name] + k + 1]

        gflat = gates[:, :, :].rearrange("p a t -> p (a t)")
        x_tok = gflat[:, 0:2048].rearrange("p (a d) -> p a d", a=NTT)
        flat = lambda t: t[:, :, :].rearrange("p a t -> p (a t)")
        rows_in = flat(act_out)
        b_nat = [gflat[:, 2048 + 256 * i:2304 + 256 * i].rearrange("p (s c) -> p s c", c=16) for i in range(2)]
        b_bar = [gflat[:, 2560 + 256 * i:2816 + 256 * i].rearrange("p (s c) -> p s c", c=16) for i in range(2)]
        b_diag = [gflat[:, 3072 + 512 * i:3584 + 512 * i].rearrange("p (s c) -> p s c", c=32) for i in range(2)]
        c_nat = [flat(hid).rearrange("p (i a s) -> p i a s", i=4, a=2), flat(stat).rearrange("p (i a s) -> p i a s", i=4, a=2)]
        b_t = [tables[:, 512 * i:512 * i + 512].rearrange("p (i m) -> p i m", i=4) for i in range(2)]
        c_t = [tables[:, 1024 + 512 * i:1536 + 512 * i].rearrange("p (s c) -> p s c", c=32) for i in range(3)]
        us = tmp[:, 0:KS, :]
        v_tok = tmp[:, KS:, :].rearrange("p a t -> p (a t)").rearrange("p (a d) -> p a d", a=NTT)
        qT, kT = sq[:, 0:KS, :], sq[:, KS:, :]
        col = lambda i: cols1[:, i, :]
        (DT, ADT, TURNS, WHOLE, FRAC, DECAY, AFRAC, SIN1, COS1, ARE, AIM, INV, FRE, FIM, CT) = range(15)

        def phase(i, which):
            buf, at = ((shared, 0), (shared, 2048), (gflat, 2048), (shared, 0))[i]
            return buf[:, at + which * 1024:at + which * 1024 + 1024].rearrange("p (j t) -> p j t", j=4)
        prod = [small[:, i * 1024:(i + 1) * 1024].rearrange("p (a t) -> p a t", a=4) for i in range(2)]
        ATT = 3 * P
        at_abs, at_pos, at_sp, at_w = (small[:, 2048 + ATT * i:2048 + ATT * (i + 1)] for i in range(4))
        merged = small[:, 0:2048].rearrange("p (k t) -> p k t", k=KD)
        gated = small[:, 2048:3072].rearrange("p (k t) -> p k t", k=4)

        mk = lambda *names: [sem(n) for n in names]
        (prep_dve, prep_act, bt_in, bt_taken, ph_ready, ph_done, bu_done, bu_free, prod_done, y_done,
         y_taken, gelu_h, gelu_l, z_done, z_read, ln_done, sp_done, sp_masked, tri_done, w_exp, av_done,
         o_half, o_taken, glu_sig, glu_y, glu_h, glu_l, pair_read, merged_sum, merged_h, merged_l, 
         ph_later, zeroed, gn_in, gn_t, vec2_in, vec2_t, w2_in, cd_in) = mk(
            "prep_dve", "prep_act", "bt_in", "bt_taken", "ph_ready", "ph_done", "bu_done", "bu_free",
            "prod_done", "y_done", "y_taken", "gelu_h", "gelu_l", "z_done", "z_read", "ln_done", "sp_done",
            "sp_masked", "tri_done", "w_exp", "av_done", "o_half", "o_taken", "glu_sig",
            "glu_y", "glu_h", "glu_l", "pair_read", "merged_sum", "merged_h", "merged_l", "ph_later", "zeroed", "gn_in", "gn_t", "vec2_in", "vec2_t", "w2_in",
            "cd_in")

        tiles_at = {5: [0], 6: [1], 7: [2, 3], 8: [4, 5], 9: [6, 7], 10: [8, 9], 11: [10, 11], 12: [12], 13: [13],
                    14: [14, 15]}
        PHASES_AT = {1: [0, 1], 5: [2], 11: [3]}
        NSTEP = 16

        def used_by(n):
            return slabs[n][2], slabs[n][3] + 1

        def wait_down_bank(dve, n, f, b):
            if b < 3:
                dve.wait_ge(down_bank, 3 * f + b + 1)
            else:
                wait_used(dve, n)

        def wait_used(eng, n):
            slot, c = used_by(n)
            eng.wait_ge(used[slot], c)

        def lin_pe(pe, n, b, ready=None, kt=KD, c=WCOLS, tiles=2, xa=tile_u, xb=tile_l, inc=True):
            slot = pe_slab(pe, n)
            order = [(f, k) for f in range(tiles) for k in range(kt)]
            if ready is not None:
                order.sort(key=lambda x: x[1])
            for f, k in order:
                if ready is not None and f == 0:
                    ready(k)
                mm = mm3(pe, bank[b + f // 2][:, (f % 2) * T:(f % 2 + 1) * T],
                         slab_view(wh, slot, kt, c)[:, k, f * P:(f + 1) * P],
                         slab_view(wl, slot, kt, c)[:, k, f * P:(f + 1) * P],
                         xa(k), xb(k), k == 0 and (f % 2 == 0 or ready is None), k == kt - 1)
            if inc:
                mm.then_inc(used[slot], 1)
            return mm

        def lin_quarter(pe, n, b, j):
            slot = slabs[n][2]
            for q in range(4 * j, 4 * j + 4):
                f, k = divmod(q, KD)
                mm = mm3(pe, bank[b][:, f * T:(f + 1) * T],
                         slab_view(wh, slot, KD, WCOLS)[:, k, f * P:(f + 1) * P],
                         slab_view(wl, slot, KD, WCOLS)[:, k, f * P:(f + 1) * P],
                         uh[:, k, :], ul[:, k, :], k == 0, k == KD - 1)
            if j == 3:
                mm.then_inc(used[slot], 1)

        def lin_tokens(pe, n, b, c0, width, c, kt=KD, at=0, xa=uh, xb=ul):
            slot = slabs[n][2]
            for tt in range(NTT):
                for k in range(kt):
                    mm = mm3(pe, bank[b][:, at + tt * width:at + (tt + 1) * width],
                             xa[:, k, tt * P:(tt + 1) * P], xb[:, k, tt * P:(tt + 1) * P],
                             slab_view(wh, slot, kt, c)[:, k, c0:c0 + width],
                             slab_view(wl, slot, kt, c)[:, k, c0:c0 + width], k == 0, k == kt - 1)
            return mm

        N_IN1, N_GATE1, N_GLU, N_UP1, N_OUT1, N_FFN1 = (where[w] for w in ("in1", "gate1", "glu", "up1", "out1", "ffn1"))

        def ssm_loads(sp):
            for i, nm in enumerate(("B_re", "B_im")):
                sp.dma_start(b_nat[i], a[nm][0].rearrange("(s g) p c -> (g p) s c", g=2)).then_inc(ssm_in, 16)
            for i, nm in enumerate(("C_re", "C_im")):
                for d in range(2):
                    sp.dma_start(c_nat[i][:, :, d, :], a[nm][0].rearrange("(i g) c p -> (g c) i p", g=8)).then_inc(ssm_in, 16)
            sp.dma_start(steps_t[:, :], a["shape_tables"][:, 4 * T + 2 * P:]).then_inc(ssm_in, 16)

        def later_vectors(sp):
            for l in range(LAYERS):
                for name, r0 in ROW2.items():
                    src = a[name + "_2"][l]
                    if name.startswith("cmp_pe"):
                        src = src.rearrange("(s g) p -> s (g p)", g=2)
                    else:
                        src = src.rearrange("(k p) -> k p", p=P)
                    sp.dma_start(rows_in[r0:r0 + src.shape[0], (1 + l) * P:(2 + l) * P], src).then_inc(vec2_in, 16)
            for l in range(LAYERS):
                for i, nm in enumerate(("cmp_k_w2_2", "cmp_v_w2_2")):
                    for d in range(2):
                        sp.dma_start(cmp_w2[:, l, i, d, :], a[nm][l]).then_inc(w2_in, 16)

        def b1_sp(sp):
            for tt in range(NTT):
                sp.dma_start(x_tok[:, tt, :], a["x"][0].rearrange("(a p) d -> p a d", p=P)[:, tt, :]).then_inc(x_in, 16)
            for n in range(N_FFN1):
                if n == 1:
                    ssm_loads(sp)
                if n == 2:
                    later_vectors(sp)
                sp_slab(sp, n)
            n0 = N_FFN1
            sp_slab(sp, n0)
            with sp.Fori(1, SLABS1, 1) as i:
                sp_slab(sp, n0 + 1, i, i - 1)
                sp_slab(sp, n0 + 2, i - 1, i - 1)
            sp_slab(sp, n0 + 2 * SLABS1 - 1)

        def pool_consts(pool):
            def link(ins):
                chain(pool, pool_n, pool_chain, ins)
            link(pool.memset(ident[:, :], 0.0))
            link(pool.affine_select(out=ident[:, :], in_=ident[:, :], compare_op=ALU.not_equal, fill=1.0, base=0,
                                    pattern=[[-1, P]], channel_multiplier=1))
            pool.tensor_copy(identb[:, :], ident[:, :]).then_inc(consts, 1)
            pool.memset(mean_w[:, :], 1.0 / D).then_inc(consts, 1)
            link(pool.memset(suffix[:, :], -1.0))
            pool.affine_select(out=suffix[:, :], in_=suffix[:, :], compare_op=ALU.is_ge, fill=0.0, base=0,
                               pattern=[[-1, P]], channel_multiplier=1).then_inc(consts, 1)
            pool.memset(minus1[:, :], -1.0).then_inc(consts, 1)
            link(pool.memset(causal[:, :], 0.0))
            pool.affine_select(out=causal[:, :], in_=causal[:, :], compare_op=ALU.is_ge, fill=NEG, base=0,
                               pattern=[[-1, P]], channel_multiplier=1).then_inc(consts, 1)
            link(pool.memset(earlier[:, :], 0.0))
            pool.affine_select(out=earlier[:, :], in_=earlier[:, :], compare_op=ALU.is_gt, fill=NEG, base=0,
                               pattern=[[1, P]], channel_multiplier=-1).then_inc(consts, 1)
            pool.memset(zero_w[:, :].bitcast(F32), 0.0).then_inc(consts, 1)
            for t, v, f in ((cmask, 0.0, NEG), (cvalid, 1.0, 0.0)):
                link(pool.memset(t[:, :, :], v))
                pool.affine_select(out=t[:, :, :], in_=t[:, :, :], compare_op=ALU.is_ge, fill=f, base=1 - L_CMP,
                                   pattern=[[P, NTT], [-S_CMP, N_CMP]], channel_multiplier=1).then_inc(consts, 1)

        def pool_zeros(pool):
            for t in b_diag + c_t + [kcc[:, :]]:
                pool.memset(t, 0.0).then_inc(zeroed, 1)

        def b1_pool(pool):
            def keep_earlier_keys(t):
                v = t.rearrange("p (a b) -> p a b", b=P)[:, 0:3:2, :]
                return pool.affine_select(out=v, in_=v, compare_op=ALU.is_gt, fill=0.0, base=0,
                                          pattern=[[0, 2], [1, P]], channel_multiplier=-1)
            pool.wait_ge(ssm_in, 16 * 7)
            pool.wait_ge(prep_dve, 3)
            pool.wait_ge(bt_taken, 1)
            for step in range(3):
                pool_phase(pool, 2, step)
            for h in range(HEADS):
                pool.wait_ge(ln_done, h + 1)
                if h >= 1:
                    pool.wait_ge(tri_done, h)
                pool.tensor_tensor(at_sp, at_pos, at_abs, ALU.add).then_inc(sp_done, 1)
                pool.wait_ge(sp_done, h + 1)
                keep_earlier_keys(at_sp).then_inc(sp_masked, 1)
                if h == 0:
                    pool.wait_ge(prod_done, 4)
                if h < 3:
                    pool_phase(pool, 3, h)

        def start_act_dmas(act):
            for name, (buf, r0) in [(k, (0, r)) for k, r in ROW1.items()]:
                src = a[name]
                if name in ("A_re", "A_im"):
                    src = src[0].rearrange("(s g) p -> s (g p)", g=2)
                else:
                    src = (src if name == "norm_final" else src[0]).rearrange("(k p) -> k p", p=P)
                act.dma_start(rows_in[r0:r0 + src.shape[0], 0:P], src).then_inc(vec_in, 16)
            act.dma_start(small[0:ST, 0:2], a["log_dt"][0].rearrange("(s g) -> s g", g=2)).then_inc(vec_in, 16)
        N_VEC = 16 * (len(ROW1) + 1)
        N_VEC2 = 16 * LAYERS * len(ROW2)

        def b1_pe_start(pe):
            pe.wait_ge(consts, 1)
            pe.wait_ge(x_in, 16 * NTT)
            for k in range(KD):
                for tt in range(NTT):
                    mm = pe.transpose(bank[1 + k // 2][:, (k % 2) * T + tt * P:(k % 2) * T + (tt + 1) * P],
                                      x_tok[:, tt, k * P:(k + 1) * P], ident[:, :])
                if k % 2:
                    mm.then_inc(tr_ready, 1)
            pe.wait_ge(consts, 9)
            pe.wait_ge(vec_in, N_VEC)
            pe.transpose(bank[0][:, 0:ROWS1], rows_in[0:ROWS1, 0:P], ident[0:ROWS1, 0:ROWS1])
            pe.wait_ge(prep_dve, 1)
            pe.transpose(bank[0][:, 3 * P:3 * P + ST], rows_in[0:ST, 3 * P:4 * P], ident[0:ST, 0:ST]).then_inc(tr_ready, 1)

        def b1_pe_vec2(pe):
            pe.wait_ge(vec2_in, N_VEC2)
            for l in range(LAYERS):
                mm = pe.transpose(bank[7][:, P * l:P * l + ROWS2], rows_in[0:ROWS2, P * (l + 1):P * (l + 2)],
                                  ident[0:ROWS2, 0:ROWS2])
            mm.then_inc(vec2_t, 1)

        def b1_dve_start(dve):
            link = lambda ins: chain(dve, dve_n, dve_chain, ins)
            dve.memset(quarter[:, 0:1], PI / 2)
            dve.memset(quarter[:, 1:2], EPS_RMS)
            dve.memset(quarter[:, 2:3], EPS_LN).then_inc(cd_in, 1)
            for b in range(4):
                dve.wait_ge(tr_ready, b + 1)
                dve.tensor_copy(res[:, 2 * b:2 * b + 2, :], two(bank[1 + b])).then_inc(norm_in, 2)
            dve.wait_ge(vec_in, N_VEC)
            dve.tensor_copy(rows_in[0:ST, 3 * P:4 * P].rearrange("p (g s) -> p g s", g=2),
                            small[0:ST, 0:2].rearrange("p (g o) -> p g o", o=1).to_broadcast([ST, 2, STATES])).then_inc(prep_dve, 1)
            dve.wait_ge(tr_ready, 5)
            link(dve.tensor_copy(vec1[:, :], bank[0][:, 0:ROWS1]))
            dve.tensor_copy(col(CT), bank[0][:, 3 * P:3 * P + ST]).then_inc(prep_dve, 1)

        def b1_dve_params(dve):
            link = lambda ins: chain(dve, dve_n, dve_chain, ins)
            TT = lambda o, x, y, op: link(dve.tensor_tensor(o, x, y, op))
            lre, lim = vec1[:, ROW1["A_re"]:ROW1["A_re"] + ST], vec1[:, ROW1["A_im"]:ROW1["A_im"] + ST]
            dve.wait_ge(zeroed, len(b_diag + c_t) + 1)
            dve.wait_ge(vec2_t, 1)
            for l in range(LAYERS):
                link(dve.tensor_copy(vec2[:, l, :], bank[7][:, P * l:P * l + ROWS2]))
            link(dve.tensor_scalar(half_b[:, :], vec1[:, ROW1["b_gate"]:ROW1["b_gate"] + 2 * KD], 0.5, None, ALU.mult))
            dve.wait_ge(prep_act, 1)
            TT(col(ADT), lre, col(DT), ALU.mult)
            link(dve.scalar_tensor_tensor(out=col(TURNS), in0=lim, scalar=1.0 / (2 * PI), in1=col(DT), op0=ALU.mult, op1=ALU.mult))
            link(dve.tensor_scalar(col(WHOLE), col(TURNS), ROUND, ROUND, ALU.add, ALU.subtract))
            dve.tensor_tensor(col(FRAC), col(TURNS), col(WHOLE), ALU.subtract).then_inc(prep_dve, 1)
            dve_split(dve, N_IN1 + 2)
            dve.wait_ge(ssm_in, 16 * 7)
            for i in range(2):
                dve_phase(dve, i)
            dve_split(dve, N_IN1 + 3)
            dve.wait_ge(prep_act, 2)
            TT(col(ARE), col(DECAY), col(COS1), ALU.mult)
            link(dve.tensor_scalar(col(ARE), col(ARE), 1.0, None, ALU.subtract))
            TT(col(AIM), col(DECAY), col(SIN1), ALU.mult)
            TT(col(INV), lre, lre, ALU.mult)
            TT(col(CT), lim, lim, ALU.mult)
            TT(col(INV), col(INV), col(CT), ALU.add)
            link(dve.reciprocal(col(INV), col(INV)))
            TT(col(FRE), col(ARE), lre, ALU.mult)
            TT(col(CT), col(AIM), lim, ALU.mult)
            TT(col(FRE), col(FRE), col(CT), ALU.add)
            TT(col(FRE), col(FRE), col(INV), ALU.mult)
            TT(col(FIM), col(AIM), lre, ALU.mult)
            TT(col(CT), col(ARE), lim, ALU.mult)
            TT(col(FIM), col(FIM), col(CT), ALU.subtract)
            TT(col(FIM), col(FIM), col(INV), ALU.mult)
            fre, fim = (col(i).rearrange("p (s o) -> p s o", o=1).to_broadcast([P, ST, 16]) for i in (FRE, FIM))
            t0 = flat(act_out)[:, 0:256].rearrange("p (s c) -> p s c", c=16)
            TT(b_bar[0], b_nat[0], fre, ALU.mult)
            TT(t0, b_nat[1], fim, ALU.mult)
            TT(b_bar[0], b_bar[0], t0, ALU.subtract)
            TT(b_bar[1], b_nat[1], fre, ALU.mult)
            TT(t0, b_nat[0], fim, ALU.mult)
            TT(b_bar[1], b_bar[1], t0, ALU.add)
            for i in range(2):
                for g in range(2):
                    ins = dve.tensor_copy(b_diag[i][64 * g:64 * g + 64, :, 16 * g:16 * g + 16], b_bar[i][64 * g:64 * g + 64, :, :])
                    ins.then_inc(bt_in, 1)
            dve_split(dve, N_IN1 + 4)
            dve_split(dve, N_IN1 + 5)
            dve.wait_ge(bt_taken, 1)
            for i in range(2):
                link(dve.tensor_copy(b_t[i], bank[i][:, :].rearrange("p (i m) -> p i m", i=4)))
            for i, (src, sign) in enumerate(((2, 1.0), (2, -1.0), (3, -1.0))):
                for g in range(2):
                    o = c_t[i][64 * g:64 * g + 64, :, 16 * g:16 * g + 16]
                    s_ = bank[src][64 * g:64 * g + 64, :].rearrange("p (s c) -> p s c", c=32)[:, :, 16 * g:16 * g + 16]
                    ins = dve.tensor_scalar(o, s_, sign, None, ALU.mult)
                    if i == 2 and g == 1:
                        ins.then_inc(cd_in, 1)
                    else:
                        link(ins)

        def b1_pe_params(pe):
            pe.wait_ge(bt_in, 4)
            for i in range(2):
                for q in range(4):
                    pe.transpose(bank[i][:, q * P:(q + 1) * P], b_diag[i][:, 4 * q:4 * q + 4, :].rearrange("p s c -> p (s c)"), ident[:, :])
            for i in range(2):
                for q in range(4):
                    mm = pe.transpose(bank[2 + i][:, q * P:(q + 1) * P], c_nat[i][:, q, :, :].rearrange("p a s -> p (a s)"), ident[:, :])
            mm.then_inc(bt_taken, 1)

        def dve_phase(dve, i):
            c, s = phase(i, 0), phase(i, 1)
            for j in range(4):
                ins = dve.tensor_scalar(s[:, j, :], steps_t[:, :], col(TURNS)[:, 4 * i + j:4 * i + j + 1], None, ALU.mult)
            chain(dve, dve_n, dve_chain, ins)
            chain(dve, dve_n, dve_chain, dve.tensor_scalar(c, s, ROUND, ROUND, ALU.add, ALU.subtract))
            dve.tensor_tensor(s, s, c, ALU.subtract).then_inc(ph_ready, 1)

        def pool_phase(pool, i, step):
            c, s = phase(i, 0), phase(i, 1)
            if step == 0:
                for j in range(4):
                    ins = pool.tensor_scalar(s[:, j, :], steps_t[:, :], col(TURNS)[:, 4 * i + j:4 * i + j + 1], None, ALU.mult)
                chain(pool, pool_n, pool_chain, ins)
            elif step == 1:
                chain(pool, pool_n, pool_chain, pool.tensor_scalar(c, s, ROUND, ROUND, ALU.add, ALU.subtract))
            else:
                pool.tensor_tensor(s, s, c, ALU.subtract).then_inc(ph_later, 1)

        def act_phase(act, i):
            c, s = phase(i, 0), phase(i, 1)
            if i < 2:
                act.wait_ge(ph_ready, i + 1)
            else:
                act.wait_ge(ph_later, i - 1)
            chain(act, act_n, act_chain, act.activation(c, s, ACT.Abs))
            chain(act, act_n, act_chain, act.activation(s, s, ACT.Sin, scale=2 * PI))
            act.activation(c, c, ACT.Sin, scale=-2 * PI, bias=quarter[:, 0:1]).then_inc(ph_done, 1)

        def pe_bu(pe, s):
            i, j = s // 4, s % 4
            if s >= 2:
                pe.wait_ge(bu_free, s - 1)
            pe.wait_ge(lin_free[i // 2], 1)
            r = slice(32 * j, 32 * j + 32)
            pe.matmul(bank[s % 2][:, 0:T], b_t[0][r, i, :], us[r, i, :], start=True, stop=True)
            pe.matmul(bank[s % 2][:, T:2 * T], b_t[1][r, i, :], us[r, i, :], start=True, stop=True).then_inc(bu_done, 1)

        def pe_y(pe, s):
            i, j = s // 4, s % 4
            if j == 0 and i >= 1:
                pe.wait_ge(y_taken, i)
            pe.wait_ge(prod_done, s + 1)
            p = prod[s % 2]
            for n, (c, q) in enumerate(((0, 0), (1, 3), (2, 2), (2, 1))):
                mm = pe.matmul(bank[3][32 * j:32 * j + 32, 0:T], c_t[c][:, s, :], p[:, q, :], start=n == 0, stop=n == 3)
            mm.then_inc(y_done, 1)

        def dve_state(dve, s):
            i, j = s // 4, s % 4
            link = lambda ins: chain(dve, dve_n, dve_chain, ins)
            cos2 = phase(i, 0)[:, j:j + 1, :].to_broadcast([P, 2, T])
            sin2 = phase(i, 1)[:, j:j + 1, :].to_broadcast([P, 2, T])
            dve.wait_ge(bu_done, s + 1)
            if s >= 1:
                dve.wait_ge(prod_done, s)
            if j == 0:
                dve.wait_ge(ph_done, i + 1)
            dve.tensor_tensor(act_out[:, :, :], two(bank[s % 2]), cos2, ALU.mult)
            dve.tensor_tensor(hid[:, :, :], two(bank[s % 2]), sin2, ALU.mult).then_inc(bu_free, 1)
            dve.wait_ge(bu_free, s + 1)
            dve.tensor_tensor(stat[:, 0, :], act_out[:, 0, :], hid[:, 1, :], ALU.add)
            link(dve.tensor_tensor(stat[:, 1, :], act_out[:, 1, :], hid[:, 0, :], ALU.subtract))
            decay = col(DECAY)[:, s:s + 1].to_broadcast([P, T])
            dve.tensor_tensor_scan(act_out[:, 0, :], decay, stat[:, 0, :], 0.0, ALU.mult, ALU.add)
            link(dve.tensor_tensor_scan(act_out[:, 1, :], decay, stat[:, 1, :], 0.0, ALU.mult, ALU.add))
            if s >= 2:
                dve.wait_ge(y_done, s - 1)
            p = prod[s % 2]
            dve.tensor_tensor(p[:, 0:2, :], act_out[:, :, :], cos2, ALU.mult)
            dve.tensor_tensor(p[:, 2:4, :], act_out[:, :, :], sin2, ALU.mult).then_inc(prod_done, 1)

        def dve_y(dve, i):
            dve.wait_ge(y_done, 4 * i + 4)
            dve.scalar_tensor_tensor(out=us[:, i, :], in0=us[:, i, :], scalar=v1("D_skip")(i), in1=bank[3][:, 0:T],
                                     op0=ALU.mult, op1=ALU.add).then_inc(y_taken, 1)

        def head(h):
            r = slice(64 * (h % 2), 64 * (h % 2) + 64)
            return h // 2, r, (2, 7)[h % 2]

        def pe_z(pe, h):
            j, r, b = head(h)
            if h == 0:
                for b_ in range(2):
                    pe.wait_ge(lin_free[b_], 4)
            if h >= 2:
                pe.wait_ge(w_exp, h - 1)
            pe.matmul(bank[b][:, 0:T], kT[r, j, 0:P], qT[r, j, :], start=True, stop=True, skip_group_check=True)
            pe.matmul(bank[b][:, T:T + P], kT[r, j, P:T], qT[r, j, P:T], start=False, stop=True,
                      skip_group_check=True).then_inc(z_done, 1)

        def pe_tri(pe, h):
            j, r, b = head(h)
            pe.wait_ge(sp_masked, h + 1)
            pe.matmul(bank[b][:, 0:T], suffix[:, :], at_sp[:, 0:T], start=False, stop=True, skip_group_check=True)
            pe.matmul(bank[b][:, P:T], minus1[:, :], at_sp[:, T:T + P], start=False, stop=True, skip_group_check=True)
            pe.matmul(bank[b][:, T:T + P], suffix[:, :], at_sp[:, T:T + P], start=False, stop=True, skip_group_check=True)
            for c in (0, T):
                mm = pe.matmul(bank[b][:, c:c + P], identb[:, :], earlier[:, :], start=False, stop=True,
                               skip_group_check=True)
            mm.then_inc(tri_done, 1)

        def pe_av(pe, h):
            j, r, b = head(h)
            pe.wait_ge(w_exp, h + 1)
            if h % 2 == 0 and j >= 1:
                pe.wait_ge(o_taken, j)
            c = slice(h * HD, h * HD + HD)
            pe.matmul(bank[6][r, 0:T], v_tok[:, 0, c], at_w[:, 0:T], start=True, stop=True, skip_group_check=True)
            pe.matmul(bank[6][r, P:T], v_tok[:, 1, c], at_w[:, T:T + P], start=False, stop=True,
                      skip_group_check=True).then_inc(av_done, 1)

        def act_softplus(act, h):
            link = lambda ins: chain(act, act_n, act_chain, ins)
            b = head(h)[2]
            act.wait_ge(z_done, h + 1)
            if h >= 1:
                act.wait_ge(sp_done, h)
            link(act.activation(at_abs, bank[b][:, 0:ATT], ACT.Abs))
            act.activation(at_pos, bank[b][:, 0:ATT], ACT.Relu).then_inc(z_read, 1)
            link(act.activation(at_abs, at_abs, ACT.Exp, scale=-1.0))
            act.activation(at_abs, at_abs, ACT.Ln, bias=1.0).then_inc(ln_done, 1)

        def act_weights(act, h):
            act.wait_ge(tri_done, h + 1)
            if h >= 1:
                act.wait_ge(av_done, h)
            act.activation(at_w, bank[head(h)[2]][:, 0:ATT], ACT.Exp).then_inc(w_exp, 1)

        def act_o(act, j):
            act.wait_ge(av_done, 2 * j + 2)
            act.copy(bh[:, KS + j, :], bank[6][:, 0:T]).then_inc(o_half, 1)

        def dve_o(dve, j):
            dve.wait_ge(o_half, j + 1)
            dve.tensor_tensor(bl[:, KS + j, :], bank[6][:, 0:T], bh[:, KS + j, :].bitcast(F32), ALU.subtract).then_inc(o_taken, 1)

        def b1_pe(pe):
            idx, ln, tb = norms["mix1"]
            b1_pe_start(pe)
            norm_pe(pe, idx, ln, tb, KD, tile_res)
            for g in range(NSTEP):
                n = N_IN1 + g
                if g >= 8:
                    pe_z(pe, g - 8)
                if g >= 2:
                    pe.wait_ge(lin_free[g % 2], g // 2)
                b = 4 + g % 2
                if g in (6, 7):
                    pe_slab(pe, n)
                    lin_tokens(pe, n, b, 0, WCOLS, WCOLS).then_inc(used[slabs[n][2]], 1)
                else:
                    ready = (lambda k: pe.wait_ge(norm_out, tb + k + 1)) if g == 0 else None
                    lin_pe(pe, n, b, ready)
                if g == 0:
                    b1_pe_vec2(pe)
                if g == 3:
                    b1_pe_params(pe)
                if g == 4:
                    pe.wait_ge(cd_in, 2)
                for s in tiles_at.get(g, [])[1:]:
                    pe_bu(pe, s)
                if g >= 8:
                    pe_tri(pe, g - 8)
                for s in tiles_at.get(g - 1, []):
                    pe_y(pe, s)
                for s in tiles_at.get(g + 1, [])[:1]:
                    pe_bu(pe, s)
                if g >= 9:
                    pe_av(pe, g - 9)
            pe_av(pe, HEADS - 1)
            pe.wait_ge(gelu_l, 1)
            lin_pe(pe, N_GLU, 0, None, KS, DS, 4, lambda k: bh[:, k, :], lambda k: bl[:, k, :])
            pe_up(pe, N_UP1, 0, lambda: pe.wait_ge(o_taken, 4), lambda: pe.wait_ge(glu_l, 1), 1)
            idx, ln, tb = norms["mlp1"]
            pe_out(pe, N_OUT1, 0, tb)
            norm_pe(pe, idx, ln, tb, KD, tile_res)
            ffn_pe(pe, N_FFN1, SLABS1, False, 0, tb)
            idx, ln, tb = norms["final1"]
            norm_pe(pe, idx, ln, tb, KD, tile_res)

        def pe_up(pe, n0, r, ready_b, ready_a, extra=0, order="BA"):
            for q in range(4):
                p, which = q // 2, order[q % 2]
                off = KS if which == "B" else 0
                (ready_b if which == "B" else ready_a)()
                if q == 0 and extra:
                    pe.wait_ge(glu_sig, 1)
                if q >= 2:
                    pe.wait_ge(pair_read, 4 * r + q - 1)
                lin_pe(pe, n0 + q, 2 * (q % 2), None, KS, 512, 4,
                       lambda k, off=off: bh[:, off + k, :], lambda k, off=off: bl[:, off + k, :])

        def pe_out(pe, n0, r, tb):
            for q in range(4):
                def ready(k):
                    if k % 2 == 0:
                        pe.wait_ge(merged_l, 4 * r + k // 2 + 1)
                if q >= 2:
                    pe.wait_ge(norm_in, tb + 2 * (q - 1))
                lin_pe(pe, n0 + q, 4 + q % 2, ready if q == 0 else None)

        def act_up(act, n0, r, q):
            p = q // 2
            if q % 2:
                for f in range(2):
                    k = 4 * p + 2 * f
                    act.wait_ge(merged_sum, 4 * r + 2 * p + f + 1)
                    act.copy(uh[:, k:k + 2, :], merged[:, k:k + 2, :]).then_inc(merged_h, 1)

        def dve_up(dve, n0, r, q, order="BA"):
            link = lambda ins: chain(dve, dve_n, dve_chain, ins)
            p, which = q // 2, order[q % 2]
            wait_used(dve, n0 + q)
            g0 = (KD if which == "B" else 0) + 4 * p
            o = merged[:, 4 * p:4 * p + 4, :] if q % 2 == 0 else gated
            for f in range(2):
                ins = dve.scalar_tensor_tensor(out=o[:, 2 * f:2 * f + 2, :], in0=gates[:, g0 + 2 * f:g0 + 2 * f + 2, :], scalar=1.0,
                                               in1=two(bank[2 * (q % 2) + f]), op0=ALU.add, op1=ALU.mult)
            ins.then_inc(pair_read, 1)
            if q % 2:
                dve.wait_ge(pair_read, 4 * r + q + 1)
                two_tiles = [slice(4 * p + 2 * f, 4 * p + 2 * f + 2) for f in range(2)]
                for f, k in enumerate(two_tiles):
                    dve.tensor_tensor(merged[:, k, :], merged[:, k, :], gated[:, 2 * f:2 * f + 2, :], ALU.add).then_inc(merged_sum, 1)
                for f, k in enumerate(two_tiles):
                    dve.wait_ge(merged_h, 4 * r + 2 * p + f + 1)
                    dve.tensor_tensor(ul[:, k, :], merged[:, k, :], uh[:, k, :].bitcast(F32), ALU.subtract).then_inc(merged_l, 1)

        def dve_out(dve, n0, q, o):
            wait_used(dve, n0 + q)
            dve.scalar_tensor_tensor(out=o[:, 2 * q:2 * q + 2, :], in0=two(bank[4 + q % 2]), scalar=0.5, in1=res[:, 2 * q:2 * q + 2, :],
                                     op0=ALU.mult, op1=ALU.add).then_inc(norm_in, 2)

        def b1_act(act):
            link = lambda ins: chain(act, act_n, act_chain, ins)
            start_act_dmas(act)
            act.wait_ge(cd_in, 1)
            idx, ln, tb = norms["mix1"]
            norm_squares(act, ln, tb, KD, tile_res)
            act_round(act, 0)
            norm_act(act, idx, ln, tb, KD, tile_res, 1.0, 1, tile_tmp, None, tile_u, squares=False)
            act_round(act, 1)
            act.wait_ge(prep_dve, 2)
            act.activation(col(DT), col(CT), ACT.Exp).then_inc(prep_act, 1)
            for g in range(NSTEP):
                n = N_IN1 + g
                if g >= 8:
                    act_softplus(act, g - 8)
                act_round(act, n + 2)
                if g == 0:
                    act.wait_ge(prep_dve, 3)
                    act.activation(col(DECAY), col(ADT), ACT.Exp)
                    link(act.activation(col(AFRAC), col(FRAC), ACT.Abs))
                    act.activation(col(SIN1), col(FRAC), ACT.Sin, scale=2 * PI)
                    act.activation(col(COS1), col(AFRAC), ACT.Sin, scale=-2 * PI, bias=quarter[:, 0:1]).then_inc(prep_act, 1)
                if g == 12:
                    act.wait_ge(prod_done, 12)
                wait_used(act, n)
                b = bank[4 + g % 2]
                if g < 2:
                    act.copy(us[:, 2 * g:2 * g + 2, :], two(b)).then_inc(lin_free[g % 2], 1)
                elif g < 8:
                    o = (qT[:, 2 * (g - 2):2 * (g - 2) + 2, :] if g < 4 else kT[:, 2 * (g - 4):2 * (g - 4) + 2, :] if g < 6
                         else v_tok[:, :, (g - 6) * WCOLS:(g - 5) * WCOLS])
                    act.activation(o, two(b), ACT.Copy, scale=SCALE_N if g < 4 else 1.0).then_inc(lin_free[g % 2], 1)
                else:
                    for f in range(2):
                        k = 2 * (g - 8) + f
                        ins = act.activation(gates[:, k, :], b[:, f * T:(f + 1) * T], ACT.Tanh, scale=0.5, bias=half_b[:, k:k + 1])
                    ins.then_inc(lin_free[g % 2], 1)
                for i in PHASES_AT.get(g, []):
                    act_phase(act, i)
                if g >= 8:
                    act_weights(act, g - 8)
                if g >= 9 and g % 2 == 0:
                    act_o(act, (g - 10) // 2)
            act_o(act, 3)
            act.wait_ge(y_taken, 4)
            link(act.activation(us[:, :, :], us[:, :, :], ACT.Gelu_apprx_tanh))
            act.copy(bh[:, 0:KS, :], us[:, :, :]).then_inc(gelu_h, 1)
            act_round(act, N_GLU + 2)
            wait_used(act, N_GLU)
            for f in range(KS):
                ins = act.activation(gated[:, f, :], bank[f // 2][:, (f % 2) * T:(f % 2 + 1) * T], ACT.Sigmoid,
                                     bias=v1("b_glu")(f))
            ins.then_inc(glu_sig, 1)
            act.wait_ge(glu_y, 1)
            act.copy(bh[:, 0:KS, :], us[:, :, :]).then_inc(glu_h, 1)
            for q in range(4):
                act_round(act, N_UP1 + q + 2)
                act_up(act, N_UP1, 0, q)
            for q in range(4):
                act_round(act, N_OUT1 + q + 2)
            idx, ln, tb = norms["mlp1"]
            norm_act(act, idx, ln, tb, KD, tile_res, 1.0, 1, tile_tmp, None, tile_u)
            ffn_act_engine(act, N_FFN1, SLABS1, False, 0)
            idx, ln, tb = norms["final1"]
            norm_act(act, idx, ln, tb, KD, tile_res, 1.0, 1, tile_tmp, None, tile_u)

        def b1_dve(dve):
            link = lambda ins: chain(dve, dve_n, dve_chain, ins)
            b1_dve_start(dve)
            dve_split(dve, 0)
            idx, ln, tb = norms["mix1"]
            norm_dve(dve, idx, ln, tb, KD, tile_res, v1("norm_mix"), tile_tmp, None, tile_u, tile_l)
            dve_split(dve, 1)
            b1_dve_params(dve)
            for g in range(NSTEP):
                n = N_IN1 + g
                for s in tiles_at.get(g - 1, []):
                    if s % 4 == 3 and s < ST - 1:
                        dve_y(dve, s // 4)
                if g >= 4:
                    dve_split(dve, n + 2)
                for s in tiles_at.get(g, []):
                    dve_state(dve, s)
                if g >= 9 and g % 2 == 0:
                    dve_o(dve, (g - 10) // 2)
            dve_y(dve, 3)
            dve_o(dve, 3)
            dve.wait_ge(gelu_h, 1)
            dve.tensor_tensor(bl[:, 0:KS, :], us[:, :, :], bh[:, 0:KS, :].bitcast(F32), ALU.subtract).then_inc(gelu_l, 1)
            dve_split(dve, N_GLU + 2)
            dve.wait_ge(glu_sig, 1)
            dve.tensor_tensor(us[:, :, :], us[:, :, :], gated, ALU.mult).then_inc(glu_y, 1)
            dve.wait_ge(glu_h, 1)
            dve.tensor_tensor(bl[:, 0:KS, :], us[:, :, :], bh[:, 0:KS, :].bitcast(F32), ALU.subtract).then_inc(glu_l, 1)
            for b in range(2):
                dve.wait_ge(lin_free[b], 8)
            for q in range(4):
                dve_split(dve, N_UP1 + q + 2)
                dve_up(dve, N_UP1, 0, q)
            for q in range(4):
                if q < 3:
                    dve_split(dve, N_OUT1 + q + 2)
                dve_out(dve, N_OUT1, q, res)
            dve_split(dve, N_OUT1 + 5)
            idx, ln, tb = norms["mlp1"]
            norm_dve(dve, idx, ln, tb, KD, tile_res, v1("norm_mlp"), tile_tmp, None, tile_u, tile_l)
            ffn_dve_engine(dve, N_FFN1, SLABS1, False, 0)
            for b in range(4):
                wait_down_bank(dve, N_FFN1 + 2 * SLABS1 - 1, 0, b)
                dve.tensor_tensor(res[:, 2 * b:2 * b + 2, :], two(bank[b]), res[:, 2 * b:2 * b + 2, :], ALU.add).then_inc(norm_in, 2)
            dve_split(dve, N_FFN1 + 2 * SLABS1 + 1)
            idx, ln, tb = norms["final1"]
            norm_dve(dve, idx, ln, tb, KD, tile_res, v1("norm_final"), tile_tmp, None, tile_u, tile_l, ALPHA)

        cos_n, sin_n, cos_m, sin_m = (tables[:, i * T:(i + 1) * T] for i in range(4))
        perm_n, perm_m = tables[:, 4 * T:4 * T + P], tables[:, 4 * T + P:4 * T + 2 * P]
        q_n = shared[:, 0:1024].rearrange("p (h t) -> p h t", h=HPG)
        kc, vc, ks, kw = (shared[:, 1024 + i * T:1024 + (i + 1) * T] for i in range(4))
        ksw = shared[:, 1024 + 2 * T:1024 + 4 * T].rearrange("p (a t) -> p a t", a=2)
        vsw = shared[:, 2048:2560].rearrange("p (w a d) -> p a w d", w=2, a=NTT)
        vs, vw = (shared[:, 2048 + i * T:2048 + (i + 1) * T].rearrange("p (a d) -> p a d", a=NTT) for i in range(2))
        vm = shared[:, 2560:3584].rearrange("p (a d) -> p a d", a=NTT)
        qm, km = sq, tmp
        cq = small[:, 0:512].rearrange("p (k t) -> p k t", k=2)
        ckv, kpe = small[:, 512:768], small[0:ROPE_M, 768:1024]
        kper = small[0:ROPE_M, 1024:1280]
        gn_f = small[32:56, 768:1024]
        gn = small[:, 1280:1328].rearrange("p (a h c) -> p a h c", a=NTT, c=3)
        rope_raw = [small[:, 1344 + 512 * i:1856 + 512 * i].rearrange("p (a t) -> p a t", a=2) for i in range(2)]
        rope_tmp = small[:, 2368:2880].rearrange("p (a t) -> p a t", a=2)
        c_scores = small[:, 0:240]
        c_sums = small[:, 240:288].rearrange("p (c n) -> p c n", c=3)
        vcc = small[0:N_CMP, 320:448]
        chid = [small[:, 448 + 32 * i:448 + 32 * i + 2 * N_CMP] for i in range(2)]
        m_sin = small[:, 1344:3392].rearrange("p (a t) -> p a t", a=HEADS)
        ctok = [small[0:2 * N_CMP, 512 + P * i:512 + P * (i + 1)] for i in range(2)]
        probs = [flat(hid)[:, 0:ATT], flat(act_out)[:, 0:ATT]]
        probs_t = [flat(stat)[:, 0:ATT], small[:, 768:768 + ATT]]
        p_cmp_t = small[0:N_CMP, 1344:3392]
        x_f = [flat(act_out)[:, 0:480], flat(hid)[:, 0:480]]
        x_halves = [[flat(t_)[:, 512 * i:512 * i + 480] for t_ in (bh, bl)] for i in range(2)]
        (rope_in, perm_done, rope_done, m_read, m_perm, m_sined, m_roped, km_k, km_pe, kpe_perm, x_blocks, x_l, chid_in, w2_done, ctok_in, ctok_t, w2_read, cs_done, cs_shift, cs_exp, cs_ready, ct_done, ct_taken, a_done, max_done, exp_done, p_ready, t_done, t_taken, o_done, o2_half, o2_taken, bank7_free, tok_done, final_t, final_copied, out_done) = mk(
            "rope_in", "perm_done", "rope_done", "m_read", "m_perm", "m_sined", "m_roped", "km_k", "km_pe", "kpe_perm", "x_blocks", "x_l", "chid_in", "w2_done", "ctok_in", "ctok_t", "w2_read", "cs_done", "cs_shift", "cs_exp", "cs_ready", "ct_done", "ct_taken", "a_done", "max_done", "exp_done", "p_ready", "t_done", "t_taken", "o_done", "o2_half", "o2_taken", "bank7_free", "tok_done", "final_t", "final_copied", "out_done")
        lin2 = [sem("in_read0"), sem("in_read1")]
        NROPE = 4
        RAW_AT = (1, 2, 2, 3)
        B7 = NROPE + 3
        NU = HEADS + 2 * HEADS
        EARLY = 2
        NQ = 4 * (8 - EARLY)
        C0 = 4

        def unit(m):
            if m < HEADS:
                return (lambda c: qm[0:QK_M, m, c], lambda c: km[0:QK_M, m, c],
                        lambda tt: vm[:, tt, m * HD:(m + 1) * HD], m, None)
            h, w = (m - HEADS) // 2, (m - HEADS) % 2
            g, hp = h // HPG, h % HPG
            r = slice(g * HD, (g + 1) * HD)
            k_, v_ = ((ks, vs), (kw, vw))[w]
            return (lambda c: q_n[r, hp, c], lambda c: k_[r, c], lambda tt: v_[:, tt, r], h, 1 + w)

        def unit_cols(tt):
            return slice(0, P) if tt == 0 else slice(P, 3 * P)

        def b2_ffn_sp(sp, l, tag):
            n0 = where[(tag, l)]
            sp_slab(sp, n0)
            sp_slab(sp, n0 + 1)
            with sp.Fori(1, SLABS2 - 1, 1) as i:
                sp_slab(sp, n0 + 2, (l, i), i - 1)
                sp_slab(sp, n0 + 3, (l, i - 1), i - 1)
                sp_slab(sp, n0 + 4, (l, i), i - 1)
            for n in range(3 * SLABS2 - 4, 3 * SLABS2):
                sp_slab(sp, n0 + n)

        def b2_sp(sp, l):
            if l == 0:
                sp.wait_ge(y_done, ST)
                sp.dma_start(tables[:, 0:4 * T + 2 * P], a["shape_tables"][:, 0:4 * T + 2 * P]).then_inc(rope_in, 16)
            b2_ffn_sp(sp, l, "fa")
            for n in range(where[("in2", l)], where[("fb", l)]):
                sp_slab(sp, n)
            b2_ffn_sp(sp, l, "fb")

        def pe_perm(pe, l, r):
            n = NROPE * l + r
            pe.wait_ge(lin2[r % 2], 8 * l + RAW_AT[r])
            pe.wait_ge(bank7_free, B7 * l + r + 1)
            if n == 0:
                pe.wait_ge(rope_in, 16)
            w = T if r == 2 else 2 * T
            raw_ = rope_raw[r % 2]
            pe.matmul(bank[7][:, 0:w], perm_n, raw_[:, 0:w // T, :], start=True, stop=True).then_inc(perm_done, 1)

        def pe_scores(pe, l, m):
            q_, k_, _, h, _w = unit(m)
            n = NU * l + m
            b = bank[m % 2]
            if m >= 2:
                pe.wait_ge(exp_done, n - 1)
            for tt in range(NTT):
                c = unit_cols(tt)
                pe.matmul(b[:, c], q_(slice(tt * P, (tt + 1) * P)), k_(slice(0, (tt + 1) * P)), start=tt == 0, stop=True,
                          skip_group_check=True)
            for c in (0, 2 * P):
                mm = pe.matmul(b[:, c:c + P], identb[:, :], causal[:, :], start=False, stop=True, skip_group_check=True)
            mm.then_inc(a_done, 1)

        def pe_turn(pe, l, m):
            n = NU * l + m
            pe.wait_ge(p_ready, n + 1)
            if m >= 2:
                pe.wait_ge(t_taken, n - 1)
            b = bank[2 + m % 2]
            for q in range(3):
                mm = pe.transpose(b[:, q * P:(q + 1) * P], probs[m % 2][:, q * P:(q + 1) * P], ident[:, :])
            mm.then_inc(t_done, 1)

        def pe_values(pe, l, m):
            _, _, v_, h, w = unit(m)
            n = NU * l + m
            r = slice(64 * (h % 2), 64 * (h % 2) + 64)
            first = w is None or w == 1
            pair = h // 2 + (0 if w is None else 4)
            if first and h % 2 == 0 and pair > 0:
                pe.wait_ge(o2_taken, 8 * l + pair)
            pe.wait_ge(t_taken, n + 1)
            pt = probs_t[m % 2]
            pe.matmul(bank[6][r, 0:T], v_(0), pt[:, 0:T], start=first, stop=True, skip_group_check=True)
            mm = pe.matmul(bank[6][r, P:T], v_(1), pt[:, T:3 * P], start=False, stop=True, skip_group_check=True)
            if w == 2:
                if h == 0:
                    pe.wait_ge(ct_taken, 4 * l + 4)
                g = h // HPG
                mm = pe.matmul(bank[6][r, 0:T], vcc[:, g * HD:(g + 1) * HD], p_cmp_t[:, h * T:(h + 1) * T], start=False, stop=True,
                               skip_group_check=True)
            mm.then_inc(o_done, 1)

        def b2_pe(pe, l):
            idx, ln, tb = norms["final1"] if l == 0 else norms[("fb", l - 1)]
            ffn_pe(pe, where[("fa", l)], SLABS2, True, SLABS1 + 2 * l * SLABS2, tb)
            idx, ln, tb = norms[("fa", l)]
            norm_pe(pe, idx, ln, tb, KD, tile_tmp)
            n0 = where[("in2", l)]
            for i in range(7):
                n = n0 + i
                b = 4 + i % 2
                if i == 2:
                    pe.wait_ge(norm_in, norms[("q", l)][2] + 2)
                elif i >= 3:
                    pe.wait_ge(lin2[i % 2], 8 * l + (i - 1) // 2)
                ready = (lambda k: pe.wait_ge(norm_out, tb + k + 1)) if i == 0 else None
                slot = slabs[n][2]
                if i in (0, 2, 3, 4, 5):
                    lin_pe(pe, n, b, ready)
                elif i == 1:
                    pe_slab(pe, n)
                    c = KV_RANK + ROPE_M + 3 * HEADS
                    for k in range(KD):
                        mm3(pe, bank[b][:, 0:T], slab_view(wh, slot, KD, c)[:, k, 0:P], slab_view(wl, slot, KD, c)[:, k, 0:P],
                            uh[:, k, :], ul[:, k, :], k == 0, k == KD - 1)
                    for k in range(KD):
                        mm = mm3(pe, bank[b][0:56, T:2 * T], slab_view(wh, slot, KD, c)[:, k, P:c],
                                 slab_view(wl, slot, KD, c)[:, k, P:c], uh[:, k, :], ul[:, k, :], k == 0, k == KD - 1)
                    mm.then_inc(used[slot], 1)
                else:
                    pe_slab(pe, n)
                    lin_tokens(pe, n, b, 0, WCOLS, WCOLS).then_inc(used[slot], 1)
                if i == 1:
                    qi, _, qt = norms[("q", l)]
                    norm_pe(pe, qi, None, qt, 2, lambda k: cq[:, k, :])
                if i == 2:
                    vi, _, vt = norms[("kv", l)]
                    pe.wait_ge(root_done, qi + 1)
                    norm_pe(pe, vi, None, vt, 1, lambda k: ckv)
                if i == 2:
                    pe.wait_ge(gn_in, l + 1)
                    for tt in range(NTT):
                        mm = pe.transpose(bank[7][:, tt * 24:(tt + 1) * 24], gn_f[:, tt * P:(tt + 1) * P], ident[32:56, 32:56])
                    mm.then_inc(gn_t, 1)
                if 3 <= i:
                    pe_perm(pe, l, i - 3)
            n = where[("uq", l)]
            slot = pe_slab(pe, n)
            for k in range(2):
                pe.wait_ge(norm_out, qt + k + 1)
            for h in range(HEADS):
                for k in range(2):
                    mm = mm3(pe, bank[h // 2][0:QK_M, (h % 2) * T:(h % 2 + 1) * T],
                             slab_view(wh, slot, 2, HEADS * QK_M)[:, k, h * QK_M:(h + 1) * QK_M],
                             slab_view(wl, slot, 2, HEADS * QK_M)[:, k, h * QK_M:(h + 1) * QK_M],
                             hh[:, k, :], hl[:, k, :], k == 0, k == 1)
            mm.then_inc(used[slot], 1)
            pe.wait_ge(norm_out, vt + 1)

            def cmp_hidden(i):
                n = where[("cmp", l)] + i
                slot = pe_slab(pe, n)
                pe.wait_ge(x_l, 2 * l + i + 1)
                xh, xl = (t_.rearrange("p (s c) -> p s c", s=16) for t_ in x_halves[i])
                for k in range(16):
                    mm = mm3(pe, bank[6 + i][0:2 * N_CMP, 0:P], slab_view(wh, slot, 16, P)[:, k, :], slab_view(wl, slot, 16, P)[:, k, :],
                             xh[:, k, :], xl[:, k, :], k == 0, k == 15, swap=True)
                mm.then_inc(used[slot], 1)

            def cmp_turn(i):
                pe.wait_ge(ctok_in, 2 * l + i + 1)
                pe.transpose(bank[6 + i][:, T:T + 2 * N_CMP], ctok[i], ident[0:2 * N_CMP, 0:2 * N_CMP]).then_inc(ctok_t, 1)

            cmp_hidden(0)
            for b in range(4):
                pe.wait_ge(m_read, 4 * l + b + 1)
                pe.matmul(bank[b][HD:QK_M, :], perm_m[HD:QK_M, HD:QK_M], qm[HD:QK_M, 2 * b:2 * b + 2, :], start=True,
                          stop=True).then_inc(m_perm, 1)
            pe.wait_ge(bank7_free, B7 * l + NROPE + 1)
            cmp_hidden(1)
            cmp_turn(0)
            n = where[("ukv", l)]
            slot = pe_slab(pe, n)
            wk = lambda w_: slab_view(w_, slot, 1, 2 * HEADS * HD)[:, 0, :].rearrange("p (h c) -> p h c", h=HEADS)
            for tt in range(NTT):
                pe.wait_ge(lin2[tt], 8 * l + 3)
                c = slice(tt * P, (tt + 1) * P)
                mm = mm3(pe, bank[4 + tt][:, :], ckh[:, c], ckl[:, c], wk(wh)[:, :, HD:], wk(wl)[:, :, HD:], True, True)
            mm.then_inc(tok_done, 1)
            cmp_turn(1)
            for h in range(HEADS):
                if h % 2 == 0:
                    pe.wait_ge(m_sined, 4 * l + h // 2 + 1)
                mm = mm3(pe, bank[h // 2][0:HD, (h % 2) * T:(h % 2 + 1) * T], wk(wh)[:, h, 0:HD], wk(wl)[:, h, 0:HD], ckh[:, :], ckl[:, :],
                         True, True)
            mm.then_inc(used[slot], 1)
            pe.wait_ge(lin2[0], 8 * l + 4)
            lin_pe(pe, where[("gate2", l)], 4)
            pe.wait_ge(chid_in, 2 * l + 2)
            pe.matmul(bank[7][0:ROPE_M, 0:T], perm_m[0:ROPE_M, 0:ROPE_M], kpe, start=True, stop=True).then_inc(kpe_perm, 1)
            pe.matmul(bank[6][:, 0:2 * N_CMP], cmp_w2[:, l, 0, :, :].rearrange("p a d -> p (a d)"), chid[0],
                      start=True, stop=True).then_inc(w2_done, 1)
            pe.wait_ge(lin2[1], 8 * l + 4)
            for g in range(KVH):
                mm = pe.matmul(bank[5][0:N_CMP, g * HD:(g + 1) * HD], chid[1][:, g * N_CMP:(g + 1) * N_CMP], cmp_w2[:, l, 1, 0, :],
                               start=True, stop=True)
            mm.then_inc(w2_done, 1)
            pe.wait_ge(w2_read, 2 * l + 2)
            lin_pe(pe, where[("gate2", l)] + 1, 5)
            pe.wait_ge(bank7_free, B7 * l + NROPE + 2)
            pe.wait_ge(rope_done, NROPE * l + NROPE)
            o7 = bank[7][:, 0:NTT * HEADS * N_CMP].rearrange("p (a g h c) -> p a h g c", a=NTT, g=KVH, h=HPG)
            for tt in range(NTT):
                for hp in range(HPG):
                    mm = pe.matmul(o7[:, tt, hp], q_n[:, hp, tt * P:(tt + 1) * P], kcc[:, :].rearrange("p (g c) -> p g c", g=KVH),
                                   start=tt + hp == 0, stop=True, skip_group_check=True)
            mm.then_inc(cs_done, 1)
            pe.wait_ge(m_roped, l + 1)
            pe.wait_ge(km_k, 4 * l + 4)
            pe.wait_ge(km_pe, l + 1)
            for s in range(NU + 2):
                if s < NU:
                    pe_scores(pe, l, s)
                if s < NQ:
                    i, j = divmod(s, 4)
                    i += EARLY
                    n = where[("gate2", l)] + i
                    if j == 0:
                        pe.wait_ge(lin2[i % 2], 8 * l + 4 + i // 2)
                        pe_slab(pe, n)
                    lin_quarter(pe, n, 4 + i % 2, j)
                if 1 <= s <= NU:
                    pe_turn(pe, l, s - 1)
                if C0 <= s < C0 + 4:
                    q = s - C0
                    if q == 0:
                        pe.wait_ge(cs_ready, l + 1)
                        pe.wait_ge(bank7_free, B7 * l + B7)
                    else:
                        pe.wait_ge(ct_taken, 4 * l + q)
                    for h in (2 * q, 2 * q + 1):
                        for tt in range(NTT):
                            mm = pe.transpose(bank[7][0:N_CMP, (h % 2) * T + tt * P:(h % 2) * T + (tt + 1) * P],
                                              c_scores[:, (tt * HEADS + h) * N_CMP:(tt * HEADS + h + 1) * N_CMP], ident[:, :])
                    mm.then_inc(ct_done, 1)
                if s >= 2:
                    pe_values(pe, l, s - 2)
            pe_up(pe, where[("proj", l)], l + 1, lambda: pe.wait_ge(o2_taken, 8 * l + 8), lambda: pe.wait_ge(o2_taken, 8 * l + 4), 0, "AB")
            idx, ln, tb = norms[("mix", l)]
            pe_out(pe, where[("out2", l)], l + 1, tb)
            norm_pe(pe, idx, ln, tb, KD, tile_tmp, 0)
            ffn_pe(pe, where[("fb", l)], SLABS2, True, SLABS1 + (2 * l + 1) * SLABS2, tb)
            idx, ln, tb = norms[("fb", l)]
            norm_pe(pe, idx, ln, tb, KD, tile_tmp)

        def pe_output(pe):
            for tt in range(NTT):
                for k in range(KD):
                    if tt == 0:
                        pe.wait_ge(norm_h, norms[("fb", LAYERS - 1)][2] + k + 1)
                    mm = pe.transpose(bank[2 * tt + k // 4][:, (k % 4) * P:(k % 4 + 1) * P], sq[:, k, tt * P:(tt + 1) * P], ident[:, :])
                    if k % 4 == 3:
                        mm.then_inc(final_t, 1)

        def act_exp(act, l, m):
            n = NU * l + m
            act.wait_ge(max_done, n + 1)
            if m >= 2:
                act.wait_ge(t_done, n - 1)
            for tt in range(NTT):
                c = unit_cols(tt)
                mm = act.activation(probs[m % 2][:, c], bank[m % 2][:, c], ACT.Exp, bias=cols1[:, m % 2, tt:tt + 1],
                                    accum_out=cols1[:, m % 2, 2 + tt:3 + tt])
            mm.then_inc(exp_done, 1)

        def act_turned(act, l, m):
            n = NU * l + m
            act.wait_ge(t_done, n + 1)
            if m >= 2:
                act.wait_ge(o_done, n - 1)
            act.copy(probs_t[m % 2], bank[2 + m % 2][:, 0:ATT]).then_inc(t_taken, 1)

        def last_of_pair(m):
            if m < HEADS:
                return m // 2 if m % 2 else None
            return 4 + (m - HEADS) // 4 if (m - HEADS) % 4 == 3 else None

        def act_blocks(act, l, i):
            if i == 0:
                act.wait_ge(rope_done, NROPE * l + 3)
            src = (kc, vc)[i].rearrange("p (c s q) -> p q s c", s=8, q=2)
            o = x_f[i].rearrange("p (s g c) -> p s g c", s=16, g=KVH)
            for par in range(2):
                for g in range(KVH):
                    for half in range(2):
                        ins = act.copy(o[64 * par:64 * par + 64, 8 * half:8 * half + 8, g, :],
                                       src[64 * g:64 * g + 64, par, :, half:half + N_CMP])
            ins.then_inc(x_blocks, 1)

        def act_gates(act, l, i):
            wait_used(act, where[("gate2", l)] + i)
            act.activation(gates[:, 2 * i:2 * i + 2, :], two(bank[4 + i % 2]), ACT.Tanh, scale=0.5).then_inc(lin2[i % 2], 1)

        def b2_act(act, l):
            link = lambda ins: chain(act, act_n, act_chain, ins)
            ffn_act_engine(act, where[("fa", l)], SLABS2, True, SLABS1 + 2 * l * SLABS2)
            idx, ln, tb = norms[("fa", l)]
            norm_act(act, idx, ln, tb, KD, tile_tmp, 1.0, 2, tile_tmp, v2(l, "ln_f1_b"), tile_u)
            n0 = where[("in2", l)]
            for i in range(7):
                n = n0 + i
                act_round(act, n + 2)
                wait_used(act, n)
                b = bank[4 + i % 2]
                r = i - 2
                if 2 <= r < NROPE:
                    act.wait_ge(rope_done, NROPE * l + r - 1)
                elif r >= 0 and l > 0:
                    act.wait_ge(rope_done, NROPE * l)
                if i == 0:
                    act.copy(cq, two(b)).then_inc(norm_in, 2)
                    idx, ln, tb = norms[("q", l)]
                    norm_squares(act, ln, tb, 2, lambda k: cq[:, k, :])
                elif i == 1:
                    act.copy(ckv, b[:, 0:T]).then_inc(norm_in, 1)
                    act.activation(gn_f, b[32:56, T:2 * T], ACT.Tanh, scale=0.5).then_inc(gn_in, 1)
                    act.copy(kpe, b[0:ROPE_M, T:2 * T]).then_inc(lin2[1], 1)
                    idx, ln, tb = norms[("q", l)]
                    norm_act(act, idx, ln, tb, 2, lambda k: cq[:, k, :], float(D // Q_RANK), 1, lambda k: cq[:, k, :], None,
                             lambda k: hh[:, k, :], squares=False,
                             meanwhile=lambda: norm_squares(act, None, norms[("kv", l)][2], 1, lambda k: ckv))
                elif i in (2, 3):
                    act.activation(rope_raw[r % 2], two(b), ACT.Copy, scale=SCALE_N).then_inc(lin2[i % 2], 1)
                    if i == 2:
                        idx, ln, tb = norms[("kv", l)]
                        norm_act(act, idx, ln, tb, 1, lambda k: ckv, float(D // KV_RANK), 1, lambda k: ckv, None, lambda k: ckh[:, :],
                                 squares=False)
                elif i == 4:
                    act.copy(rope_raw[r % 2][:, 0, :], b[:, 0:T])
                    act.copy(vc, b[:, T:2 * T]).then_inc(lin2[0], 1)
                elif i == 5:
                    act.copy(rope_raw[r % 2], two(b)).then_inc(lin2[1], 1)
                    act_blocks(act, l, 0)
                else:
                    act.copy(vsw, b[:, :].rearrange("p (a w d) -> p a w d", a=NTT, w=2)).then_inc(lin2[0], 1)
                    act_blocks(act, l, 1)
            n = where[("uq", l)]
            act_round(act, n + 2)
            wait_used(act, n)
            for b in range(4):
                act.activation(qm[0:QK_M, 2 * b:2 * b + 2, :], two(bank[b])[0:QK_M], ACT.Copy, scale=SCALE_M).then_inc(m_read, 1)
            for i in range(2):
                n = where[("cmp", l)] + i
                act_round(act, n + 2)
                wait_used(act, n)
                act.copy(ctok[i], bank[6 + i][0:2 * N_CMP, 0:P]).then_inc(ctok_in, 1)
            act_round(act, where[("ukv", l)] + 2)
            act.wait_ge(tok_done, l + 1)
            for tt in range(NTT):
                act.copy(vm[:, tt, :], bank[4 + tt][:, :]).then_inc(lin2[tt], 1)
            for i in range(2):
                act.wait_ge(ctok_t, 2 * l + i + 1)
                act.activation(chid[i], bank[6 + i][:, T:T + 2 * N_CMP], ACT.Gelu_apprx_tanh,
                               bias=v2(l, ("cmp_k_b1", "cmp_v_b1")[i])(0)).then_inc(chid_in, 1)
            wait_used(act, where[("ukv", l)])
            for b in range(4):
                act.copy(km[0:HD, 2 * b:2 * b + 2, :], two(bank[b])[0:HD]).then_inc(km_k, 1)
            for i in range(EARLY):
                act_round(act, where[("gate2", l)] + i + 2)
                act_gates(act, l, i)
            act.wait_ge(cs_shift, l + 1)
            act.activation(c_scores, c_scores, ACT.Exp).then_inc(cs_exp, 1)
            for s in range(NU + 2):
                if s < NU:
                    act_exp(act, l, s)
                if s < NQ and s % 4 < 2:
                    act_round_half(act, where[("gate2", l)] + EARLY + s // 4 + 2, s % 4)
                if 1 <= s <= NU:
                    act_turned(act, l, s - 1)
                if 4 <= s <= NQ and s % 4 == 0:
                    act_gates(act, l, EARLY + s // 4 - 1)
                pair = last_of_pair(s - 2) if s >= 2 else None
                if pair is not None:
                    act.wait_ge(o_done, NU * l + s - 1)
                    act.copy(bh[:, pair, :], bank[6][:, 0:T]).then_inc(o2_half, 1)
            for q in range(4):
                act_round(act, where[("proj", l)] + q + 2)
                act_up(act, where[("proj", l)], l + 1, q)
            for q in range(4):
                act_round(act, where[("out2", l)] + q + 2)
            idx, ln, tb = norms[("mix", l)]
            norm_act(act, idx, ln, tb, KD, tile_tmp, 1.0, 2, tile_tmp, v2(l, "ln_mix_b"), tile_u)
            ffn_act_engine(act, where[("fb", l)], SLABS2, True, SLABS1 + (2 * l + 1) * SLABS2)
            idx, ln, tb = norms[("fb", l)]
            norm_act(act, idx, ln, tb, KD, tile_tmp, 1.0, 2, tile_tmp, v2(l, "ln_f2_b"), tile_u if l < LAYERS - 1 else (lambda k: sq[:, k, :]))

        def dve_rope(dve, l, r):
            n = NROPE * l + r
            w = 1 if r == 2 else 2
            link = lambda ins: chain(dve, dve_n, dve_chain, ins)
            o = (q_n[:, 0:2, :], q_n[:, 2:4, :], kc.rearrange("p (a t) -> p a t", a=1), ksw)[r]
            bc = lambda t_: t_.rearrange("p (a t) -> p a t", a=1).to_broadcast([P, w, T])
            dve.wait_ge(perm_done, n + 1)
            dve.tensor_tensor(rope_tmp[:, 0:w, :], two(bank[7])[:, 0:w, :], bc(sin_n), ALU.mult).then_inc(bank7_free, 1)
            link(dve.tensor_tensor(o, rope_raw[r % 2][:, 0:w, :], bc(cos_n), ALU.mult))
            dve.wait_ge(bank7_free, B7 * l + r + 2)
            dve.tensor_tensor(o, o, rope_tmp[:, 0:w, :], ALU.add).then_inc(rope_done, 1)
            dve.wait_ge(rope_done, n + 1)

        def dve_ffn_end(dve, l, tag):
            for b in range(4):
                wait_down_bank(dve, where[(tag, l)] + 3 * SLABS2 - 1, 1 + 2 * l + (tag == "fb"), b)
                dve.scalar_tensor_tensor(out=tmp[:, 2 * b:2 * b + 2, :], in0=two(bank[b]), scalar=0.5, in1=res[:, 2 * b:2 * b + 2, :],
                                         op0=ALU.mult, op1=ALU.add).then_inc(norm_in, 2)
            n = where[(tag, l)] + 3 * SLABS2 + 1
            if n < len(slabs):
                dve_split(dve, n)

        def dve_max(dve, l, m):
            n = NU * l + m
            dve.wait_ge(a_done, n + 1)
            for tt in range(NTT):
                ins = dve.tensor_reduce(cols1[:, m % 2, tt:tt + 1], bank[m % 2][:, unit_cols(tt)], AX.X, ALU.max, negate=True)
            ins.then_inc(max_done, 1)

        def dve_weigh(dve, l, m):
            link = lambda ins: chain(dve, dve_n, dve_chain, ins)
            n = NU * l + m
            _, _, _, h, w = unit(m)
            inv = cols1[:, m % 2, 4:6]
            dve.wait_ge(exp_done, n + 1)
            link(dve.reciprocal(inv, cols1[:, m % 2, 2:4]))
            if w is not None:
                link(dve.tensor_tensor(inv, inv, gn[:, :, h, w], ALU.mult))
            for tt in range(NTT):
                c = unit_cols(tt)
                ins = dve.tensor_scalar(probs[m % 2][:, c], probs[m % 2][:, c], inv[:, tt:tt + 1], None, ALU.mult)
            ins.then_inc(p_ready, 1)

        def b2_dve(dve, l):
            link = lambda ins: chain(dve, dve_n, dve_chain, ins)
            TT = lambda o, x, y, op: link(dve.tensor_tensor(o, x, y, op))
            ffn_dve_engine(dve, where[("fa", l)], SLABS2, True, SLABS1 + 2 * l * SLABS2)
            dve_ffn_end(dve, l, "fa")
            idx, ln, tb = norms[("fa", l)]
            norm_dve(dve, idx, ln, tb, KD, tile_tmp, v2(l, "ln_f1_g"), tile_tmp, v2(l, "ln_f1_b"), tile_u, tile_l, ALPHA)
            n0 = where[("in2", l)]
            for i in range(7):
                dve_split(dve, n0 + i + 2)
                if i == 1:
                    idx, ln, tb = norms[("q", l)]
                    norm_dve(dve, idx, ln, tb, 2, lambda k: cq[:, k, :], v2(l, "q_norm_g"), lambda k: cq[:, k, :], None,
                             lambda k: hh[:, k, :], lambda k: hl[:, k, :])
                if i == 2:
                    dve.wait_ge(gn_t, l + 1)
                    dve.tensor_scalar(gn.rearrange("p a h c -> p (a h c)"), bank[7][:, 0:NTT * 3 * HEADS], 0.5, 0.5,
                                      ALU.mult, ALU.add).then_inc(bank7_free, 1)
                    idx, ln, tb = norms[("kv", l)]
                    norm_dve(dve, idx, ln, tb, 1, lambda k: ckv, v2(l, "kv_norm_g"), lambda k: ckv, None,
                             lambda k: ckh[:, :], lambda k: ckl[:, :])
                if i >= 3:
                    dve_rope(dve, l, i - 3)
                if i >= 5:
                    j = i - 5
                    dve.wait_ge(x_blocks, 2 * l + j + 1)
                    pe_rows = vec2[:, l, ROW2[("cmp_pe_k", "cmp_pe_v")[j]]:ROW2[("cmp_pe_k", "cmp_pe_v")[j]] + 16]
                    x3 = x_f[j].rearrange("p (s c) -> p s c", s=16)
                    TT(x3, x3, pe_rows.rearrange("p (s o) -> p s o", o=1).to_broadcast([P, 16, 2 * N_CMP]), ALU.add)
                    link(dve.tensor_copy(x_halves[j][0], x_f[j]))
                    dve.tensor_tensor(x_halves[j][1], x_f[j], x_halves[j][0].bitcast(F32), ALU.subtract).then_inc(x_l, 1)
            dve_split(dve, where[("uq", l)] + 2)
            dve_split(dve, where[("cmp", l)] + 2)
            bc = lambda t_, r: t_[r].rearrange("p (a t) -> p a t", a=1).to_broadcast([ROPE_M, 2, T])
            r = slice(HD, QK_M)
            for b in range(4):
                dve.wait_ge(m_perm, 4 * l + b + 1)
                dve.tensor_tensor(m_sin[r, 2 * b:2 * b + 2, :], two(bank[b])[r], bc(sin_m, r), ALU.mult).then_inc(m_sined, 1)
            dve_split(dve, where[("cmp", l)] + 3)
            all_heads = lambda t_: t_[r].rearrange("p (a t) -> p a t", a=1).to_broadcast([ROPE_M, HEADS, T])
            TT(qm[r, :, :], qm[r, :, :], all_heads(cos_m), ALU.mult)
            dve.wait_ge(m_sined, 4 * l + 4)
            dve.tensor_tensor(qm[r, :, :], qm[r, :, :], m_sin[r, :, :], ALU.add).then_inc(m_roped, 1)
            dve_split(dve, where[("ukv", l)] + 2)
            dve.wait_ge(w2_done, 2 * l + 1)
            for g in range(KVH):
                r = slice(g * HD, (g + 1) * HD)
                ins = dve.tensor_copy(kcc[r, g * N_CMP:(g + 1) * N_CMP], bank[6][r, g * N_CMP:(g + 1) * N_CMP])
            ins.then_inc(w2_read, 1)
            dve.wait_ge(w2_done, 2 * l + 2)
            dve.tensor_copy(vcc, bank[5][0:N_CMP, 0:P]).then_inc(w2_read, 1)
            r = slice(0, ROPE_M)
            dve.wait_ge(kpe_perm, l + 1)
            dve.tensor_tensor(rope_tmp[r, 0, :], bank[7][r, 0:T], sin_m[r], ALU.mult).then_inc(bank7_free, 1)
            TT(kper, kpe, cos_m[r], ALU.mult)
            dve.wait_ge(bank7_free, B7 * l + NROPE + 2)
            TT(kper, kper, rope_tmp[r, 0, :], ALU.add)
            dve.tensor_copy(km[HD:QK_M, :, :], kper.rearrange("p (a t) -> p a t", a=1).to_broadcast([ROPE_M, HEADS, T])).then_inc(km_pe, 1)
            dve_split(dve, where[("gate2", l)] + 2)
            dve_split(dve, where[("gate2", l)] + 3)
            dve.wait_ge(cs_done, l + 1)
            s4 = lambda t_: t_.rearrange("p (a h c) -> p a h c", a=NTT, c=N_CMP)
            s3 = c_scores.rearrange("p (n c) -> p n c", c=N_CMP)
            bc4 = lambda t_: t_[:, :, :].rearrange("p a (h c) -> p a h c", h=1).to_broadcast([P, NTT, HEADS, N_CMP])
            bc3 = lambda t_: t_.rearrange("p (n o) -> p n o", o=1).to_broadcast([P, NTT * HEADS, N_CMP])
            dve.tensor_tensor(s4(c_scores), s4(bank[7][:, 0:240]), bc4(cmask), ALU.add).then_inc(bank7_free, 1)
            dve.wait_ge(bank7_free, B7 * (l + 1))
            link(dve.tensor_reduce(c_sums[:, 0, :], s3, AX.X, ALU.max))
            dve.tensor_tensor(s3, s3, bc3(c_sums[:, 0, :]), ALU.subtract).then_inc(cs_shift, 1)
            dve.wait_ge(cs_exp, l + 1)
            link(dve.tensor_reduce(c_sums[:, 1, :], s3, AX.X, ALU.add))
            link(dve.reciprocal(c_sums[:, 2, :], c_sums[:, 1, :]))
            g3 = c_sums[:, 2, :].rearrange("p (a h) -> p a h", a=NTT)
            TT(g3, g3, gn[:, :, :, 0], ALU.mult)
            TT(s3, s3, bc3(c_sums[:, 2, :]), ALU.mult)
            dve.tensor_tensor(s4(c_scores), s4(c_scores), bc4(cvalid), ALU.mult).then_inc(cs_ready, 1)
            for s in range(NU + 2):
                if s < NU:
                    dve_max(dve, l, s)
                if 2 <= s < NQ + 2:
                    dve_split_quarter(dve, where[("gate2", l)] + EARLY + (s - 2) // 4 + 2, (s - 2) % 4)
                if s < NU:
                    dve_weigh(dve, l, s)
                if C0 <= s < C0 + 4:
                    q = s - C0
                    dve.wait_ge(ct_done, 4 * l + q + 1)
                    dve.tensor_copy(p_cmp_t[:, 2 * T * q:2 * T * (q + 1)], bank[7][0:N_CMP, :]).then_inc(ct_taken, 1)
                pair = last_of_pair(s - 2) if s >= 2 else None
                if pair is not None:
                    dve.wait_ge(o2_half, 8 * l + pair + 1)
                    dve.tensor_tensor(bl[:, pair, :], bank[6][:, 0:T], bh[:, pair, :].bitcast(F32), ALU.subtract).then_inc(o2_taken, 1)
            for b in range(2):
                dve.wait_ge(lin2[b], 8 * (l + 1))
            for q in range(4):
                dve_split(dve, where[("proj", l)] + q + 2)
                dve_up(dve, where[("proj", l)], l + 1, q, "AB")
            for q in range(4):
                if q < 3:
                    dve_split(dve, where[("out2", l)] + q + 2)
                dve_out(dve, where[("out2", l)], q, tmp)
            dve_split(dve, where[("out2", l)] + 5)
            idx, ln, tb = norms[("mix", l)]
            norm_dve(dve, idx, ln, tb, KD, tile_tmp, v2(l, "ln_mix_g"), tile_tmp, v2(l, "ln_mix_b"), tile_u, tile_l, ALPHA, 0)
            ffn_dve_engine(dve, where[("fb", l)], SLABS2, True, SLABS1 + (2 * l + 1) * SLABS2)
            dve_ffn_end(dve, l, "fb")
            idx, ln, tb = norms[("fb", l)]
            last = l == LAYERS - 1
            norm_dve(dve, idx, ln, tb, KD, tile_tmp, v2(l, "ln_f2_g"), tile_tmp, v2(l, "ln_f2_b"), None if last else tile_u,
                     None if last else tile_l, None if last else ALPHA)

        out_tok = gflat[:, 0:NTT * D].rearrange("p (a d) -> p a d", a=NTT)

        def dve_output(dve):
            for tt in range(NTT):
                for b in range(2):
                    dve.wait_ge(final_t, 2 * tt + b + 1)
                    dve.tensor_copy(out_tok[:, tt, b * 512:(b + 1) * 512], bank[2 * tt + b][:, :]).then_inc(final_copied, 1)

        def sp_output(sp):
            for tt in range(NTT):
                sp.wait_ge(final_copied, 2 * tt + 2)
                sp.dma_start(out[0].rearrange("(a p) d -> p a d", p=P)[:, tt, :], out_tok[:, tt, :]).then_inc(out_done, 16)
            sp.wait_ge(out_done, 16 * NTT)

        block = ctx.enter_context(nc.Block())
        layers = range(LAYERS)

        @block.sync
        def _(sp):
            b1_sp(sp)
            for l in layers:
                b2_sp(sp, l)
            sp_output(sp)

        @block.gpsimd
        def _(pool):
            pool_consts(pool)
            pool_zeros(pool)
            b1_pool(pool)
            for l in layers:
                for name in ("fa", "mix", "fb"):
                    norm_pool(pool, norms[(name, l)][2])

        @block.scalar
        def _(act):
            b1_act(act)
            for l in layers:
                b2_act(act, l)

        @block.vector
        def _(dve):
            b1_dve(dve)
            for l in layers:
                b2_dve(dve, l)
            dve_output(dve)

        @block.tensor
        def _(pe):
            b1_pe(pe)
            pe.wait_ge(w2_in, 16 * 4 * LAYERS)
            for l in layers:
                b2_pe(pe, l)
            pe_output(pe)


_INS = ["x", "norm_mix", "w_in", "A_re", "A_im", "log_dt", "B_re", "B_im", "C_re", "C_im", "D_skip", "w_glu", "b_glu",
        "w_up_ssm", "w_up_attn", "w_gate", "b_gate", "w_out", "norm_mlp", "w_ff1", "w_ff2", "norm_final", "ln_f1_g_2",
        "ln_f1_b_2", "ffn1_wg_2", "ffn1_wu_2", "ffn1_wd_2", "w_in_2", "q_norm_g_2", "w_uq_2", "kv_norm_g_2",
        "w_ukv_2", "cmp_pe_k_2", "cmp_k_w1_2", "cmp_k_b1_2", "cmp_k_w2_2", "cmp_pe_v_2", "cmp_v_w1_2", "cmp_v_b1_2",
        "cmp_v_w2_2", "w_proj_mla_2", "w_proj_nsa_2", "w_out_2", "ln_mix_g_2", "ln_mix_b_2", "ffn2_wg_2", "ffn2_wu_2",
        "ffn2_wd_2", "ln_f2_g_2", "ln_f2_b_2"]


def kernel(**inputs):
    import concourse.bacc as bacc
    from concourse.bass_utils import run_bass_kernel_spmd

    nc = bacc.Bacc("TRN2", target_bir_lowering=False, num_devices=1)
    arrays = {name: np.ascontiguousarray(inputs[name]) for name in _INS}
    arrays["shape_tables"] = shape_tables()
    a = {name: nc.dram_tensor(name, v.shape, mybir.dt.from_np(v.dtype), kind="ExternalInput").ap()
         for name, v in arrays.items()}
    out = nc.dram_tensor("out", (1, T, D), F32, kind="ExternalOutput").ap()
    hybrid_ssm_attention_kernel(nc, a, out)
    r = run_bass_kernel_spmd(nc, [arrays], core_ids=[0])
    return r.results[0]["out"]
```
